# Optimizing a Trainium2 kernel written in Bass

```python
import math
import jax, jax.numpy as jnp
from jax import lax
import numpy as np

D_MODEL = 2048
BATCH = 1
SEQ = 256
DEPTH = 1

N_META = 16
D_FF = 5632
EPS = 1e-6
HG_HEADS = 12
HG_DK = 128
HG_DV = 128
HG_K = HG_HEADS * HG_DK
HG_WIDTH = HG_HEADS * HG_DV
HG_CHUNK = 64
S5_GROUP = 16
S5_GROUPS = 32
S5_WIDTH = S5_GROUP * S5_GROUPS
S5_STATE = 64
DT_MIN = 1e-3
DT_MAX = 1e-1
IN_COLS = 3 * HG_K + HG_WIDTH + S5_WIDTH + 2 * D_MODEL

kernel_name = "hybrid_hgrn2_s5_macaron_meta"

def _rms_norm(x, g):
    xf = x.astype(jnp.float32)
    y = xf * lax.rsqrt(jnp.mean(xf * xf, axis=-1, keepdims=True) + EPS)
    return (y * g.astype(jnp.float32)).astype(x.dtype)

def _swiglu(x, w_gate, w_up, w_down):
    return (jax.nn.silu(x @ w_gate) * (x @ w_up)) @ w_down

def _split_points():
    sizes = (HG_K, HG_K, HG_WIDTH, HG_WIDTH, S5_WIDTH, D_MODEL)
    return [int(v) for v in np.cumsum(sizes)]

def _hgrn2_chunkwise(q, logf, k, v):
    B, L, H, DK = q.shape
    DV = v.shape[-1]
    n = L // HG_CHUNK

    def to_chunks(a):
        return a.reshape(B, n, HG_CHUNK, H, a.shape[-1]).swapaxes(0, 1)

    causal = jnp.tril(jnp.ones((HG_CHUNK, HG_CHUNK), bool))[None, :, :, None, None]

    def step(S, inp):
        qi, gi, ki, vi = inp
        b = jnp.cumsum(gi, axis=1)
        b_last = b[:, -1]
        o_inter = jnp.einsum('bthk,bhkv->bthv', qi * jnp.exp(b), S)
        diff = b[:, :, None] - b[:, None, :]
        decay = jnp.exp(jnp.where(causal, diff, -jnp.inf))
        attn = jnp.einsum('bthk,bshk,btshk->btsh', qi, ki, decay)
        o_intra = jnp.einsum('btsh,bshv->bthv', attn, vi)
        k_dec = ki * jnp.exp(b_last[:, None] - b)
        S_new = jnp.exp(b_last)[..., None] * S + jnp.einsum('bchk,bchv->bhkv', k_dec, vi)
        return S_new, o_inter + o_intra

    S0 = jnp.zeros((B, H, DK, DV), jnp.float32)
    _, o = lax.scan(step, S0, tuple(map(to_chunks, (q, logf, k, v))))
    return o.swapaxes(0, 1).reshape(B, L, H, DV)

def _s5_scan(u, lam_re, lam_im, log_step, b_re, b_im, c_re, c_im, d_skip):
    f32 = jnp.float32
    lr, li = lam_re.astype(f32), lam_im.astype(f32)
    dt = jnp.exp(log_step.astype(f32))[:, None]
    mag = jnp.exp(lr * dt)
    abar_re, abar_im = mag * jnp.cos(li * dt), mag * jnp.sin(li * dt)
    num_re, num_im = abar_re - 1.0, abar_im
    den = lr * lr + li * li
    coef_re = (num_re * lr + num_im * li) / den
    coef_im = (num_im * lr - num_re * li) / den
    br, bi = b_re.astype(f32), b_im.astype(f32)
    bbar_re = coef_re[..., None] * br - coef_im[..., None] * bi
    bbar_im = coef_re[..., None] * bi + coef_im[..., None] * br
    bu_re = jnp.einsum('blgp,gnp->blgn', u, bbar_re)
    bu_im = jnp.einsum('blgp,gnp->blgn', u, bbar_im)
    a_re = jnp.broadcast_to(abar_re, bu_re.shape)
    a_im = jnp.broadcast_to(abar_im, bu_im.shape)

    def combine(e1, e2):
        ar1, ai1, br1, bi1 = e1
        ar2, ai2, br2, bi2 = e2
        return (ar2 * ar1 - ai2 * ai1,
                ar2 * ai1 + ai2 * ar1,
                ar2 * br1 - ai2 * bi1 + br2,
                ar2 * bi1 + ai2 * br1 + bi2)

    _, _, xr, xi = lax.associative_scan(combine, (a_re, a_im, bu_re, bu_im), axis=1)
    y = (jnp.einsum('gpn,blgn->blgp', c_re.astype(f32), xr)
         - jnp.einsum('gpn,blgn->blgp', c_im.astype(f32), xi))
    return y + d_skip.astype(f32) * u

def _mixer(u, lb, w_in, hg_norm, hg_w_proj, s5_lam_re, s5_lam_im, s5_log_step,
           s5_b_re, s5_b_im, s5_c_re, s5_c_im, s5_d, s5_w_glu_a, s5_w_glu_b, w_out):
    f32 = jnp.float32
    B, L, _ = u.shape
    proj = u @ w_in
    q, f_logit, i_in, g_out, s5_u, gate_hg, gate_s5 = jnp.split(proj, _split_points(), axis=-1)

    qh = (jax.nn.silu(q.astype(f32)) * HG_DK ** -0.5).reshape(B, L, HG_HEADS, HG_DK)
    f = lb + (1.0 - lb) * jax.nn.sigmoid(f_logit.astype(f32))
    logf = jnp.log(f).reshape(B, L, HG_HEADS, HG_DK)
    kh = (1.0 - f).reshape(B, L, HG_HEADS, HG_DK)
    vh = i_in.astype(f32).reshape(B, L, HG_HEADS, HG_DV)
    pad = HG_CHUNK - N_META
    padw = ((0, 0), (pad, 0), (0, 0), (0, 0))
    o = _hgrn2_chunkwise(jnp.pad(qh, padw), jnp.pad(logf, padw),
                         jnp.pad(kh, padw), jnp.pad(vh, padw))[:, pad:]
    o = o * lax.rsqrt(jnp.mean(o * o, axis=-1, keepdims=True) + EPS)
    o = o.reshape(B, L, HG_WIDTH) * hg_norm.astype(f32) * jax.nn.silu(g_out.astype(f32))
    y_hg = o.astype(u.dtype) @ hg_w_proj

    us = s5_u.astype(f32).reshape(B, L, S5_GROUPS, S5_GROUP)
    ys = _s5_scan(us, s5_lam_re, s5_lam_im, s5_log_step, s5_b_re, s5_b_im,
                  s5_c_re, s5_c_im, s5_d)
    z = jax.nn.gelu(ys.reshape(B, L, S5_WIDTH)).astype(u.dtype)
    y_s5 = (z @ s5_w_glu_a) * jax.nn.sigmoid(z @ s5_w_glu_b)

    merged = jax.nn.sigmoid(gate_hg) * y_hg + jax.nn.sigmoid(gate_s5) * y_s5
    return merged @ w_out

def setup_inputs(seed: int = 0) -> dict:
    key = jax.random.key(seed)
    ks = jax.random.split(key, 32)
    f32 = jnp.float32

    def nrm(k, shape, scale):
        return jax.random.normal(k, shape, f32) * scale

    def gain(k, shape):
        return 1.0 + 0.02 * jax.random.normal(k, shape, f32)

    Ld = DEPTH
    n_idx = jnp.arange(S5_STATE, dtype=f32)
    return {
        "x": nrm(ks[0], (BATCH, SEQ, D_MODEL), 1.0),
        "meta_tokens": nrm(ks[1], (N_META, D_MODEL), 1.0),
        "norm_ffn1": gain(ks[2], (Ld, D_MODEL)),
        "ffn1_w_gate": nrm(ks[3], (Ld, D_MODEL, D_FF), D_MODEL ** -0.5),
        "ffn1_w_up": nrm(ks[4], (Ld, D_MODEL, D_FF), D_MODEL ** -0.5),
        "ffn1_w_down": nrm(ks[5], (Ld, D_FF, D_MODEL), D_FF ** -0.5),
        "norm_mix": gain(ks[6], (Ld, D_MODEL)),
        "w_in": nrm(ks[7], (Ld, D_MODEL, IN_COLS), D_MODEL ** -0.5),
        "hg_lower_bounds": nrm(ks[8], (Ld + 1, HG_K), 0.1),
        "hg_norm": gain(ks[9], (Ld, HG_WIDTH)),
        "hg_w_proj": nrm(ks[10], (Ld, HG_WIDTH, D_MODEL), HG_WIDTH ** -0.5),
        "s5_lam_re": -0.5 + nrm(ks[11], (Ld, S5_GROUPS, S5_STATE), 0.01),
        "s5_lam_im": math.pi * n_idx + nrm(ks[12], (Ld, S5_GROUPS, S5_STATE), 0.01),
        "s5_log_step": jax.random.uniform(ks[13], (Ld, S5_GROUPS), f32,
                                          math.log(DT_MIN), math.log(DT_MAX)),
        "s5_b_re": nrm(ks[14], (Ld, S5_GROUPS, S5_STATE, S5_GROUP), (2 * S5_GROUP) ** -0.5),
        "s5_b_im": nrm(ks[15], (Ld, S5_GROUPS, S5_STATE, S5_GROUP), (2 * S5_GROUP) ** -0.5),
        "s5_c_re": nrm(ks[16], (Ld, S5_GROUPS, S5_GROUP, S5_STATE), (2 * S5_STATE) ** -0.5),
        "s5_c_im": nrm(ks[17], (Ld, S5_GROUPS, S5_GROUP, S5_STATE), (2 * S5_STATE) ** -0.5),
        "s5_d": nrm(ks[18], (Ld, S5_GROUPS, S5_GROUP), 1.0),
        "s5_w_glu_a": nrm(ks[19], (Ld, S5_WIDTH, D_MODEL), S5_WIDTH ** -0.5),
        "s5_w_glu_b": nrm(ks[20], (Ld, S5_WIDTH, D_MODEL), S5_WIDTH ** -0.5),
        "w_out": nrm(ks[21], (Ld, D_MODEL, D_MODEL), D_MODEL ** -0.5),
        "norm_ffn2": gain(ks[22], (Ld, D_MODEL)),
        "ffn2_w_gate": nrm(ks[23], (Ld, D_MODEL, D_FF), D_MODEL ** -0.5),
        "ffn2_w_up": nrm(ks[24], (Ld, D_MODEL, D_FF), D_MODEL ** -0.5),
        "ffn2_w_down": nrm(ks[25], (Ld, D_FF, D_MODEL), D_FF ** -0.5),
        "norm_final": gain(ks[26], (D_MODEL,)),
    }

def reference(x, meta_tokens, norm_ffn1, ffn1_w_gate, ffn1_w_up, ffn1_w_down, norm_mix,
              w_in, hg_lower_bounds, hg_norm, hg_w_proj, s5_lam_re, s5_lam_im, s5_log_step,
              s5_b_re, s5_b_im, s5_c_re, s5_c_im, s5_d, s5_w_glu_a, s5_w_glu_b, w_out,
              norm_ffn2, ffn2_w_gate, ffn2_w_up, ffn2_w_down, norm_final):
    B = x.shape[0]
    meta = jnp.broadcast_to(meta_tokens.astype(x.dtype)[None], (B, N_META, D_MODEL))
    h = jnp.concatenate([meta, x], axis=1)
    lbs = jnp.cumsum(jax.nn.softmax(hg_lower_bounds.astype(jnp.float32), axis=0), axis=0)
    for l in range(DEPTH):
        h = h + 0.5 * _swiglu(_rms_norm(h, norm_ffn1[l]), ffn1_w_gate[l], ffn1_w_up[l], ffn1_w_down[l])
        mix = _mixer(_rms_norm(h, norm_mix[l]), lbs[l], w_in[l], hg_norm[l], hg_w_proj[l],
                     s5_lam_re[l], s5_lam_im[l], s5_log_step[l], s5_b_re[l], s5_b_im[l],
                     s5_c_re[l], s5_c_im[l], s5_d[l], s5_w_glu_a[l], s5_w_glu_b[l], w_out[l])
        h = h + mix.astype(h.dtype)
        h = h + 0.5 * _swiglu(_rms_norm(h, norm_ffn2[l]), ffn2_w_gate[l], ffn2_w_up[l], ffn2_w_down[l])
    return _rms_norm(h, norm_final)[:, N_META:]


_drawn_inputs = setup_inputs


def setup_inputs(seed=0):
    import zlib

    import numpy as np

    out = dict(_drawn_inputs(seed))
    spreads = {}
    factors = {'meta_tokens': 2.78,
     'norm_ffn1': 6.141,
     'norm_mix': 5.666,
     'hg_lower_bounds': 8.0,
     'hg_norm': 21.989,
     's5_lam_re': 64.0,
     's5_lam_im': 40.184,
     's5_log_step': 41.8,
     's5_b_re': 56.968,
     's5_b_im': 56.792,
     's5_c_re': 56.224,
     's5_c_im': 55.656,
     'norm_ffn2': 23.826,
     'norm_final': 8.408}
    for name, (base, spread) in spreads.items():
        noise = np.random.default_rng([zlib.crc32(name.encode()), seed]).standard_normal(out[name].shape)
        drawn = base * np.exp(spread * noise) if base else spread * noise
        out[name] = __import__('jax').numpy.asarray(drawn.astype(out[name].dtype))
    for name, factor in factors.items():
        out[name] = (out[name] * factor).astype(out[name].dtype)
    return out
```

```python
import concourse.bass as bass
from concourse import mybir
from contextlib import ExitStack

P = 128
D = 2048
DT = D // P
META, SEQ = 16, 256
T = META + SEQ
FF = 5632
HEADS, DK = 12, 128
HG = HEADS * DK
GROUPS, GP, STATE = 32, 16, 64
S5W = GROUPS * GP
UT = S5W // P
ST = GROUPS * STATE // P
SPU = ST // UT
EPS = 1e-6
LEVELS = 8

KT, NC = 4, 256
RING = 4
LEAD = 3
FF_BLOCKS = FF // NC
HALVES = (12, 10)
HT = HALVES[0] * 2
HG_BLOCKS = HG // NC
U_BLOCK = 4 * HG_BLOCKS
GATE_BLOCK = U_BLOCK + S5W // NC
GATES = 2 * D // NC
GA = HEADS - HG_BLOCKS
GB = GATES - GA

FFN_QUADS = 2 * FF_BLOCKS + 2 * (FF // (KT * P))
Q_U = FFN_QUADS
Q_SCAN = Q_U + S5W // NC
Q_REST = Q_SCAN + ST
Q_HEADS = Q_REST + 3 * HG_BLOCKS - ST
Q_GATES = Q_HEADS + HEADS
Q_GLU = Q_GATES + GB
Q_PROJ = Q_GLU + 4 * (S5W // (KT * P))
Q_OUT = Q_PROJ + 2 * (HG // (KT * P))
Q_FFN2 = Q_OUT + 2 * (D // (KT * P))
UNITS = 4 * (Q_FFN2 + FFN_QUADS)
PASS_GLU, PASS_PROJ, PASS_OUT, PASS_FFN2 = 4, 8, 10, 12
M_HEADS = 20
M_GATES = M_HEADS + HEADS

PI = 3.14159265358979
TWO_PI_PARTS = (6.28125, 0.0019340515136718750, 1.2556659146e-06)
INV_TWO_PI = 0.15915494309189535
ROUNDER = 12582912.0
GELU_A, GELU_B = 0.044715, 1.5957691216057308


class Tally:

    def __init__(self, engine, sem):
        self.engine, self.sem, self.base, self.n = engine, sem, 0, 0

    def __call__(self, ins):
        ins.then_inc(self.sem, 1)
        self.n += 1

    def join(self):
        self.engine.wait_ge(self.sem, self.base + self.n)

    def turn(self, i, per):
        self.start, self.per = self.n + (self.base if isinstance(self.base, int) else 0), per
        self.base, self.n = i * per + self.start, 0

    def done(self, times):
        assert self.n == self.per, (self.n, self.per)
        self.base, self.n = self.start + times * self.per, 0


def program(nc, xT, metaT, gains, ffn1, w_in, hg_lb, hg_norm, w_proj, s5v, s5b, s5c, s5d, w_glu, w_out, ffn2, outT):
    f32, f32r, i32 = mybir.dt.float32, mybir.dt.float32r, mybir.dt.int32
    bf16 = mybir.dt.bfloat16
    ALU, ACT, AX = mybir.AluOpType, mybir.ActivationFunctionType, mybir.AxisListType
    MUL, ADD, SUB = ALU.mult, ALU.add, ALU.subtract
    ds = bass.ds

    top = ExitStack()
    with top:
        def sem(name):
            return top.enter_context(nc.semaphore(name))

        def sb(name, shape, dt=f32):
            return top.enter_context(nc.sbuf_tensor(name, shape, dt))

        raw = sb("raw", [P, RING, KT, NC])
        w_hi = sb("w_hi", [P, RING, KT, NC], f32r)
        w_lo = sb("w_lo", [P, RING, KT, NC], f32r)
        h = sb("h", [P, DT, T])
        x_hi = sb("x_hi", [P, DT, T], f32r)
        x_lo = sb("x_lo", [P, DT, T], f32r)
        gain = sb("gain", [P, 4, DT])
        ones = sb("ones", [P, P])
        ident = sb("ident", [P, P])
        scr = sb("scr", [P, 6, T])
        lb = sb("lb", [P, 2, HEADS])
        hgn = sb("hgn", [P, HEADS])
        dsk = sb("dsk", [P, UT])
        mag = sb("mag", [P, ST])
        ss = sb("ss", [P, 2, 2])
        small = sb("small", [P, 3])
        ps = top.enter_context(nc.psum_tensor("ps", [P, 8, 512], f32))

        def at(offset, name, shape, dt=f32):
            with ExitStack() as c:
                if offset:
                    c.enter_context(nc.sbuf_tensor("below_" + name, [P, offset], f32))
                return c.enter_context(nc.sbuf_tensor(name, shape, dt))

        TAB = 2 * HT * T + 2016
        h_hi = at(0, "h_hi", [P, HT, T], f32r)
        h_lo = at(HT * T, "h_lo", [P, HT, T], f32r)
        sv = at(2 * HT * T, "sv", [P, 14, ST])
        lbt = at(2 * HT * T + 1760, "lbt", [P, 3, HEADS])
        bd = at(2 * HT * T + 224, "bd", [P, 2, ST, 2 * GP])
        btmp = at(2 * HT * T + 1248, "btmp", [P, ST * 32])
        bprod = at(2 * HT * T + 1760, "bprod", [P, ST, GP])
        e_re = at(TAB, "e_re", [P, ST, T])
        e_im = at(TAB + ST * T, "e_im", [P, ST, T])
        bt = at(TAB + 2 * ST * T, "bt", [P, UT, 2, P])
        cd = at(TAB + 2 * ST * T + 1024, "cd", [P, ST, 2, 2 * GP])
        QFV = 3 * HEADS * T
        qfv = at(0, "qfv", [P, 3 * HEADS, T])
        ys = at(QFV, "ys", [P, UT, SEQ])
        U5 = QFV + UT * SEQ
        u5 = at(U5, "u5", [P, UT, T])
        st_u = at(U5 + UT * T, "st_u", [P, T])
        st_b = at(U5 + UT * T + T, "st_b", [P, 2, P])
        st_c = at(U5 + UT * T + T + 256, "st_c", [P, SPU, 2, 2 * GP])
        sx = at(U5 + UT * T + T + 512, "sx", [P, 2, T])
        assert U5 + UT * T + T + 512 + 2 * T <= TAB
        gates_a = at(QFV, "gates_a", [P, 2 * GA, SEQ])
        z_hi = at(QFV + 3072, "z_hi", [P, UT, SEQ], f32r)
        z_lo = at(QFV + 4096, "z_lo", [P, UT, SEQ], f32r)
        gout = at(QFV + 5120, "gout", [P, HEADS, SEQ])
        HD = QFV + 5120 + 3072
        qs = at(HD, "qs", [P, LEVELS + 1, SEQ])
        ks = at(HD + 2304, "ks", [P, LEVELS, T])
        fm = at(HD + 2304 + 2176, "fm", [P, 560])
        mask = at(HD + 5040, "mask", [P, LEVELS, P], bf16)
        prod = at(HD + 5552, "prod", [P, LEVELS, P])
        att = at(HD + 6576, "att", [P, 3, P])
        att_m = at(HD + 6960, "att_m", [META, 2, P])
        v_tok = at(HD + 7216, "v_tok", [P, 2, P])
        v_meta = at(HD + 7472, "v_meta", [META, P])
        o_hi = at(HEADS * T, "o_hi", [P, HEADS, SEQ], f32r)
        o_lo = at(HEADS * T + 3072, "o_lo", [P, HEADS, SEQ], f32r)
        gates_b = at(HD, "gates_b", [P, 2 * GB, SEQ])
        sgs = at(HD + 5120, "sgs", [P, 3, SEQ])
        y_a = at(QFV + 5120, "y_a", [P, 8, SEQ])
        y_b = at(HD + 5120, "y_b", [P, 8, SEQ])
        ybuf = (y_a, y_b)

        raw_ready = [sem(f"raw_ready{j}") for j in range(RING)]
        hi_ready = sem("hi_ready")
        lo_ready = sem("lo_ready")
        unit_done = sem("unit_done")
        x_in = [sem(f"x_in{c}") for c in range(4)]
        meta_in = sem("meta_in")
        small_in = [sem(f"small_in{c}") for c in range(9)]
        consts = sem("consts")
        dve_step = sem("dve_step")
        pool_step = sem("pool_step")
        act_step = sem("act_step")
        sq_ready = sem("sq_ready")
        sq_used = sem("sq_used")
        summed = sem("summed")
        lb_exp = sem("lb_exp")
        root_ready = sem("root_ready")
        xf_ready = sem("xf_ready")
        xhi_ready = sem("xhi_ready")
        x_ready = sem("x_ready")
        sig_ready = sem("sig_ready")
        gated = sem("gated")
        hidden = sem("hidden")
        hhi_ready = sem("hhi_ready")
        h_ready = sem("h_ready")
        pair_out = sem("pair_out")
        block_out = sem("block_out")
        sv_act = sem("sv_act")
        sv_pool = sem("sv_pool")
        den_inv = sem("den_inv")
        bbar_ready = sem("bbar_ready")
        bt_psum = sem("bt_psum")
        bt_out = sem("bt_out")
        tables = sem("tables")
        staged = sem("staged")
        bu_done = sem("bu_done")
        bu_taken = sem("bu_taken")
        scanned = sem("scanned")
        cx_done = sem("cx_done")
        ys_done = sem("ys_done")
        z_arg = sem("z_arg")
        z_sig = sem("z_sig")
        z_val = sem("z_val")
        zhi_ready = sem("zhi_ready")
        z_ready = sem("z_ready")
        head_sig = sem("head_sig")
        v_staged = sem("v_staged")
        levels = sem("levels")
        mask_ready = sem("mask_ready")
        scored = sem("scored")
        v_ready = sem("v_ready")
        att_ready = sem("att_ready")
        o_done = sem("o_done")
        ss_ready = sem("ss_ready")
        rr_ready = sem("rr_ready")
        on_ready = sem("on_ready")
        ot_psum = sem("ot_psum")
        ot_done = sem("ot_done")
        sgo_ready = sem("sgo_ready")
        og_ready = sem("og_ready")
        ohi_ready = sem("ohi_ready")
        o_ready = sem("o_ready")
        glu_sig = sem("glu_sig")
        merged = sem("merged")
        mhi_ready = sem("mhi_ready")
        m_ready = sem("m_ready")
        y_final = sem("y_final")
        stored = [sem(f"stored{c}") for c in range(4)]

        block = top.enter_context(nc.Block())

        @block.sync
        def _(sp):
            for c in range(4):
                sp.dma_start(h[:, 4 * c:4 * c + 4, META:T],
                             xT.rearrange("(k p) t -> p k t", p=P)[:, 4 * c:4 * c + 4, :]).then_inc(x_in[c], 16)

            def load(j, w, group, col, u):
                sp.wait_ge(lo_ready, u + 1)
                sp.dma_start(raw[:, j, :, :],
                             w.rearrange("(g t p) n -> p g t n", t=KT, p=P)[:, ds(group, 1), :, ds(col, NC)]
                             .rearrange("p g t n -> p (g t) n")).then_inc(raw_ready[j], 16)

            def column_block(w, col, q):
                for j in range(4):
                    load(j, w, j, col, 4 * q + j)

            def passes(w, first_group, groups, q):
                for p in range(2):
                    with sp.Fori(0, groups) as g:
                        for j in range(4):
                            load(j, w, g + first_group, (4 * p + j) * NC, (g + q) * 4 + j)
                    q += groups
                return q

            def ffn(w_gate, w_up, w_down, q):
                first = 0
                for blocks in HALVES:
                    with sp.Fori(0, blocks) as b:
                        column_block(w_gate, (b + first) * NC, b * 2 + q)
                        column_block(w_up, (b + first) * NC, b * 2 + q + 1)
                    q += 2 * blocks
                    q = passes(w_down, first // 2, blocks // 2, q)
                    first += blocks

            def columns(first, n, q):
                with sp.Fori(0, n) as b:
                    column_block(w_in, (b + first) * NC, b + q)

            ffn(*ffn1, 0)
            columns(U_BLOCK, 2, Q_U)
            columns(0, U_BLOCK, Q_SCAN)
            columns(GATE_BLOCK, GATES, Q_HEADS + HG_BLOCKS)
            for p in range(2):
                for s in range(2):
                    for j in range(4):
                        load(j, w_glu[s], 0, (4 * p + j) * NC, 4 * (Q_GLU + 2 * p + s) + j)
            passes(w_proj, 0, HG // (KT * P), Q_PROJ)
            passes(w_out, 0, D // (KT * P), Q_OUT)
            ffn(*ffn2, Q_FFN2)
            for c in range(4):
                sp.wait_ge(y_final, 4 * c + 4)
                sp.dma_start(outT.rearrange("(k p) t -> p k t", p=P)[:, 4 * c:4 * c + 4, :],
                             h[:, 4 * c:4 * c + 4, META:T]).then_inc(stored[c], 16)
            for c in range(4):
                sp.wait_ge(stored[c], 16)

        @block.tensor
        def _(pe):
            pe.sem_inc(unit_done, RING)
            pe.sem_inc(cx_done, 1)

            def unit(j, u, banks, n, rhs, start, stop):
                pe.wait_ge(lo_ready, u + RING + 1)
                for c in range(2):
                    out = ps[:, banks + c, 0:n]
                    for k in range(KT):
                        hi, lo = w_hi[:, j, k, c * P:(c + 1) * P], w_lo[:, j, k, c * P:(c + 1) * P]
                        x_h, x_l = rhs(k)
                        pe.matmul(out, hi, x_h, start=start and k == 0, stop=False)
                        pe.matmul(out, hi, x_l, start=False, stop=False)
                        last = pe.matmul(out, lo, x_h, start=False, stop=stop and k == KT - 1)
                last.then_inc(unit_done, 1)

            def rows(hi, lo, first, c0, n):
                return lambda k: (hi[:, first + k, c0:c0 + n], lo[:, first + k, c0:c0 + n])

            def column_block(q, banks, c0, x_need, between=None):
                for j in range(4):
                    pe.wait_ge(x_ready, x_need + 4 * j + 4)
                    unit(j, 4 * q + j, banks, T - c0, rows(x_hi, x_lo, 4 * j, c0, T - c0), j == 0, j == 3)
                    if between:
                        between(j)

            def one_pass(index, q, groups, hi, lo, c0, n, need):
                def quad(g, start, stop):
                    need(g)
                    for j in range(4):
                        if start and index:
                            pe.wait_ge(pair_out, 4 * (index - 1) + j + 1)
                        def rhs(k):
                            if isinstance(g, int):
                                return hi[:, 4 * g + k, c0:c0 + n], lo[:, 4 * g + k, c0:c0 + n]
                            return (hi[:, ds(g * 4 + k, 1), c0:c0 + n].rearrange("p a t -> p (a t)"),
                                    lo[:, ds(g * 4 + k, 1), c0:c0 + n].rearrange("p a t -> p (a t)"))
                        unit(j, (g + q) * 4 + j, 2 * j, n, rhs, start, stop)
                quad(0, True, groups == 1)
                if groups > 2:
                    with pe.Fori(1, groups - 1) as g:
                        quad(g, False, False)
                if groups > 1:
                    quad(groups - 1, False, True)

            def norm(index, c0):
                if index:
                    passes = (0, PASS_GLU, PASS_FFN2, 16)[index]
                    pe.wait_ge(pair_out, 4 * passes - 3)
                pe.wait_ge(summed, 6 * index + 6)
                for c in range(2):
                    pe.matmul(ps[:, 0, 0:T - c0], ones[:, :], scr[:, 4 + c, c0:T], start=c == 0, stop=False)
                pe.wait_ge(sq_ready, 8 * index + 8)
                for c in range(2):
                    last = pe.matmul(ps[:, 0, 0:T - c0], ones[:, :], scr[:, 2 + c, c0:T], start=False, stop=c == 1)
                last.then_inc(sq_used, 1)

            def ffn(f, c0, q):
                first, index = 0, f * PASS_FFN2
                for blocks in HALVES:
                    done = f * FF_BLOCKS + first
                    if index:
                        pe.wait_ge(pair_out, 4 * index)
                    with pe.Fori(0, blocks) as b:
                        pe.wait_ge(gated, b + done + 1)
                        column_block(b * 2 + q, 0, c0, f * 2 * DT)
                        pe.wait_ge(hidden, b + done + 1)
                        column_block(b * 2 + q + 1, 2, c0, f * 2 * DT)
                    q += 2 * blocks
                    for p in range(2):
                        if p == 0:
                            pe.wait_ge(gated, 1 + done + blocks)
                            pe.wait_ge(hidden, 1 + done + blocks)
                        one_pass(index, q, blocks // 2, h_hi, h_lo, c0, T - c0,
                                 lambda g: pe.wait_ge(h_ready, g * 2 + done + 2))
                        q += blocks // 2
                        index += 1
                    first += blocks

            pe.wait_ge(consts, 2)
            norm(0, 0)
            pe.wait_ge(root_ready, 1)
            ffn(0, 0, 0)
            norm(1, 0)
            pe.wait_ge(pair_out, 4 * PASS_GLU)
            pe.wait_ge(bbar_ready, 1)
            for ut in range(UT):
                for r in range(2):
                    last = pe.transpose(ps[:, 4 + r, ut * P:(ut + 1) * P],
                                        bd[:, r, SPU * ut:SPU * (ut + 1), :].rearrange("p a b -> p (a b)"), ident[:, :])
            last.then_inc(bt_psum, 1)
            pe.wait_ge(root_ready, 2)
            for m in range(2):
                column_block(Q_U + m, 2 * m, 0, DT)
            pe.wait_ge(block_out, 2)
            with pe.Fori(0, UT) as ut:
                def project_in(jj, turn):
                    for r in range(2):
                        last = pe.matmul(ps[:, 4 + r, 0:T], st_b[32 * jj:32 * jj + 32, r, :], st_u[32 * jj:32 * jj + 32, :],
                                         start=True, stop=True)
                    last.then_inc(bu_done, 1)
                pe.wait_ge(staged, ut + 1)
                pe.wait_ge(bu_taken, ut * SPU + 1)
                project_in(0, ut)
                for jj in range(SPU):
                    pe.wait_ge(block_out, ut * SPU + jj + 1)

                    def between(j, jj=jj):
                        if j == 2 and jj < SPU - 1:
                            pe.wait_ge(bu_taken, ut * SPU + jj + 2)
                            project_in(jj + 1, ut)
                    column_block(ut * SPU + Q_SCAN + jj, 2 * (jj % 2), 0, DT, between)
                    pe.wait_ge(scanned, ut * SPU + jj + 1)
                    if jj == 0:
                        pe.wait_ge(ys_done, ut + 1)
                    for r in range(2):
                        last = pe.matmul(ps[32 * jj:32 * jj + 32, 6, 0:SEQ], st_c[:, jj, r, :], sx[:, r, META:T],
                                         start=r == 0, stop=r == 1)
                    last.then_inc(cx_done, 1)
            for m in (18, 19):
                pe.wait_ge(block_out, m - 1)
                column_block(Q_U + m, 2 * (m % 2), 0, DT)
            pe.wait_ge(block_out, M_HEADS)
            pe.wait_ge(ys_done, UT + 1)

            def score(hd):
                pe.wait_ge(levels, hd + 1)
                pe.wait_ge(v_staged, hd + 1)
                for b in range(2):
                    pe.transpose(ps[:, 2, b * P:(b + 1) * P], scr[:, 2, META + b * P:META + (b + 1) * P], ident[:, :])
                pe.transpose(ps[0:META, 2, 2 * P:3 * P], scr[:, 2, 0:META], ident[:, :])
                blk = [slice(META + b * P, META + (b + 1) * P) for b in range(2)]
                pe.matmul(ps[:, 3, 0:P], ks[:, 7, blk[0]], qs[:, 8, P:2 * P], start=True, stop=True)
                pe.matmul(ps[0:META, 3, P:2 * P], ks[:, 4, 0:META], qs[:, 8, 0:P], start=True, stop=True)
                pe.matmul(ps[0:META, 3, 2 * P:3 * P], ks[:, 5, 0:META], qs[:, 8, P:2 * P], start=True, stop=True)
                for b in range(2):
                    for l in range(LEVELS):
                        if b and l == 4:
                            pe.wait_ge(ot_done, hd + 1)
                        k = max(l - 1, 0)
                        last = pe.matmul(ps[:, 4 + 2 * b + l // 4, (l % 4) * P:(l % 4 + 1) * P], ks[:, k, blk[b]],
                                         qs[:, l, b * P:(b + 1) * P], start=True, stop=True)
                last.then_inc(scored, 1)

            def mix(hd):
                pe.wait_ge(att_ready, hd + 1)
                pe.wait_ge(v_ready, hd + 1)
                pe.matmul(ps[:, 2, 0:P], att[:, 0, :], v_tok[:, 0, :], start=True, stop=False)
                pe.matmul(ps[:, 2, 0:P], att_m[0:META, 0, :], v_meta[0:META, :], start=False, stop=True)
                pe.matmul(ps[:, 2, P:2 * P], att[:, 1, :], v_tok[:, 1, :], start=True, stop=False)
                pe.matmul(ps[:, 2, P:2 * P], att[:, 2, :], v_tok[:, 0, :], start=False, stop=False)
                pe.matmul(ps[:, 2, P:2 * P], att_m[0:META, 1, :], v_meta[0:META, :], start=False, stop=True)\
                    .then_inc(o_done, 1)

            def back(hd):
                pe.wait_ge(on_ready, hd + 1)
                for b in range(2):
                    last = pe.transpose(ps[:, 7, b * P:(b + 1) * P], scr[:, 4, b * P:(b + 1) * P], ident[:, :])
                last.then_inc(ot_psum, 1)

            def head(hd):
                score(hd)
                pe.wait_ge(block_out, hd + M_HEADS)
                column_block(hd + Q_HEADS, 0, META, DT, lambda j: mix(hd) if j == 2 else None)
                back(hd)

            with pe.Fori(0, HEADS) as hd:
                head(hd)
            pe.wait_ge(ot_done, HEADS + 1)
            pe.wait_ge(block_out, M_GATES)
            with pe.Fori(0, GB // 2) as i:
                for c in range(2):
                    pe.wait_ge(block_out, i * 2 + M_GATES + c - 1)
                    column_block(i * 2 + Q_GATES + c, 2 * c, META, DT)
            pe.wait_ge(block_out, M_GATES + GB)
            for index in range(PASS_GLU, PASS_PROJ):
                one_pass(index, Q_GLU + index - PASS_GLU, 1, z_hi, z_lo, 0, SEQ, lambda g: pe.wait_ge(z_ready, 1))
            for p in range(2):
                one_pass(PASS_PROJ + p, Q_PROJ + 3 * p, 3, o_hi, o_lo, 0, SEQ, lambda g: pe.wait_ge(o_ready, 4))
            for p in range(2):
                one_pass(PASS_OUT + p, Q_OUT + 4 * p, 4, x_hi, x_lo, META, SEQ, lambda g: pe.wait_ge(m_ready, g * 2 + 2))
            norm(2, META)
            pe.wait_ge(root_ready, 3)
            ffn(1, META, Q_FFN2)
            norm(3, META)

        @block.scalar
        def _(act):
            step = Tally(act, act_step)
            act.dma_start(h[:, :, 0:META], metaT.rearrange("(k p) t -> p k t", p=P)).then_inc(meta_in, 16)
            act.dma_start(gain[:, :, :], gains).then_inc(small_in[0], 16)
            act.dma_start(sv[:, 0:3, :], s5v).then_inc(small_in[1], 16)
            act.dma_start(lb[:, :, :], hg_lb).then_inc(small_in[2], 16)
            act.dma_start(hgn[:, :], hg_norm).then_inc(small_in[3], 16)
            act.dma_start(dsk[:, :], s5d).then_inc(small_in[4], 16)
            act.dma_start(btmp[:, 0:2 * ST * GP].rearrange("p (r j c) -> p r j c", r=2, j=ST), s5b).then_inc(small_in[5], 16)

            def split(q, j):
                slot = (j + LEAD) % 4
                if isinstance(q, int) and 4 * q + j + LEAD >= UNITS:
                    return
                q1 = q + (j + LEAD) // 4
                act.wait_ge(raw_ready[slot], q1 * 16 + 16)
                act.wait_ge(unit_done, q * 4 + j + LEAD + 1)
                act.activation(w_hi[:, slot, :, :], raw[:, slot, :, :], ACT.Copy).then_inc(hi_ready, 1)

            def square(index, c0, k):
                if index:
                    passes = (0, PASS_GLU, PASS_FFN2, 16)[index]
                    act.wait_ge(pair_out, 4 * (passes - 2) + k + 1)
                elif k % 2 == 0:
                    act.wait_ge(x_in[k // 2], 16)
                if k >= 3:
                    act.wait_ge(summed, 6 * index + k - 2)
                at_k = 2 * (k % 2) if k else 4
                act.activation(scr[:, at_k:at_k + 2, c0:T], h[:, 2 * k:2 * k + 2, c0:T], ACT.Square).then_inc(sq_ready, 1)

            def norm(index, c0):
                act.wait_ge(sq_used, index + 1)
                act.activation(scr[:, 4, c0:T], ps[:, 0, 0:T - c0], ACT.Sqrt, bias=small[:, 1:2]).then_inc(root_ready, 1)
                if index < 3:
                    for k in range(DT):
                        act.wait_ge(xf_ready, index * DT + k + 1)
                        act.activation(x_hi[:, k, c0:T], scr[:, k % 4, c0:T], ACT.Copy).then_inc(xhi_ready, 1)

            def plain_pass(q, groups, after=None):
                if groups > 1:
                    with act.Fori(0, groups - 1) as g:
                        for j in range(4):
                            split(g + q, j)
                for j in range(4):
                    if j and after:
                        after(j - 1)
                    split(q + groups - 1, j)
                if after:
                    after(3)

            def ffn(f, c0, q, between=None):
                first = 0
                for blocks in HALVES:
                    done = f * FF_BLOCKS + first
                    with act.Fori(0, blocks) as b:
                        for j in range(4):
                            split(b * 2 + q, j)
                        act.wait_ge(unit_done, b * 8 + RING + 4 * q + 4)
                        act.activation(scr[:, 0:2, c0:T], ps[:, 0:2, 0:T - c0], ACT.Sigmoid).then_inc(sig_ready, 1)
                        for j in range(4):
                            split(b * 2 + q + 1, j)
                        act.wait_ge(hidden, b + done + 2)
                        act.activation(h_hi[:, ds(b * 2, 2), c0:T], scr[:, 4:6, c0:T], ACT.Copy).then_inc(hhi_ready, 1)
                    q += 2 * blocks
                    if between and not first:
                        between(0)
                    for p in range(2):
                        plain_pass(q, blocks // 2, (lambda j, p=p: square(1 + 2 * f, c0, 4 * p + j)) if first else None)
                        q += blocks // 2
                        if between and not first:
                            between(1 + p)
                    first += blocks

            def head_inputs(hd):
                def tile(t):
                    return qfv[:, ds(hd + t, 1), :].rearrange("p a t -> p (a t)")
                act.activation(scr[:, 0, 0:SEQ], tile(0)[:, META:T], ACT.Sigmoid)
                act.activation(scr[:, 1, :], tile(HEADS), ACT.Sigmoid).then_inc(head_sig, 1)
                act.activation(scr[:, 2, :], tile(2 * HEADS), ACT.Copy).then_inc(v_staged, 1)

            def parameters(stage):
                if stage == 0:
                    act.wait_ge(small_in[1], 16)
                    act.activation(sv[:, 3, :], sv[:, 2, :], ACT.Exp).then_inc(sv_act, 1)
                    act.wait_ge(dve_step, 3)
                    act.activation(lbt[:, 0:2, :], lbt[:, 0:2, :], ACT.Exp).then_inc(lb_exp, 1)
                elif stage == 1:
                    act.wait_ge(sv_pool, 1)
                    act.activation(mag[:, :], sv[:, 4, :], ACT.Exp).then_inc(sv_act, 1)
                else:
                    act.wait_ge(sv_pool, 2)
                    act.activation(sv[:, 10:12, :], sv[:, 8:10, :], ACT.Sin).then_inc(sv_act, 1)

            act.wait_ge(meta_in, 16)
            act.wait_ge(consts, 2)
            for k in range(DT // 2):
                square(0, 0, k)
            norm(0, 0)
            for u in range(LEAD):
                act.wait_ge(raw_ready[u], 16)
                act.activation(w_hi[:, u, :, :], raw[:, u, :, :], ACT.Copy).then_inc(hi_ready, 1)
            for g in range(2):
                act.dma_start(cd[64 * g:64 * g + 64, :, :, g * GP:(g + 1) * GP], s5c[64 * g:64 * g + 64])\
                    .then_inc(small_in[6 + g], 16)
            ffn(0, 0, 0, parameters)
            norm(1, 0)
            act.wait_ge(bt_psum, 1)
            for r in range(2):
                ins = act.activation(bt[:, :, r, :], ps[:, 4 + r, :].rearrange("p (u s) -> p u s", u=UT), ACT.Copy)
            ins.then_inc(bt_out, 1)

            def take_block(m, out, banks, n, func):
                act.wait_ge(unit_done, (m + Q_U) * 4 + RING + 4)
                act.activation(out, ps[:, banks:banks + 2, 0:n], func).then_inc(block_out, 1)

            for m in range(2):
                for j in range(4):
                    split(Q_U + m, j)
                take_block(m, u5[:, 2 * m:2 * m + 2, :], 2 * m, T, ACT.Copy)
            act.wait_ge(tables, 1)
            act.wait_ge(bt_out, 1)
            with act.Fori(0, UT) as ut:
                act.wait_ge(block_out, 2)
                act.wait_ge(cx_done, ut * SPU + 1)
                act.activation(st_u[:, :], u5[:, ds(ut, 1), :].rearrange("p a t -> p (a t)"), ACT.Copy)
                act.activation(st_b[:, :, :], bt[:, ds(ut, 1), :, :].rearrange("p a r s -> p (a r) s"), ACT.Copy)
                act.activation(st_c[:, :, :, :], cd[:, ds(ut * SPU, SPU), :, :], ACT.Copy).then_inc(staged, 1)
                for jj in range(SPU):
                    for j in range(4):
                        split(ut * SPU + Q_SCAN + jj, j)
                    take_block(ut * SPU + 2 + jj, qfv[:, ds((ut * SPU + jj) * 2, 2), :], 2 * (jj % 2), T, ACT.Copy)
            for m in (18, 19):
                for j in range(4):
                    split(Q_U + m, j)
                    if m == 18 and j == 1:
                        act.wait_ge(z_arg, 1)
                        act.activation(scr[:, 0:4, 0:SEQ], scr[:, 0:4, 0:SEQ], ACT.Sigmoid, scale=GELU_B).then_inc(z_sig, 1)
                    if m == 18 and j == 3:
                        act.wait_ge(z_val, 1)
                        act.activation(z_hi[:, :, :], ys[:, :, :], ACT.Copy).then_inc(zhi_ready, 1)
                    if m == 19 and j == 0:
                        act.wait_ge(z_ready, 1)
                        head_inputs(0)
                take_block(m, qfv[:, 2 * m - 4:2 * m - 2, :], 2 * (m % 2), T, ACT.Copy)

            def beside_head(hd, out, func, following):
                act.wait_ge(scored, hd + 1)
                act.activation(v_tok[:, :, :], ps[:, 2, 0:2 * P].rearrange("p (b v) -> p b v", b=2), ACT.Copy)
                act.activation(v_meta[:, :], ps[0:META, 2, 2 * P:3 * P], ACT.Copy)
                act.activation(att[:, 2, :], ps[:, 3, 0:P], ACT.Copy)
                act.activation(att_m[:, :, :], ps[0:META, 3, P:3 * P].rearrange("p (b v) -> p b v", b=2), ACT.Copy)\
                    .then_inc(v_ready, 1)
                if following:
                    act.wait_ge(levels, hd + 1)
                    head_inputs(hd + 1)
                split(hd + Q_HEADS, 1)
                split(hd + Q_HEADS, 2)
                act.wait_ge(o_done, hd + 1)
                for b in range(2):
                    ins = act.activation(scr[:, 3, b * P:(b + 1) * P], ps[:, 2, b * P:(b + 1) * P], ACT.Square,
                                         accum_out=ss[:, 0, b:b + 1])
                ins.then_inc(ss_ready, 1)
                split(hd + Q_HEADS, 3)
                take_block(hd + M_HEADS, out, 0, SEQ, func)
                if following:
                    split(hd + Q_HEADS + 1, 0)

            split(Q_HEADS, 0)
            with act.Fori(0, HG_BLOCKS) as hd:
                beside_head(hd, gout[:, ds(hd * 2, 2), :], ACT.Copy, True)
            with act.Fori(HG_BLOCKS, HEADS - 1) as hd:
                beside_head(hd, gates_a[:, ds(hd * 2 - HEADS, 2), :], ACT.Sigmoid, True)
            beside_head(HEADS - 1, gates_a[:, HEADS - 2:HEADS, :], ACT.Sigmoid, False)

            def gate_pair(i, c, side=None):
                for j in range(4):
                    split(i * 2 + Q_GATES + c, j)
                    if side:
                        side(j)
                take_block(i * 2 + M_GATES + c, gates_b[:, ds(i * 4 + 2 * c, 2), :], 2 * c, SEQ, ACT.Sigmoid)

            act.wait_ge(ot_done, HEADS + 1)
            with act.Fori(0, 4) as i:
                def side(j):
                    if j == 0:
                        act.activation(sgs[:, :, :], gout[:, ds(i * 3, 3), :], ACT.Sigmoid).then_inc(sgo_ready, 1)
                    if j == 3:
                        act.wait_ge(og_ready, i + 1)
                        act.activation(o_hi[:, ds(i * 3, 3), :], gout[:, ds(i * 3, 3), :], ACT.Copy).then_inc(ohi_ready, 1)
                gate_pair(i, 0, side)
                gate_pair(i, 1)
            gate_pair(4, 0)
            gate_pair(4, 1)

            for index in range(PASS_GLU, PASS_PROJ):
                q = Q_GLU + index - PASS_GLU

                def glu_gate(j, index=index):
                    act.wait_ge(unit_done, 4 * (Q_GLU + index - PASS_GLU) + RING + j + 1)
                    act.activation(ps[:, 2 * j:2 * j + 2, 0:SEQ], ps[:, 2 * j:2 * j + 2, 0:SEQ], ACT.Sigmoid)\
                        .then_inc(glu_sig, 1)
                plain_pass(q, 1, glu_gate if index % 2 else None)
            for p in range(2):
                def take_merged(j, p=p):
                    act.wait_ge(merged, 4 * p + j + 1)
                    act.activation(x_hi[:, 8 * p + 2 * j:8 * p + 2 * j + 2, META:T], ybuf[p][:, 2 * j:2 * j + 2, :],
                                   ACT.Copy).then_inc(mhi_ready, 1)
                plain_pass(Q_PROJ + 3 * p, 3, take_merged)
            for p in range(2):
                plain_pass(Q_OUT + 4 * p, 4, lambda j, p=p: square(2, META, 4 * p + j))
            norm(2, META)
            ffn(1, META, Q_FFN2)
            norm(3, META)


        @block.vector
        def _(dve):
            step = Tally(dve, dve_step)
            tt, ts, stt = dve.tensor_tensor, dve.tensor_scalar, dve.scalar_tensor_tensor
            dve.sem_inc(lo_ready, RING)
            for credit in (gated, hidden, bu_taken, ys_done, ot_done):
                dve.sem_inc(credit, 1)

            def split(q, j):
                slot = (j + LEAD) % 4
                if isinstance(q, int) and 4 * q + j + LEAD >= UNITS:
                    return
                dve.wait_ge(hi_ready, q * 4 + j + LEAD + 1)
                tt(w_lo[:, slot, :, :], raw[:, slot, :, :], w_hi[:, slot, :, :].bitcast(f32), SUB).then_inc(lo_ready, 1)

            def settle(q, j):
                dve.wait_ge(lo_ready, q * 4 + j + LEAD + 1 + RING)

            def norm(index, c0):
                if index:
                    dve.wait_ge(pair_out, 4 * (0, PASS_GLU, PASS_FFN2, 16)[index])
                dve.wait_ge(root_ready, index + 1)
                step(dve.reciprocal(scr[:, 5, c0:T], scr[:, 4, c0:T]))
                step.join()

                def lower(k):
                    dve.wait_ge(xhi_ready, index * DT + k + 1)
                    tt(x_lo[:, k, c0:T], scr[:, k % 4, c0:T], x_hi[:, k, c0:T].bitcast(f32), SUB).then_inc(x_ready, 1)

                for k in range(DT):
                    out = h[:, k, c0:T] if index == 3 else scr[:, k % 4, c0:T]
                    if k >= 4 and index < 3:
                        dve.wait_ge(x_ready, index * DT + k - 3)
                    stt(out, h[:, k, c0:T], gain[:, index, k:k + 1], scr[:, 5, c0:T], MUL, MUL)\
                        .then_inc(y_final if index == 3 else xf_ready, 1)
                    if k and index < 3:
                        lower(k - 1)
                if index < 3:
                    lower(DT - 1)

            def add_squares(index, c0, k):
                dve.wait_ge(sq_ready, 8 * index + k + 1)
                if k > 1:
                    dve.wait_ge(summed, 6 * index + k - 1)
                at_k = 2 * (k % 2)
                tt(scr[:, 4:6, c0:T], scr[:, 4:6, c0:T], scr[:, at_k:at_k + 2, c0:T], ADD).then_inc(summed, 1)

            def plain_pass(q, groups, take, before=None):
                if groups > 1:
                    with dve.Fori(0, groups - 1) as g:
                        for j in range(4):
                            split(g + q, j)
                for j in range(5):
                    if j:
                        if before:
                            before(j - 1)
                        dve.wait_ge(unit_done, 4 * (q + groups - 1) + RING + j)
                        take(j - 1)
                    if j < 4:
                        split(q + groups - 1, j)

            def ffn(f, c0, q, between=None):
                first = 0
                for blocks in HALVES:
                    done = f * FF_BLOCKS + first
                    with dve.Fori(0, blocks) as b:
                        for j in range(4):
                            split(b * 2 + q, j)
                        dve.wait_ge(sig_ready, b + done + 1)
                        tt(scr[:, 2:4, c0:T], ps[:, 0:2, 0:T - c0], scr[:, 0:2, c0:T], MUL).then_inc(gated, 1)
                        for j in range(4):
                            split(b * 2 + q + 1, j)
                        dve.wait_ge(gated, b + done + 2)
                        dve.wait_ge(unit_done, b * 8 + RING + 4 * q + 8)
                        tt(scr[:, 4:6, c0:T], ps[:, 2:4, 0:T - c0], scr[:, 2:4, c0:T], MUL).then_inc(hidden, 1)
                        dve.wait_ge(hhi_ready, b + done + 1)
                        tt(h_lo[:, ds(b * 2, 2), c0:T], scr[:, 4:6, c0:T], h_hi[:, ds(b * 2, 2), c0:T].bitcast(f32), SUB)\
                            .then_inc(h_ready, 1)
                    q += 2 * blocks
                    for p in range(2):
                        def residual(j, p=p):
                            rows = slice(8 * p + 2 * j, 8 * p + 2 * j + 2)
                            stt(h[:, rows, c0:T], ps[:, 2 * j:2 * j + 2, 0:T - c0], 0.5, h[:, rows, c0:T], MUL, ADD)\
                                .then_inc(pair_out, 1)
                        if first:
                            dve.wait_ge(pair_out, 4 * (f * PASS_FFN2 + p + 1))

                        def add(j, p=p):
                            if 4 * p + j >= 2:
                                add_squares(1 + 2 * f, c0, 4 * p + j - 1)
                        plain_pass(q, blocks // 2, residual, add if first else None)
                        q += blocks // 2
                        if between and not first:
                            between(1 + p)
                    first += blocks

            dve.wait_ge(small_in[2], 16)
            step(tt(lbt[:, 2, :], lb[:, 0, :], lb[:, 1, :], ALU.max))
            step.join()
            step(tt(lbt[:, 0, :], lb[:, 0, :], lbt[:, 2, :], SUB))
            step(tt(lbt[:, 1, :], lb[:, 1, :], lbt[:, 2, :], SUB))

            def parameters(stage):
                if stage == 1:
                    dve.wait_ge(lb_exp, 1)
                    step(tt(lbt[:, 2, :], lbt[:, 0, :], lbt[:, 1, :], ADD))
                    step.join()
                    step(dve.reciprocal(lbt[:, 1, :], lbt[:, 2, :]))
                    step.join()
                    step(tt(lb[:, 0, :], lbt[:, 0, :], lbt[:, 1, :], MUL))
                    step.join()
                    step(ts(lb[:, 1, :], lb[:, 0, :], -1.0, 1.0, MUL, ADD))
                if stage == 2:
                    dve.wait_ge(sv_pool, 3)
                    dve.reciprocal(sv[:, 13, :], sv[:, 12, :]).then_inc(den_inv, 1)

            dve.wait_ge(small_in[0], 16)
            for k in range(1, 7):
                add_squares(0, 0, k)
            norm(0, 0)
            for u in range(LEAD):
                dve.wait_ge(hi_ready, u + 1)
                tt(w_lo[:, u, :, :], raw[:, u, :, :], w_hi[:, u, :, :].bitcast(f32), SUB).then_inc(lo_ready, 1)
            ffn(0, 0, 0, parameters)
            norm(1, 0)
            for m in range(2):
                for j in range(4):
                    split(Q_U + m, j)

            dve.wait_ge(tables, 1)
            dve.wait_ge(small_in[4], 16)
            with dve.Fori(0, UT) as ut:
                step.turn(ut, SPU * 12)
                for jj in range(SPU):
                    tile = ut * SPU + jj

                    def e(table, c0):
                        return table[:, ds(ut * SPU + jj, 1), c0:T].rearrange("p a t -> p (a t)")
                    split(tile + Q_SCAN, 0)
                    settle(tile + Q_SCAN, 0)
                    dve.wait_ge(bu_done, tile + 1)
                    step(tt(scr[:, 0, :], ps[:, 4, 0:T], e(e_re, 0), MUL))
                    step(tt(scr[:, 1, :], ps[:, 5, 0:T], e(e_im, 0), MUL))
                    step(tt(scr[:, 2, :], ps[:, 5, 0:T], e(e_re, 0), MUL))
                    tt(scr[:, 3, :], ps[:, 4, 0:T], e(e_im, 0), MUL).then_inc(bu_taken, 1)
                    split(tile + Q_SCAN, 1)
                    dve.wait_ge(bu_taken, tile + 2)
                    step(tt(scr[:, 0, :], scr[:, 0, :], scr[:, 1, :], ADD))
                    step(tt(scr[:, 2, :], scr[:, 2, :], scr[:, 3, :], SUB))
                    step.join()
                    decay = mag[:, ds(tile, 1)].broadcast_to([P, T])
                    step(dve.tensor_tensor_scan(scr[:, 1, :], decay, scr[:, 0, :], 0.0, MUL, ADD))
                    step(dve.tensor_tensor_scan(scr[:, 3, :], decay, scr[:, 2, :], 0.0, MUL, ADD))
                    step.join()
                    split(tile + Q_SCAN, 2)
                    step(tt(scr[:, 0, META:T], scr[:, 1, META:T], e(e_re, META), MUL))
                    step(tt(scr[:, 2, META:T], scr[:, 3, META:T], e(e_im, META), MUL))
                    step(tt(scr[:, 4, META:T], scr[:, 1, META:T], e(e_im, META), MUL))
                    step(tt(scr[:, 5, META:T], scr[:, 3, META:T], e(e_re, META), MUL))
                    step.join()
                    dve.wait_ge(cx_done, tile + 1)
                    step(tt(sx[:, 0, META:T], scr[:, 0, META:T], scr[:, 2, META:T], SUB))
                    tt(sx[:, 1, META:T], scr[:, 4, META:T], scr[:, 5, META:T], ADD).then_inc(scanned, 1)
                    split(tile + Q_SCAN, 3)
                dve.wait_ge(cx_done, ut * SPU + SPU + 1)
                stt(ys[:, ds(ut, 1), :].rearrange("p a t -> p (a t)"),
                    u5[:, ds(ut, 1), META:T].rearrange("p a t -> p (a t)"), dsk[:, ds(ut, 1)], ps[:, 6, 0:SEQ],
                    MUL, ADD).then_inc(ys_done, 1)
            step.done(UT)

            g = scr[:, 0:4, 0:SEQ]
            split(Q_REST, 0)
            dve.wait_ge(ys_done, UT + 1)
            step(tt(g, ys[:, :, :], ys[:, :, :], MUL))
            step.join()
            step(ts(g, g, GELU_A, 1.0, MUL, ADD))
            step.join()
            split(Q_REST, 1)
            tt(g, g, ys[:, :, :], MUL).then_inc(z_arg, 1)
            split(Q_REST, 2)
            dve.wait_ge(z_sig, 1)
            tt(ys[:, :, :], ys[:, :, :], g, MUL).then_inc(z_val, 1)
            split(Q_REST, 3)
            dve.wait_ge(z_val, 1)
            dve.wait_ge(zhi_ready, 1)
            tt(z_lo[:, :, :], ys[:, :, :], z_hi[:, :, :].bitcast(f32), SUB).then_inc(z_ready, 1)

            f_at = (0, 272, 408, 476, 510, 528, 536, 540)

            def level(i):
                m = 1 << i
                c0 = 0 if m < META else META
                n = T - c0
                k_old, k_new = [ks[:, i + d, c0:T].rearrange("p (b s m) -> p b s m", s=2, m=m) for d in range(2)]
                q_old, q_new = [qs[:, i + 1 + d, :].rearrange("p (b s m) -> p b s m", s=2, m=m) for d in range(2)]
                skip = META // m if m < META else (1 if m == META else 0)
                at_k = skip if m >= META else 0
                f_k = fm[:, f_at[i] + at_k:f_at[i] + at_k + n // m].rearrange("p (b s) -> p b s", s=2)
                f_q = fm[:, f_at[i] + skip:f_at[i] + skip + SEQ // m].rearrange("p (b s) -> p b s", s=2)

                def wide(f, nb):
                    return f.unsqueeze(2).broadcast_to([P, nb, m])
                step.join()
                step(tt(k_new[:, :, 0, :], k_old[:, :, 0, :], wide(f_k[:, :, 1], n // m // 2), MUL))
                step(tt(q_new[:, :, 1, :], q_old[:, :, 1, :], wide(f_q[:, :, 0], SEQ // m // 2), MUL))
                step(dve.tensor_copy(k_new[:, :, 1, :], k_old[:, :, 1, :]))
                step(dve.tensor_copy(q_new[:, :, 0, :], q_old[:, :, 0, :]))
                step(tt(fm[:, f_at[i + 1]:f_at[i + 1] + n // m // 2], f_k[:, :, 0], f_k[:, :, 1], MUL))

            def head_levels(hd, part):
                if part == 0:
                    dve.wait_ge(head_sig, hd + 1)
                    step(stt(qs[:, 0, :], qfv[:, ds(hd, 1), META:T].rearrange("p a t -> p (a t)"), DK ** -0.5,
                             scr[:, 0, 0:SEQ], MUL, MUL))
                    step(ts(fm[:, 0:T], scr[:, 1, :], lb[:, 1, ds(hd, 1)], lb[:, 0, ds(hd, 1)], MUL, ADD))
                    step.join()
                    step(ts(ks[:, 0, :], fm[:, 0:T], -1.0, 1.0, MUL, ADD))
                    step(tt(qs[:, 1, :], qs[:, 0, :], fm[:, META:T], MUL))
                    for i in range(3):
                        level(i)
                else:
                    for i in range(3, 7):
                        level(i)
                    step.join()
                    ts(ks[:, 5, 0:META], ks[:, 4, 0:META], fm[:, f_at[7]:f_at[7] + 1], None, MUL).then_inc(levels, 1)

            split(Q_REST + 1, 0)
            split(Q_REST + 1, 1)
            dve.wait_ge(mask_ready, 1)
            head_levels(0, 0)
            split(Q_REST + 1, 2)
            head_levels(0, 1)
            split(Q_REST + 1, 3)

            def head(hd, following):
                def masked(b):
                    step(tt(prod[:, :, :], ps[:, 4 + 2 * b:6 + 2 * b, :].rearrange("p b (l t) -> p (b l) t", l=4),
                            mask[:, :, :], MUL))
                    step.join()
                    ins = dve.tensor_reduce(att[:, b, :], prod[:, :, :].rearrange("p l t -> p t l"), AX.X, ADD)
                    if b:
                        ins.then_inc(att_ready, 1)
                    else:
                        step(ins)
                dve.wait_ge(scored, hd + 1)
                masked(0)
                step.join()
                masked(1)
                if following:
                    head_levels(hd + 1, 0)
                    head_levels(hd + 1, 1)
                dve.wait_ge(rr_ready, hd + 1)
                for b in range(2):
                    ins = ts(scr[:, 4, b * P:(b + 1) * P], ps[:, 2, b * P:(b + 1) * P], ss[:, 1, b:b + 1], None, MUL)
                ins.then_inc(on_ready, 1)
                split(hd + Q_HEADS, 1)
                dve.wait_ge(ot_psum, hd + 1)
                ts(qfv[:, ds(hd, 1), META:T].rearrange("p a t -> p (a t)"), ps[:, 7, 0:SEQ], hgn[:, ds(hd, 1)], None, MUL)\
                    .then_inc(ot_done, 1)
                split(hd + Q_HEADS, 2)
                split(hd + Q_HEADS, 3)
                if following:
                    split(hd + Q_HEADS + 1, 0)

            split(Q_HEADS, 0)
            dve.wait_ge(small_in[3], 16)
            with dve.Fori(0, HEADS - 1) as hd:
                step.turn(hd, 42)
                head(hd, True)
            step.done(HEADS - 1)
            head(HEADS - 1, False)

            dve.wait_ge(ot_done, HEADS + 1)
            with dve.Fori(0, 4) as i:
                step.turn(i, 1)
                g3 = gout[:, ds(i * 3, 3), :]
                split(i * 2 + Q_GATES, 0)
                dve.wait_ge(sgo_ready, i + 1)
                step(tt(g3, g3, sgs[:, :, :], MUL))
                split(i * 2 + Q_GATES, 1)
                step.join()
                tt(g3, g3, qfv[:, ds(i * 3, 3), META:T], MUL).then_inc(og_ready, 1)
                split(i * 2 + Q_GATES, 2)
                split(i * 2 + Q_GATES, 3)
                split(i * 2 + Q_GATES + 1, 0)
                dve.wait_ge(og_ready, i + 1)
                dve.wait_ge(ohi_ready, i + 1)
                tt(o_lo[:, ds(i * 3, 3), :], g3, o_hi[:, ds(i * 3, 3), :].bitcast(f32), SUB).then_inc(o_ready, 1)
                for j in range(1, 4):
                    split(i * 2 + Q_GATES + 1, j)
            step.done(4)
            for c in range(2):
                for j in range(4):
                    split(Q_GATES + 8 + c, j)

            dve.wait_ge(block_out, M_GATES + GB)
            for index in range(PASS_GLU, PASS_PROJ):
                p = (index - PASS_GLU) // 2
                y = ybuf[p]

                def take_a(j, y=y):
                    dve.tensor_copy(y[:, 2 * j:2 * j + 2, :], ps[:, 2 * j:2 * j + 2, 0:SEQ]).then_inc(pair_out, 1)

                def take_b(j, y=y, p=p):
                    dve.wait_ge(glu_sig, 4 * p + j + 1)
                    yy = y[:, 2 * j:2 * j + 2, :]
                    tt(yy, ps[:, 2 * j:2 * j + 2, 0:SEQ], yy, MUL).then_inc(pair_out, 1)
                    dve.wait_ge(pair_out, 4 * (PASS_GLU + 2 * p + 1) + j + 1)
                    t = DT + 8 * p + 2 * j - 2 * GA
                    step(tt(yy, yy, gates_b[:, t:t + 2, :], MUL))
                if index % 2:
                    dve.wait_ge(pair_out, 4 * index)
                plain_pass(Q_GLU + index - PASS_GLU, 1, take_b if index % 2 else take_a)
            step.join()
            for p in range(2):
                def take_proj(j, p=p):
                    t = 8 * p + 2 * j
                    gate = gates_a[:, t:t + 2, :] if t < 2 * GA else gates_b[:, t - 2 * GA:t - 2 * GA + 2, :]
                    yy = ybuf[p][:, 2 * j:2 * j + 2, :]
                    tt(scr[:, 0:2, 0:SEQ], ps[:, 2 * j:2 * j + 2, 0:SEQ], gate, MUL).then_inc(pair_out, 1)
                    dve.wait_ge(pair_out, 4 * (PASS_PROJ + p) + j + 1)
                    tt(yy, yy, scr[:, 0:2, 0:SEQ], ADD).then_inc(merged, 1)
                    dve.wait_ge(merged, 4 * p + j + 1)
                    dve.wait_ge(mhi_ready, 4 * p + j + 1)
                    tt(x_lo[:, t:t + 2, META:T], yy, x_hi[:, t:t + 2, META:T].bitcast(f32), SUB).then_inc(m_ready, 1)
                plain_pass(Q_PROJ + 3 * p, 3, take_proj)
            for p in range(2):
                def take_out(j, p=p):
                    t = 8 * p + 2 * j
                    tt(h[:, t:t + 2, META:T], ps[:, 2 * j:2 * j + 2, 0:SEQ], h[:, t:t + 2, META:T], ADD).then_inc(pair_out, 1)

                def add(j, p=p):
                    if 4 * p + j >= 2:
                        add_squares(2, META, 4 * p + j - 1)
                plain_pass(Q_OUT + 4 * p, 4, take_out, add)
            norm(2, META)
            ffn(1, META, Q_FFN2)
            norm(3, META)

        @block.gpsimd
        def _(pool):
            step = Tally(pool, pool_step)
            tt, ts = pool.tensor_tensor, pool.tensor_scalar

            def chain(ins):
                step(ins)
                step.join()
            pool.memset(cd[:, :, :, :], 0.0).then_inc(consts, 1)
            pool.memset(ones[:, :], 1.0 / D)
            for c, value in enumerate((1.0 / DK, EPS, -0.5)):
                pool.memset(small[:, c:c + 1], value)
            pool.memset(bd[:, :, :, :], 0.0)
            chain(pool.memset(ident[:, :], 0.0))
            pool.affine_select(out=ident[:, :], in_=ident[:, :], compare_op=ALU.not_equal, fill=1.0, base=0,
                               pattern=[[-1, P]], channel_multiplier=1).then_inc(consts, 1)
            v = [sv[:, i, :] for i in range(14)]
            lr, li = v[0], v[1]
            pool.wait_ge(sv_act, 1)
            tt(v[4], lr, v[3], MUL).then_inc(sv_pool, 1)
            chain(tt(v[5], li, v[3], MUL))
            chain(ts(v[6], v[5], INV_TWO_PI, None, MUL))
            chain(ts(v[6], v[6], ROUNDER, None, ADD))
            chain(ts(v[6], v[6], -ROUNDER, None, ADD))
            for part in TWO_PI_PARTS:
                chain(ts(v[7], v[6], part, None, MUL))
                chain(tt(v[5], v[5], v[7], SUB))
            chain(ts(v[8], v[5], 0.5, None, MUL))
            ts(v[9], v[5], 0.25, None, MUL).then_inc(sv_pool, 1)
            chain(tt(v[12], lr, lr, MUL))
            chain(tt(v[7], li, li, MUL))
            tt(v[12], v[12], v[7], ADD).then_inc(sv_pool, 1)
            pool.wait_ge(sv_act, 3)
            sn, sq, c, s, n = v[10], v[11], v[8], v[7], v[9]
            chain(tt(v[6], sq, sq, MUL))
            chain(ts(v[6], v[6], -2.0, 1.0, MUL, ADD))
            chain(tt(s, sn, v[6], MUL))
            chain(ts(s, s, 2.0, None, MUL))
            chain(tt(c, sn, sn, MUL))
            chain(ts(c, c, -2.0, 1.0, MUL, ADD))
            chain(tt(n, c, c, MUL))
            chain(tt(v[5], s, s, MUL))
            chain(tt(n, n, v[5], ADD))
            chain(ts(n, n, -0.5, 1.5, MUL, ADD))
            chain(tt(s, s, n, MUL))
            chain(tt(c, c, n, MUL))
            a_re, a_im = v[10], v[11]
            chain(tt(a_re, mag[:, :], c, MUL))
            chain(tt(a_im, mag[:, :], s, MUL))
            chain(ts(a_re, a_re, -1.0, None, ADD))
            pool.wait_ge(den_inv, 1)
            c_re, c_im = v[3], v[4]
            chain(tt(c_re, a_re, lr, MUL))
            chain(tt(c_im, a_im, li, MUL))
            chain(tt(c_re, c_re, c_im, ADD))
            chain(tt(c_re, c_re, v[13], MUL))
            chain(tt(c_im, a_im, lr, MUL))
            chain(tt(v[5], a_re, li, MUL))
            chain(tt(c_im, c_im, v[5], SUB))
            chain(tt(c_im, c_im, v[13], MUL))
            pool.wait_ge(small_in[5], 16)
            b = btmp[:, 0:2 * ST * GP].rearrange("p (r j c) -> p r j c", r=2, j=ST)
            for g in range(2):
                rows = slice(64 * g, 64 * g + 64)

                def coef(x):
                    return x[rows, :].unsqueeze(2).broadcast_to([64, ST, GP])
                for r, (other, op) in enumerate(((1, SUB), (0, ADD))):
                    out = bd[rows, r, :, g * GP:(g + 1) * GP]
                    chain(tt(out, b[rows, r, :, :], coef(c_re), MUL))
                    chain(tt(bprod[rows, :, :], b[rows, other, :, :], coef(c_im), MUL))
                    chain(tt(out, out, bprod[rows, :, :], op))
            pool.sem_inc(bbar_ready, 1)
            for g in range(2):
                pool.wait_ge(small_in[6 + g], 16)
            chain(ts(cd[:, :, 1, :], cd[:, :, 1, :], -1.0, None, MUL))
            pool.memset(e_re[:, :, 0:1], 1.0)
            chain(pool.memset(e_im[:, :, 0:1], 0.0))
            p_re, p_im, n_re, n_im = c, s, v[9], v[10]
            tmp = btmp[:, :].rearrange("p (j t) -> p j t", j=ST)
            n = 1
            while n < T:
                for t0 in range(0, min(n, T - n), 32):
                    w = min(32, n - t0, T - n - t0)
                    src, dst = slice(t0, t0 + w), slice(n + t0, n + t0 + w)

                    def power(x):
                        return x.unsqueeze(2).broadcast_to([P, ST, w])
                    for out, one, two, op in ((e_re, p_re, p_im, SUB), (e_im, p_im, p_re, ADD)):
                        chain(tt(out[:, :, dst], e_re[:, :, src], power(one), MUL))
                        chain(tt(tmp[:, :, 0:w], e_im[:, :, src], power(two), MUL))
                        chain(tt(out[:, :, dst], out[:, :, dst], tmp[:, :, 0:w], op))
                chain(tt(n_re, p_re, p_re, MUL))
                chain(tt(v[5], p_im, p_im, MUL))
                chain(tt(n_re, n_re, v[5], SUB))
                chain(tt(n_im, p_re, p_im, MUL))
                chain(ts(n_im, n_im, 2.0, None, MUL))
                p_re, p_im, n_re, n_im = n_re, n_im, p_re, p_im
                n *= 2
            pool.sem_inc(tables, 1)
            pool.wait_ge(ys_done, UT + 1)
            chain(pool.memset(mask[:, :, :], 0.0))
            chain(pool.affine_select(out=mask[:, 0, :], in_=mask[:, 0, :], compare_op=ALU.not_equal, fill=1.0, base=0,
                                     pattern=[[-1, P]], channel_multiplier=1))
            for l in range(1, LEVELS):
                m = 1 << (l - 1)
                right = mask[:, l, :].rearrange("p (b s m) -> p b s m", s=2, m=m)[:, :, 1, :]
                nb = P // (2 * m)
                chain(pool.memset(right, 1.0))
                chain(pool.affine_select(out=right, in_=right, compare_op=ALU.is_ge, fill=0.0, base=0,
                                         pattern=[[-2 * m, nb], [0, m]], channel_multiplier=1))
                chain(pool.affine_select(out=right, in_=right, compare_op=ALU.is_ge, fill=0.0, base=m - 1,
                                         pattern=[[2 * m, nb], [0, m]], channel_multiplier=-1))
            pool.sem_inc(mask_ready, 1)
            with pool.Fori(0, HEADS) as hd:
                step.turn(hd, 2)
                pool.wait_ge(ss_ready, hd + 1)
                chain(tt(ss[:, 1, :], ss[:, 0, :], small[:, 0:1].broadcast_to([P, 2]), MUL))
                chain(tt(ss[:, 1, :], ss[:, 1, :], small[:, 1:2].broadcast_to([P, 2]), ADD))
                tt(ss[:, 1, :], ss[:, 1, :], small[:, 2:3].broadcast_to([P, 2]), ALU.pow).then_inc(rr_ready, 1)
            step.done(HEADS)


def kernel(x, meta_tokens, norm_ffn1, ffn1_w_gate, ffn1_w_up, ffn1_w_down, norm_mix, w_in, hg_lower_bounds, hg_norm,
           hg_w_proj, s5_lam_re, s5_lam_im, s5_log_step, s5_b_re, s5_b_im, s5_c_re, s5_c_im, s5_d, s5_w_glu_a,
           s5_w_glu_b, w_out, norm_ffn2, ffn2_w_gate, ffn2_w_up, ffn2_w_down, norm_final):
    import numpy as np
    import concourse.bacc as bacc
    from concourse.bass_utils import run_bass_kernel_spmd

    nc = bacc.Bacc("TRN2", target_bir_lowering=False, num_devices=1)
    arrays = {}

    def tensor(name, a):
        a = np.ascontiguousarray(a)
        arrays[name] = a
        return nc.dram_tensor(name, a.shape, mybir.dt.from_np(a.dtype), kind="ExternalInput").ap()

    def tiles(a, n):
        return np.asarray(a).reshape(n, P).T

    args = [
        tensor("xT", np.asarray(x)[0].T),
        tensor("metaT", np.asarray(meta_tokens).T),
        tensor("gains", np.stack([tiles(g, DT) for g in (norm_ffn1, norm_mix, norm_ffn2, norm_final)], 1)),
        [tensor(n, np.asarray(w)[0]) for n, w in (("gate1", ffn1_w_gate), ("up1", ffn1_w_up), ("down1", ffn1_w_down))],
        tensor("w_in", np.asarray(w_in)[0]),
        tensor("hg_lb", np.stack([tiles(r, HEADS) for r in np.asarray(hg_lower_bounds)], 1)),
        tensor("hg_norm", tiles(hg_norm, HEADS)),
        tensor("w_proj", np.asarray(hg_w_proj)[0]),
        tensor("s5v", np.stack([tiles(v, ST) for v in (s5_lam_re, s5_lam_im, np.repeat(np.asarray(s5_log_step)[0], STATE))], 1)),
        tensor("s5b", np.stack([np.asarray(b).reshape(ST, P, GP).transpose(1, 0, 2) for b in (s5_b_re, s5_b_im)], 1)),
        tensor("s5c", np.stack([np.asarray(c)[0].transpose(0, 2, 1).reshape(ST, P, GP).transpose(1, 0, 2)
                                for c in (s5_c_re, s5_c_im)], 2)),
        tensor("s5d", tiles(s5_d, UT)),
        [tensor(n, np.asarray(w)[0]) for n, w in (("glu_a", s5_w_glu_a), ("glu_b", s5_w_glu_b))],
        tensor("w_out", np.asarray(w_out)[0]),
        [tensor(n, np.asarray(w)[0]) for n, w in (("gate2", ffn2_w_gate), ("up2", ffn2_w_up), ("down2", ffn2_w_down))],
        nc.dram_tensor("outT", (D, SEQ), mybir.dt.float32, kind="ExternalOutput").ap(),
    ]
    program(nc, *args)
    r = run_bass_kernel_spmd(nc, [arrays], core_ids=[0])
    return r.results[0]["outT"].T[None]
```

```python
import concourse.bass as bass
from concourse import mybir
from contextlib import ExitStack

P = 128
D = 2048
DT = D // P
META, SEQ = 16, 256
T = META + SEQ
FF = 5632
HEADS, DK = 12, 128
HG = HEADS * DK
GROUPS, GP, STATE = 32, 16, 64
S5W = GROUPS * GP
UT = S5W // P
ST = GROUPS * STATE // P
SPU = ST // UT
EPS = 1e-6
LEVELS = 8

KT, NC = 4, 256
RING = 4
LEAD = 3
FF_BLOCKS = FF // NC
HALVES = (12, 10)
HT = HALVES[0] * 2
HG_BLOCKS = HG // NC
U_BLOCK = 4 * HG_BLOCKS
GATE_BLOCK = U_BLOCK + S5W // NC
GATES = 2 * D // NC
GA = HEADS - HG_BLOCKS
GB = GATES - GA

FFN_QUADS = 2 * FF_BLOCKS + 2 * (FF // (KT * P))
Q_U = FFN_QUADS
Q_SCAN = Q_U + S5W // NC
Q_REST = Q_SCAN + ST
Q_HEADS = Q_REST + 3 * HG_BLOCKS - ST
Q_GATES = Q_HEADS + HEADS
Q_GLU = Q_GATES + GB
Q_PROJ = Q_GLU + 4 * (S5W // (KT * P))
Q_OUT = Q_PROJ + 2 * (HG // (KT * P))
Q_FFN2 = Q_OUT + 2 * (D // (KT * P))
UNITS = 4 * (Q_FFN2 + FFN_QUADS)
PASS_GLU, PASS_PROJ, PASS_OUT, PASS_FFN2 = 4, 8, 10, 12
PASSES_BEFORE = (0, PASS_GLU, PASS_FFN2, 16)
NORM_BANK = (7, 0, 7, 0)
M_HEADS = 20
M_GATES = M_HEADS + HEADS

PI = 3.14159265358979
TWO_PI_PARTS = (6.28125, 0.0019340515136718750, 1.2556659146e-06)
INV_TWO_PI = 0.15915494309189535
ROUNDER = 12582912.0
GELU_A, GELU_B = 0.044715, 1.5957691216057308


class Tally:

    def __init__(self, engine, sem):
        self.engine, self.sem, self.base, self.n = engine, sem, 0, 0

    def __call__(self, ins):
        ins.then_inc(self.sem, 1)
        self.n += 1

    def join(self):
        self.engine.wait_ge(self.sem, self.base + self.n)

    def turn(self, i, per):
        self.start, self.per = self.n + (self.base if isinstance(self.base, int) else 0), per
        self.base, self.n = i * per + self.start, 0

    def done(self, times):
        assert self.n == self.per, (self.n, self.per)
        self.base, self.n = self.start + times * self.per, 0


def program(nc, xT, metaT, gains, ffn1, w_in, hg_lb, hg_norm, w_proj, s5v, s5b, s5c, s5d, w_glu, w_out, ffn2, outT):
    f32, f32r, i32 = mybir.dt.float32, mybir.dt.float32r, mybir.dt.int32
    bf16 = mybir.dt.bfloat16
    ALU, ACT, AX = mybir.AluOpType, mybir.ActivationFunctionType, mybir.AxisListType
    MUL, ADD, SUB = ALU.mult, ALU.add, ALU.subtract
    ds = bass.ds

    top = ExitStack()
    with top:
        def sem(name):
            return top.enter_context(nc.semaphore(name))

        def sb(name, shape, dt=f32):
            return top.enter_context(nc.sbuf_tensor(name, shape, dt))

        raw = sb("raw", [P, RING, KT, NC])
        w_hi = sb("w_hi", [P, RING, KT, NC], f32r)
        w_lo = sb("w_lo", [P, RING, KT, NC], f32r)
        h = sb("h", [P, DT, T])
        x_hi = sb("x_hi", [P, DT, T], f32r)
        x_lo = sb("x_lo", [P, DT, T], f32r)
        gain = sb("gain", [P, 4, DT])
        ones = sb("ones", [P, P])
        ident = sb("ident", [P, P])
        scr = sb("scr", [P, 6, T])
        lb = sb("lb", [P, 2, HEADS])
        hgn = sb("hgn", [P, HEADS])
        dsk = sb("dsk", [P, UT])
        mag = sb("mag", [P, ST])
        ss = sb("ss", [P, 2, 2])
        small = sb("small", [P, 3])
        ps = top.enter_context(nc.psum_tensor("ps", [P, 8, 512], f32))

        def at(offset, name, shape, dt=f32):
            with ExitStack() as c:
                if offset:
                    c.enter_context(nc.sbuf_tensor("below_" + name, [P, offset], f32))
                return c.enter_context(nc.sbuf_tensor(name, shape, dt))

        TAB = 2 * HT * T + 2016
        h_hi = at(0, "h_hi", [P, HT, T], f32r)
        h_lo = at(HT * T, "h_lo", [P, HT, T], f32r)
        sv = at(2 * HT * T, "sv", [P, 14, ST])
        lbt = at(2 * HT * T + 1760, "lbt", [P, 3, HEADS])
        bd = at(2 * HT * T + 224, "bd", [P, 2, ST, 2 * GP])
        btmp = at(2 * HT * T + 1248, "btmp", [P, ST * 32])
        bprod = at(2 * HT * T + 1760, "bprod", [P, ST, GP])
        e_re = at(TAB, "e_re", [P, ST, T])
        e_im = at(TAB + ST * T, "e_im", [P, ST, T])
        bt = at(TAB + 2 * ST * T, "bt", [P, UT, 2, P])
        cd = at(TAB + 2 * ST * T + 1024, "cd", [P, ST, 2, 2 * GP])
        QFV = 3 * HEADS * T
        qfv = at(0, "qfv", [P, 3 * HEADS, T])
        ys = at(QFV, "ys", [P, UT, SEQ])
        U5 = QFV + UT * SEQ
        u5 = at(U5, "u5", [P, UT, T])
        st_u = at(U5 + UT * T, "st_u", [P, T])
        st_b = at(U5 + UT * T + T, "st_b", [P, 2, P])
        st_c = at(U5 + UT * T + T + 256, "st_c", [P, SPU, 2, 2 * GP])
        sx = at(U5 + UT * T + T + 512, "sx", [P, 2, T])
        assert U5 + UT * T + T + 512 + 2 * T <= TAB
        gates_a = at(QFV, "gates_a", [P, 2 * GA, SEQ])
        z_hi = at(QFV + 3072, "z_hi", [P, UT, SEQ], f32r)
        z_lo = at(QFV + 4096, "z_lo", [P, UT, SEQ], f32r)
        gout = at(QFV + 5120, "gout", [P, HEADS, SEQ])
        HD = QFV + 5120 + 3072
        qs = at(HD, "qs", [P, LEVELS + 1, SEQ])
        ks = at(HD + 2304, "ks", [P, LEVELS, T])
        fm = at(HD + 2304 + 2176, "fm", [P, 560])
        mask = at(HD + 5040, "mask", [P, LEVELS, P], bf16)
        prod = at(HD + 5552, "prod", [P, LEVELS, P])
        att = at(HD + 6576, "att", [P, 3, P])
        att_m = at(HD + 6960, "att_m", [META, 2, P])
        v_tok = at(HD + 7216, "v_tok", [P, 2, P])
        v_meta = at(HD + 7472, "v_meta", [META, P])
        o_hi = at(HEADS * T, "o_hi", [P, HEADS, SEQ], f32r)
        o_lo = at(HEADS * T + 3072, "o_lo", [P, HEADS, SEQ], f32r)
        gates_b = at(HD, "gates_b", [P, 2 * GB, SEQ])
        sgs = at(HD + 5120, "sgs", [P, 3, SEQ])
        y_a = at(QFV + 5120, "y_a", [P, 8, SEQ])
        y_b = at(HD + 5120, "y_b", [P, 8, SEQ])
        ybuf = (y_a, y_b)

        raw_ready = [sem(f"raw_ready{j}") for j in range(RING)]
        hi_ready = sem("hi_ready")
        lo_ready = sem("lo_ready")
        unit_done = sem("unit_done")
        x_in = [sem(f"x_in{c}") for c in range(4)]
        meta_in = sem("meta_in")
        small_in = [sem(f"small_in{c}") for c in range(9)]
        consts = sem("consts")
        dve_step = sem("dve_step")
        pool_step = sem("pool_step")
        act_step = sem("act_step")
        sq_ready = sem("sq_ready")
        sq_used = sem("sq_used")
        summed = sem("summed")
        lb_exp = sem("lb_exp")
        root_ready = sem("root_ready")
        rms_inv = sem("rms_inv")
        xf_ready = sem("xf_ready")
        xhi_ready = sem("xhi_ready")
        x_ready = sem("x_ready")
        sig_ready = sem("sig_ready")
        gated = sem("gated")
        silu = sem("silu")
        hidden = sem("hidden")
        hhi_ready = sem("hhi_ready")
        h_ready = sem("h_ready")
        pair_out = sem("pair_out")
        block_out = sem("block_out")
        sv_act = sem("sv_act")
        sv_pool = sem("sv_pool")
        den_inv = sem("den_inv")
        bbar_ready = sem("bbar_ready")
        bt_psum = sem("bt_psum")
        bt_out = sem("bt_out")
        tables = sem("tables")
        staged = sem("staged")
        bu_done = sem("bu_done")
        bu_taken = sem("bu_taken")
        scanned = sem("scanned")
        cx_done = sem("cx_done")
        ys_done = sem("ys_done")
        z_arg = sem("z_arg")
        z_sig = sem("z_sig")
        z_val = sem("z_val")
        zhi_ready = sem("zhi_ready")
        z_ready = sem("z_ready")
        head_sig = sem("head_sig")
        v_staged = sem("v_staged")
        levels = sem("levels")
        mask_ready = sem("mask_ready")
        scored = sem("scored")
        v_ready = sem("v_ready")
        att_ready = sem("att_ready")
        o_done = sem("o_done")
        ss_ready = sem("ss_ready")
        rr_ready = sem("rr_ready")
        on_ready = sem("on_ready")
        ot_psum = sem("ot_psum")
        ot_done = sem("ot_done")
        sgo_ready = sem("sgo_ready")
        og_ready = sem("og_ready")
        ohi_ready = sem("ohi_ready")
        o_ready = sem("o_ready")
        glu_sig = sem("glu_sig")
        merged = sem("merged")
        mhi_ready = sem("mhi_ready")
        m_ready = sem("m_ready")
        y_final = sem("y_final")
        stored = [sem(f"stored{c}") for c in range(4)]

        block = top.enter_context(nc.Block())

        @block.sync
        def _(sp):
            def load(j, w, group, col, u):
                sp.wait_ge(lo_ready, u + 1)
                sp.dma_start(raw[:, j, :, :],
                             w.rearrange("(g t p) n -> p g t n", t=KT, p=P)[:, ds(group, 1), :, ds(col, NC)]
                             .rearrange("p g t n -> p (g t) n")).then_inc(raw_ready[j], 16)

            def column_block(w, col, q, before=None):
                for j in range(4):
                    if before:
                        before(j)
                    load(j, w, j, col, 4 * q + j)

            def passes(w, first_group, groups, q):
                for p in range(2):
                    with sp.Fori(0, groups) as g:
                        for j in range(4):
                            load(j, w, g + first_group, (4 * p + j) * NC, (g + q) * 4 + j)
                    q += groups
                return q

            def load_x(c):
                sp.dma_start(h[:, 4 * c:4 * c + 4, META:T],
                             xT.rearrange("(k p) t -> p k t", p=P)[:, 4 * c:4 * c + 4, :]).then_inc(x_in[c], 16)

            def ffn(w_gate, w_up, w_down, q):
                first = 0
                for blocks in HALVES:
                    peeled = 1 if q == 0 else 0
                    if peeled:
                        column_block(w_gate, 0, 0, load_x)
                        column_block(w_up, 0, 1)
                    with sp.Fori(peeled, blocks) as b:
                        column_block(w_gate, (b + first) * NC, b * 2 + q)
                        column_block(w_up, (b + first) * NC, b * 2 + q + 1)
                    q += 2 * blocks
                    q = passes(w_down, first // 2, blocks // 2, q)
                    first += blocks

            def columns(first, n, q):
                with sp.Fori(0, n) as b:
                    column_block(w_in, (b + first) * NC, b + q)

            ffn(*ffn1, 0)
            columns(U_BLOCK, 2, Q_U)
            columns(0, U_BLOCK, Q_SCAN)
            columns(GATE_BLOCK, GATES, Q_HEADS + HG_BLOCKS)
            for p in range(2):
                for s in range(2):
                    for j in range(4):
                        load(j, w_glu[s], 0, (4 * p + j) * NC, 4 * (Q_GLU + 2 * p + s) + j)
            passes(w_proj, 0, HG // (KT * P), Q_PROJ)
            passes(w_out, 0, D // (KT * P), Q_OUT)
            ffn(*ffn2, Q_FFN2)
            for c in range(4):
                sp.wait_ge(y_final, 4 * c + 4)
                sp.dma_start(outT.rearrange("(k p) t -> p k t", p=P)[:, 4 * c:4 * c + 4, :],
                             h[:, 4 * c:4 * c + 4, META:T]).then_inc(stored[c], 16)
            for c in range(4):
                sp.wait_ge(stored[c], 16)

        @block.tensor
        def _(pe):
            pe.sem_inc(unit_done, RING)
            pe.sem_inc(cx_done, 1)

            def unit(j, u, banks, n, rhs, start, stop):
                pe.wait_ge(lo_ready, u + RING + 1)
                for c in range(2):
                    out = ps[:, banks + c, 0:n]
                    for k in range(KT):
                        hi, lo = w_hi[:, j, k, c * P:(c + 1) * P], w_lo[:, j, k, c * P:(c + 1) * P]
                        x_h, x_l = rhs(k)
                        pe.matmul(out, hi, x_h, start=start and k == 0, stop=False)
                        pe.matmul(out, hi, x_l, start=False, stop=False)
                        last = pe.matmul(out, lo, x_h, start=False, stop=stop and k == KT - 1)
                last.then_inc(unit_done, 1)

            def rows(hi, lo, first, c0, n):
                return lambda k: (hi[:, first + k, c0:c0 + n], lo[:, first + k, c0:c0 + n])

            def column_block(q, banks, c0, x_need, between=None):
                for j in range(4):
                    pe.wait_ge(x_ready, x_need + 4 * j + 4)
                    unit(j, 4 * q + j, banks, T - c0, rows(x_hi, x_lo, 4 * j, c0, T - c0), j == 0, j == 3)
                    if between:
                        between(j)

            def one_pass(index, q, groups, hi, lo, c0, n, need):
                def quad(g, start, stop):
                    need(g)
                    for j in range(4):
                        if start and index:
                            pe.wait_ge(pair_out, 4 * (index - 1) + j + 1)
                        def rhs(k):
                            if isinstance(g, int):
                                return hi[:, 4 * g + k, c0:c0 + n], lo[:, 4 * g + k, c0:c0 + n]
                            return (hi[:, ds(g * 4 + k, 1), c0:c0 + n].rearrange("p a t -> p (a t)"),
                                    lo[:, ds(g * 4 + k, 1), c0:c0 + n].rearrange("p a t -> p (a t)"))
                        unit(j, (g + q) * 4 + j, 2 * j, n, rhs, start, stop)
                quad(0, True, groups == 1)
                if groups > 2:
                    with pe.Fori(1, groups - 1) as g:
                        quad(g, False, False)
                if groups > 1:
                    quad(groups - 1, False, True)

            def norm(index, c0):
                if index:
                    pe.wait_ge(pair_out, 4 * PASSES_BEFORE[index] + (0 if NORM_BANK[index] else -3))
                pe.wait_ge(summed, 6 * index + 6)
                for c in range(2):
                    pe.matmul(ps[:, NORM_BANK[index], 0:T - c0], ones[:, :], scr[:, 4 + c, c0:T], start=c == 0, stop=False)
                pe.wait_ge(sq_ready, 8 * index + 8)
                for c in range(2):
                    last = pe.matmul(ps[:, NORM_BANK[index], 0:T - c0], ones[:, :], scr[:, 2 + c, c0:T], start=False,
                                     stop=c == 1)
                last.then_inc(sq_used, 1)

            def ffn(f, c0, q):
                first, index = 0, f * PASS_FFN2
                for blocks in HALVES:
                    done = f * FF_BLOCKS + first
                    if index:
                        pe.wait_ge(pair_out, 4 * index - 2)

                    def block(b, mean=False):
                        pe.wait_ge(gated, b + done + 1)
                        column_block(b * 2 + q, 0, c0, f * 2 * DT)
                        if mean:
                            norm(2 * f, c0)
                        pe.wait_ge(hidden, b + done + 1)
                        column_block(b * 2 + q + 1, 2, c0, f * 2 * DT)
                    peeled = 0 if first else 1
                    if peeled:
                        block(0, True)
                    with pe.Fori(peeled, blocks) as b:
                        block(b)
                    q += 2 * blocks
                    for p in range(2):
                        if p == 0:
                            pe.wait_ge(gated, 1 + done + blocks)
                            pe.wait_ge(hidden, 1 + done + blocks)
                        one_pass(index, q, blocks // 2, h_hi, h_lo, c0, T - c0,
                                 lambda g: pe.wait_ge(h_ready, g * 2 + done + 2))
                        q += blocks // 2
                        index += 1
                    first += blocks

            pe.wait_ge(consts, 2)
            ffn(0, 0, 0)
            norm(1, 0)
            pe.wait_ge(pair_out, 4 * PASS_GLU)
            pe.wait_ge(bbar_ready, 1)
            for ut in range(UT):
                for r in range(2):
                    last = pe.transpose(ps[:, 4 + r, ut * P:(ut + 1) * P],
                                        bd[:, r, SPU * ut:SPU * (ut + 1), :].rearrange("p a b -> p (a b)"), ident[:, :])
            last.then_inc(bt_psum, 1)
            pe.wait_ge(root_ready, 2)
            for m in range(2):
                column_block(Q_U + m, 2 * m, 0, DT)
            pe.wait_ge(block_out, 2)
            with pe.Fori(0, UT) as ut:
                def project_in(jj, turn):
                    for r in range(2):
                        last = pe.matmul(ps[:, 4 + r, 0:T], st_b[32 * jj:32 * jj + 32, r, :], st_u[32 * jj:32 * jj + 32, :],
                                         start=True, stop=True)
                    last.then_inc(bu_done, 1)
                pe.wait_ge(staged, ut + 1)
                pe.wait_ge(bu_taken, ut * SPU + 1)
                project_in(0, ut)
                for jj in range(SPU):
                    pe.wait_ge(block_out, ut * SPU + jj + 1)

                    def between(j, jj=jj):
                        if j == 2 and jj < SPU - 1:
                            pe.wait_ge(bu_taken, ut * SPU + jj + 2)
                            project_in(jj + 1, ut)
                    column_block(ut * SPU + Q_SCAN + jj, 2 * (jj % 2), 0, DT, between)
                    pe.wait_ge(scanned, ut * SPU + jj + 1)
                    if jj == 0:
                        pe.wait_ge(ys_done, ut + 1)
                    for r in range(2):
                        last = pe.matmul(ps[32 * jj:32 * jj + 32, 6, 0:SEQ], st_c[:, jj, r, :], sx[:, r, META:T],
                                         start=r == 0, stop=r == 1)
                    last.then_inc(cx_done, 1)
            for m in (18, 19):
                pe.wait_ge(block_out, m - 1)
                column_block(Q_U + m, 2 * (m % 2), 0, DT)
            pe.wait_ge(block_out, M_HEADS)
            pe.wait_ge(ys_done, UT + 1)

            def score(hd):
                pe.wait_ge(levels, hd + 1)
                pe.wait_ge(v_staged, hd + 1)
                for b in range(2):
                    pe.transpose(ps[:, 2, b * P:(b + 1) * P], scr[:, 2, META + b * P:META + (b + 1) * P], ident[:, :])
                pe.transpose(ps[0:META, 2, 2 * P:3 * P], scr[:, 2, 0:META], ident[:, :])
                blk = [slice(META + b * P, META + (b + 1) * P) for b in range(2)]
                pe.matmul(ps[:, 3, 0:P], ks[:, 7, blk[0]], qs[:, 8, P:2 * P], start=True, stop=True)
                pe.matmul(ps[0:META, 3, P:2 * P], ks[:, 4, 0:META], qs[:, 8, 0:P], start=True, stop=True)
                pe.matmul(ps[0:META, 3, 2 * P:3 * P], ks[:, 5, 0:META], qs[:, 8, P:2 * P], start=True, stop=True)
                for b in range(2):
                    for l in range(LEVELS):
                        if b and l == 4:
                            pe.wait_ge(ot_done, hd + 1)
                        k = max(l - 1, 0)
                        out = ps[:, 4 + 2 * b + l // 4, (l % 4) * P:(l % 4 + 1) * P]
                        queries = qs[:, l, b * P:(b + 1) * P]
                        if l:
                            out, queries = [a.rearrange("p (b s m) -> p b s m", s=2, m=1 << (l - 1))[:, :, 1, :]
                                            for a in (out, queries)]
                        last = pe.matmul(out, ks[:, k, blk[b]], queries, start=True, stop=True)
                last.then_inc(scored, 1)

            def mix(hd):
                pe.wait_ge(att_ready, hd + 1)
                pe.wait_ge(v_ready, hd + 1)
                pe.matmul(ps[:, 2, 0:P], att[:, 0, :], v_tok[:, 0, :], start=True, stop=False)
                pe.matmul(ps[:, 2, 0:P], att_m[0:META, 0, :], v_meta[0:META, :], start=False, stop=True)
                pe.matmul(ps[:, 2, P:2 * P], att[:, 1, :], v_tok[:, 1, :], start=True, stop=False)
                pe.matmul(ps[:, 2, P:2 * P], att[:, 2, :], v_tok[:, 0, :], start=False, stop=False)
                pe.matmul(ps[:, 2, P:2 * P], att_m[0:META, 1, :], v_meta[0:META, :], start=False, stop=True)\
                    .then_inc(o_done, 1)

            def back(hd):
                pe.wait_ge(on_ready, hd + 1)
                for b in range(2):
                    last = pe.transpose(ps[:, 7, b * P:(b + 1) * P], scr[:, 4, b * P:(b + 1) * P], ident[:, :])
                last.then_inc(ot_psum, 1)

            def head(hd):
                score(hd)
                pe.wait_ge(block_out, hd + M_HEADS)
                column_block(hd + Q_HEADS, 0, META, DT, lambda j: mix(hd) if j == 1 else None)
                back(hd)

            with pe.Fori(0, HEADS) as hd:
                head(hd)
            pe.wait_ge(ot_done, HEADS + 1)
            pe.wait_ge(block_out, M_GATES)
            with pe.Fori(0, GB // 2) as i:
                for c in range(2):
                    pe.wait_ge(block_out, i * 2 + M_GATES + c - 1)
                    column_block(i * 2 + Q_GATES + c, 2 * c, META, DT)
            pe.wait_ge(block_out, M_GATES + GB)
            for index in range(PASS_GLU, PASS_PROJ):
                one_pass(index, Q_GLU + index - PASS_GLU, 1, z_hi, z_lo, 0, SEQ, lambda g: pe.wait_ge(z_ready, 1))
            for p in range(2):
                one_pass(PASS_PROJ + p, Q_PROJ + 3 * p, 3, o_hi, o_lo, 0, SEQ, lambda g: pe.wait_ge(o_ready, 4))
            for p in range(2):
                one_pass(PASS_OUT + p, Q_OUT + 4 * p, 4, x_hi, x_lo, META, SEQ, lambda g: pe.wait_ge(m_ready, g * 2 + 2))
            ffn(1, META, Q_FFN2)
            norm(3, META)

        @block.scalar
        def _(act):
            step = Tally(act, act_step)
            act.sem_inc(ot_done, 1)
            act.dma_start(h[:, :, 0:META], metaT.rearrange("(k p) t -> p k t", p=P)).then_inc(meta_in, 16)
            act.dma_start(gain[:, :, :], gains).then_inc(small_in[0], 16)
            act.dma_start(sv[:, 0:3, :], s5v).then_inc(small_in[1], 16)
            act.dma_start(lb[:, :, :], hg_lb).then_inc(small_in[2], 16)
            act.dma_start(hgn[:, :], hg_norm).then_inc(small_in[3], 16)
            act.dma_start(dsk[:, :], s5d).then_inc(small_in[4], 16)
            act.dma_start(btmp[:, 0:2 * ST * GP].rearrange("p (r j c) -> p r j c", r=2, j=ST), s5b).then_inc(small_in[5], 16)

            def split(q, j):
                slot = (j + LEAD) % 4
                if isinstance(q, int) and 4 * q + j + LEAD >= UNITS:
                    return
                q1 = q + (j + LEAD) // 4
                act.wait_ge(raw_ready[slot], q1 * 16 + 16)
                act.wait_ge(unit_done, q * 4 + j + LEAD + 1)
                act.activation(w_hi[:, slot, :, :], raw[:, slot, :, :], ACT.Copy).then_inc(hi_ready, 1)

            def square(index, c0, k):
                if index:
                    act.wait_ge(pair_out, 4 * (PASSES_BEFORE[index] - 2) + k + 1)
                if k >= 3:
                    act.wait_ge(summed, 6 * index + k - 2)
                at_k = 2 * (k % 2) if k else 4
                act.activation(scr[:, at_k:at_k + 2, c0:T], h[:, 2 * k:2 * k + 2, c0:T], ACT.Square).then_inc(sq_ready, 1)

            def root(index, c0):
                act.wait_ge(sq_used, index + 1)
                act.activation(scr[:, 4, c0:T], ps[:, NORM_BANK[index], 0:T - c0], ACT.Sqrt, bias=small[:, 1:2])\
                    .then_inc(root_ready, 1)

            def upper(index, c0, k):
                act.activation(x_hi[:, k, c0:T], h[:, k, c0:T], ACT.Copy, scale=gain[:, index, k:k + 1])\
                    .then_inc(xhi_ready, 1)

            def plain_pass(q, groups, after=None, beside=None):
                if groups > 1:
                    with act.Fori(0, groups - 1) as g:
                        for j in range(4):
                            split(g + q, j)
                for j in range(4):
                    if j and after:
                        after(j - 1)
                    split(q + groups - 1, j)
                    if beside:
                        beside(j)
                if after:
                    after(3)

            def ffn(f, c0, q, between=None):
                first = 0
                for blocks in HALVES:
                    done = f * FF_BLOCKS + first

                    def block(b, mean=False):
                        for j in range(4):
                            split(b * 2 + q, j)
                        if mean:
                            root(2 * f, c0)
                        split(b * 2 + q + 1, 0)
                        act.wait_ge(gated, b + done + 2)
                        act.activation(scr[:, 2:4, c0:T], scr[:, 0:2, c0:T], ACT.Sigmoid).then_inc(sig_ready, 1)
                        for j in range(1, 4):
                            split(b * 2 + q + 1, j)
                        act.wait_ge(hidden, b + done + 2)
                        act.activation(h_hi[:, ds(b * 2, 2), c0:T], scr[:, 2:4, c0:T], ACT.Copy).then_inc(hhi_ready, 1)
                    peeled = 0 if first else 1
                    if peeled:
                        block(0, True)
                    with act.Fori(peeled, blocks) as b:
                        block(b)
                    q += 2 * blocks
                    if between and not first:
                        between(0)
                    for p in range(2):
                        plain_pass(q, blocks // 2, (lambda j, p=p: square(1 + 2 * f, c0, 4 * p + j)) if first else None)
                        q += blocks // 2
                        if between and not first:
                            between(1 + p)
                    first += blocks

            def head_inputs(hd):
                def tile(t):
                    return qfv[:, ds(hd + t, 1), :].rearrange("p a t -> p (a t)")
                act.activation(scr[:, 0, 0:SEQ], tile(0)[:, META:T], ACT.Sigmoid)
                act.activation(scr[:, 1, :], tile(HEADS), ACT.Sigmoid).then_inc(head_sig, 1)
                act.activation(scr[:, 2, :], tile(2 * HEADS), ACT.Copy).then_inc(v_staged, 1)

            def parameters(stage):
                if stage == 0:
                    act.wait_ge(small_in[1], 16)
                    act.activation(sv[:, 3, :], sv[:, 2, :], ACT.Exp).then_inc(sv_act, 1)
                    act.wait_ge(dve_step, 3)
                    act.activation(lbt[:, 0:2, :], lbt[:, 0:2, :], ACT.Exp).then_inc(lb_exp, 1)
                elif stage == 1:
                    act.wait_ge(sv_pool, 1)
                    act.activation(mag[:, :], sv[:, 4, :], ACT.Exp).then_inc(sv_act, 1)
                else:
                    act.wait_ge(sv_pool, 2)
                    act.activation(sv[:, 10:12, :], sv[:, 8:10, :], ACT.Sin).then_inc(sv_act, 1)

            act.wait_ge(meta_in, 16)
            act.wait_ge(small_in[0], 16)
            act.wait_ge(consts, 2)
            for c in range(4):
                act.wait_ge(x_in[c], 16)
                for k in range(4 * c, 4 * c + 4):
                    upper(0, 0, k)
                if c < LEAD:
                    act.wait_ge(raw_ready[c], 16)
                    act.activation(w_hi[:, c, :, :], raw[:, c, :, :], ACT.Copy).then_inc(hi_ready, 1)
                square(0, 0, 2 * c)
                square(0, 0, 2 * c + 1)
            for g in range(2):
                act.dma_start(cd[64 * g:64 * g + 64, :, :, g * GP:(g + 1) * GP], s5c[64 * g:64 * g + 64])\
                    .then_inc(small_in[6 + g], 16)
            ffn(0, 0, 0, parameters)
            root(1, 0)
            for k in range(DT):
                act.wait_ge(xf_ready, k + 1)
                act.activation(x_hi[:, k, :], scr[:, k % 4, :], ACT.Copy, scale=gain[:, 1, k:k + 1]).then_inc(xhi_ready, 1)
                if k % 4 == 3 and k > 3:
                    split(Q_U, k // 4 - 1)
            act.wait_ge(bt_psum, 1)
            for r in range(2):
                ins = act.activation(bt[:, :, r, :], ps[:, 4 + r, :].rearrange("p (u s) -> p u s", u=UT), ACT.Copy)
            ins.then_inc(bt_out, 1)

            def take_block(m, out, banks, n, func):
                act.wait_ge(unit_done, (m + Q_U) * 4 + RING + 4)
                act.activation(out, ps[:, banks:banks + 2, 0:n], func).then_inc(block_out, 1)

            for m in range(2):
                for j in range(0 if m else 3, 4):
                    split(Q_U + m, j)
                take_block(m, u5[:, 2 * m:2 * m + 2, :], 2 * m, T, ACT.Copy)
            act.wait_ge(tables, 1)
            act.wait_ge(bt_out, 1)
            with act.Fori(0, UT) as ut:
                act.wait_ge(block_out, 2)
                act.wait_ge(cx_done, ut * SPU + 1)
                act.activation(st_u[:, :], u5[:, ds(ut, 1), :].rearrange("p a t -> p (a t)"), ACT.Copy)
                act.activation(st_b[:, :, :], bt[:, ds(ut, 1), :, :].rearrange("p a r s -> p (a r) s"), ACT.Copy)
                act.activation(st_c[:, :, :, :], cd[:, ds(ut * SPU, SPU), :, :], ACT.Copy).then_inc(staged, 1)
                for jj in range(SPU):
                    for j in range(4):
                        split(ut * SPU + Q_SCAN + jj, j)
                    take_block(ut * SPU + 2 + jj, qfv[:, ds((ut * SPU + jj) * 2, 2), :], 2 * (jj % 2), T, ACT.Copy)
            for m in (18, 19):
                for j in range(4):
                    split(Q_U + m, j)
                    if m == 18 and j == 1:
                        act.wait_ge(z_arg, 1)
                        act.activation(scr[:, 0:4, 0:SEQ], scr[:, 0:4, 0:SEQ], ACT.Sigmoid, scale=GELU_B).then_inc(z_sig, 1)
                    if m == 18 and j == 3:
                        act.wait_ge(z_val, 1)
                        act.activation(z_hi[:, :, :], ys[:, :, :], ACT.Copy).then_inc(zhi_ready, 1)
                    if m == 19 and j == 0:
                        act.wait_ge(z_ready, 1)
                        head_inputs(0)
                take_block(m, qfv[:, 2 * m - 4:2 * m - 2, :], 2 * (m % 2), T, ACT.Copy)

            def beside_head(hd, out, func, following):
                act.wait_ge(scored, hd + 1)
                act.activation(v_tok[:, :, :], ps[:, 2, 0:2 * P].rearrange("p (b v) -> p b v", b=2), ACT.Copy)
                act.activation(v_meta[:, :], ps[0:META, 2, 2 * P:3 * P], ACT.Copy)
                act.activation(att[:, 2, :], ps[:, 3, 0:P], ACT.Copy)
                act.activation(att_m[:, :, :], ps[0:META, 3, P:3 * P].rearrange("p (b v) -> p b v", b=2), ACT.Copy)\
                    .then_inc(v_ready, 1)
                if following:
                    act.wait_ge(levels, hd + 1)
                    head_inputs(hd + 1)
                split(hd + Q_HEADS, 1)
                act.wait_ge(o_done, hd + 1)
                for b in range(2):
                    ins = act.activation(scr[:, 3, b * P:(b + 1) * P], ps[:, 2, b * P:(b + 1) * P], ACT.Square,
                                         accum_out=ss[:, 0, b:b + 1])
                ins.then_inc(ss_ready, 1)
                split(hd + Q_HEADS, 2)
                act.wait_ge(rr_ready, hd + 1)
                for b in range(2):
                    ins = act.activation(scr[:, 4, b * P:(b + 1) * P], ps[:, 2, b * P:(b + 1) * P], ACT.Copy,
                                         scale=ss[:, 1, b:b + 1])
                ins.then_inc(on_ready, 1)
                split(hd + Q_HEADS, 3)
                take_block(hd + M_HEADS, out, 0, SEQ, func)
                act.wait_ge(ot_psum, hd + 1)
                act.activation(qfv[:, ds(hd, 1), META:T].rearrange("p a t -> p (a t)"), ps[:, 7, 0:SEQ], ACT.Copy,
                               scale=hgn[:, ds(hd, 1)]).then_inc(ot_done, 1)
                if following:
                    split(hd + Q_HEADS + 1, 0)

            split(Q_HEADS, 0)
            act.wait_ge(small_in[3], 16)
            with act.Fori(0, HG_BLOCKS) as hd:
                beside_head(hd, gout[:, ds(hd * 2, 2), :], ACT.Copy, True)
            with act.Fori(HG_BLOCKS, HEADS - 1) as hd:
                beside_head(hd, gates_a[:, ds(hd * 2 - HEADS, 2), :], ACT.Sigmoid, True)
            beside_head(HEADS - 1, gates_a[:, HEADS - 2:HEADS, :], ACT.Sigmoid, False)

            def gate_pair(i, c, side=None):
                for j in range(4):
                    split(i * 2 + Q_GATES + c, j)
                    if side:
                        side(j)
                take_block(i * 2 + M_GATES + c, gates_b[:, ds(i * 4 + 2 * c, 2), :], 2 * c, SEQ, ACT.Sigmoid)

            act.wait_ge(ot_done, HEADS + 1)
            with act.Fori(0, 4) as i:
                def side(j):
                    if j == 0:
                        act.activation(sgs[:, :, :], gout[:, ds(i * 3, 3), :], ACT.Sigmoid).then_inc(sgo_ready, 1)
                    if j == 3:
                        act.wait_ge(og_ready, i + 1)
                        act.activation(o_hi[:, ds(i * 3, 3), :], gout[:, ds(i * 3, 3), :], ACT.Copy).then_inc(ohi_ready, 1)
                gate_pair(i, 0, side)
                gate_pair(i, 1)
            gate_pair(4, 0)
            gate_pair(4, 1)

            for index in range(PASS_GLU, PASS_PROJ):
                q = Q_GLU + index - PASS_GLU

                def glu_gate(j, index=index):
                    act.wait_ge(unit_done, 4 * (Q_GLU + index - PASS_GLU) + RING + j + 1)
                    act.activation(ps[:, 2 * j:2 * j + 2, 0:SEQ], ps[:, 2 * j:2 * j + 2, 0:SEQ], ACT.Sigmoid)\
                        .then_inc(glu_sig, 1)
                plain_pass(q, 1, glu_gate if index % 2 else None)
            for p in range(2):
                def take_merged(j, p=p):
                    act.wait_ge(merged, 4 * p + j + 1)
                    act.activation(x_hi[:, 8 * p + 2 * j:8 * p + 2 * j + 2, META:T], ybuf[p][:, 2 * j:2 * j + 2, :],
                                   ACT.Copy).then_inc(mhi_ready, 1)
                plain_pass(Q_PROJ + 3 * p, 3, take_merged)
            def next_x(j):
                if j == 0:
                    act.wait_ge(pair_out, 4 * (PASS_OUT + 1))
                    act.wait_ge(unit_done, 4 * (Q_OUT + 6) + RING)
                for k in (2 * j, 2 * j + 1):
                    upper(2, META, k)
            for p in range(2):
                plain_pass(Q_OUT + 4 * p, 4, lambda j, p=p: square(2, META, 4 * p + j), next_x if p else None)
            act.wait_ge(unit_done, 4 * Q_FFN2 + RING)
            for k in range(DT // 2, DT):
                upper(2, META, k)
            ffn(1, META, Q_FFN2)
            root(3, META)


        @block.vector
        def _(dve):
            step = Tally(dve, dve_step)
            tt, ts, stt = dve.tensor_tensor, dve.tensor_scalar, dve.scalar_tensor_tensor
            dve.sem_inc(lo_ready, RING)
            for credit in (gated, hidden, bu_taken, ys_done):
                dve.sem_inc(credit, 1)

            def split(q, j):
                slot = (j + LEAD) % 4
                if isinstance(q, int) and 4 * q + j + LEAD >= UNITS:
                    return
                dve.wait_ge(hi_ready, q * 4 + j + LEAD + 1)
                tt(w_lo[:, slot, :, :], raw[:, slot, :, :], w_hi[:, slot, :, :].bitcast(f32), SUB).then_inc(lo_ready, 1)

            def settle(q, j):
                dve.wait_ge(lo_ready, q * 4 + j + LEAD + 1 + RING)

            def root_inverse(index, c0):
                dve.wait_ge(root_ready, index + 1)
                dve.reciprocal(scr[:, 5, c0:T], scr[:, 4, c0:T]).then_inc(rms_inv, 1)

            def lower(index, c0, k):
                dve.wait_ge(xhi_ready, index * DT + k + 1)
                stt(x_lo[:, k, c0:T], h[:, k, c0:T], gain[:, index, k:k + 1], x_hi[:, k, c0:T].bitcast(f32), MUL, SUB)\
                    .then_inc(x_ready, 1)

            def add_squares(index, c0, k):
                dve.wait_ge(sq_ready, 8 * index + k + 1)
                if k > 1:
                    dve.wait_ge(summed, 6 * index + k - 1)
                at_k = 2 * (k % 2)
                tt(scr[:, 4:6, c0:T], scr[:, 4:6, c0:T], scr[:, at_k:at_k + 2, c0:T], ADD).then_inc(summed, 1)

            def plain_pass(q, groups, take, before=None, beside=None):
                if groups > 1:
                    with dve.Fori(0, groups - 1) as g:
                        for j in range(4):
                            split(g + q, j)
                for j in range(5):
                    if j:
                        if before:
                            before(j - 1)
                        dve.wait_ge(unit_done, 4 * (q + groups - 1) + RING + j)
                        take(j - 1)
                    if j < 4:
                        split(q + groups - 1, j)
                        if beside:
                            beside(j)

            def ffn(f, c0, q, between=None):
                first = 0
                inverse = scr[:, 5:6, c0:T].broadcast_to([P, 2, T - c0])
                gate, sig = scr[:, 0:2, c0:T], scr[:, 2:4, c0:T]
                for blocks in HALVES:
                    done = f * FF_BLOCKS + first

                    def block(b, mean=False):
                        for j in range(4):
                            split(b * 2 + q, j)
                        if mean:
                            root_inverse(2 * f, c0)
                            dve.wait_ge(rms_inv, 2 * f + 1)
                        dve.wait_ge(unit_done, b * 8 + RING + 4 * q + 4)
                        tt(gate, ps[:, 0:2, 0:T - c0], inverse, MUL).then_inc(gated, 1)
                        split(b * 2 + q + 1, 0)
                        dve.wait_ge(sig_ready, b + done + 1)
                        tt(gate, gate, sig, MUL).then_inc(silu, 1)
                        split(b * 2 + q + 1, 1)
                        dve.wait_ge(silu, b * 2 + 2 * done + 1)
                        tt(gate, gate, inverse, MUL).then_inc(silu, 1)
                        split(b * 2 + q + 1, 2)
                        split(b * 2 + q + 1, 3)
                        dve.wait_ge(silu, b * 2 + 2 * done + 2)
                        dve.wait_ge(unit_done, b * 8 + RING + 4 * q + 8)
                        tt(sig, ps[:, 2:4, 0:T - c0], gate, MUL).then_inc(hidden, 1)
                        dve.wait_ge(hhi_ready, b + done + 1)
                        tt(h_lo[:, ds(b * 2, 2), c0:T], sig, h_hi[:, ds(b * 2, 2), c0:T].bitcast(f32), SUB)\
                            .then_inc(h_ready, 1)
                    peeled = 0 if first else 1
                    if peeled:
                        block(0, True)
                    with dve.Fori(peeled, blocks) as b:
                        block(b)
                    q += 2 * blocks
                    for p in range(2):
                        def residual(j, p=p):
                            rows = slice(8 * p + 2 * j, 8 * p + 2 * j + 2)
                            stt(h[:, rows, c0:T], ps[:, 2 * j:2 * j + 2, 0:T - c0], 0.5, h[:, rows, c0:T], MUL, ADD)\
                                .then_inc(pair_out, 1)
                        if first:
                            dve.wait_ge(pair_out, 4 * (f * PASS_FFN2 + p + 1))

                        def add(j, p=p):
                            if 4 * p + j >= 2:
                                add_squares(1 + 2 * f, c0, 4 * p + j - 1)
                        plain_pass(q, blocks // 2, residual, add if first else None)
                        q += blocks // 2
                        if between and not first:
                            between(1 + p)
                    first += blocks

            dve.wait_ge(small_in[2], 16)
            step(tt(lbt[:, 2, :], lb[:, 0, :], lb[:, 1, :], ALU.max))
            step.join()
            step(tt(lbt[:, 0, :], lb[:, 0, :], lbt[:, 2, :], SUB))
            step(tt(lbt[:, 1, :], lb[:, 1, :], lbt[:, 2, :], SUB))

            def parameters(stage):
                if stage == 1:
                    dve.wait_ge(lb_exp, 1)
                    step(tt(lbt[:, 2, :], lbt[:, 0, :], lbt[:, 1, :], ADD))
                    step.join()
                    step(dve.reciprocal(lbt[:, 1, :], lbt[:, 2, :]))
                    step.join()
                    step(tt(lb[:, 0, :], lbt[:, 0, :], lbt[:, 1, :], MUL))
                    step.join()
                    step(ts(lb[:, 1, :], lb[:, 0, :], -1.0, 1.0, MUL, ADD))
                if stage == 2:
                    dve.wait_ge(sv_pool, 3)
                    dve.reciprocal(sv[:, 13, :], sv[:, 12, :]).then_inc(den_inv, 1)

            dve.wait_ge(small_in[0], 16)
            for c in range(4):
                for k in range(4 * c, 4 * c + 4):
                    lower(0, 0, k)
                if c < LEAD:
                    dve.wait_ge(hi_ready, c + 1)
                    tt(w_lo[:, c, :, :], raw[:, c, :, :], w_hi[:, c, :, :].bitcast(f32), SUB).then_inc(lo_ready, 1)
                for k in (2 * c, 2 * c + 1):
                    if 0 < k < 7:
                        add_squares(0, 0, k)
            ffn(0, 0, 0, parameters)
            root_inverse(1, 0)
            for k in range(DT):
                dve.wait_ge(xhi_ready, DT + k + 1)
                stt(x_lo[:, k, :], scr[:, k % 4, :], gain[:, 1, k:k + 1], x_hi[:, k, :].bitcast(f32), MUL, SUB)\
                    .then_inc(x_ready, 1)
                if k % 4 == 3 and k > 3:
                    split(Q_U, k // 4 - 1)
            split(Q_U, 3)
            for j in range(4):
                split(Q_U + 1, j)

            dve.wait_ge(tables, 1)
            dve.wait_ge(small_in[4], 16)
            with dve.Fori(0, UT) as ut:
                step.turn(ut, SPU * 12)
                for jj in range(SPU):
                    tile = ut * SPU + jj

                    def e(table, c0):
                        return table[:, ds(ut * SPU + jj, 1), c0:T].rearrange("p a t -> p (a t)")
                    split(tile + Q_SCAN, 0)
                    settle(tile + Q_SCAN, 0)
                    dve.wait_ge(bu_done, tile + 1)
                    step(tt(scr[:, 0, :], ps[:, 4, 0:T], e(e_re, 0), MUL))
                    step(tt(scr[:, 1, :], ps[:, 5, 0:T], e(e_im, 0), MUL))
                    step(tt(scr[:, 2, :], ps[:, 5, 0:T], e(e_re, 0), MUL))
                    tt(scr[:, 3, :], ps[:, 4, 0:T], e(e_im, 0), MUL).then_inc(bu_taken, 1)
                    split(tile + Q_SCAN, 1)
                    dve.wait_ge(bu_taken, tile + 2)
                    step(tt(scr[:, 0, :], scr[:, 0, :], scr[:, 1, :], ADD))
                    step(tt(scr[:, 2, :], scr[:, 2, :], scr[:, 3, :], SUB))
                    step.join()
                    decay = mag[:, ds(tile, 1)].broadcast_to([P, T])
                    step(dve.tensor_tensor_scan(scr[:, 1, :], decay, scr[:, 0, :], 0.0, MUL, ADD))
                    step(dve.tensor_tensor_scan(scr[:, 3, :], decay, scr[:, 2, :], 0.0, MUL, ADD))
                    step.join()
                    split(tile + Q_SCAN, 2)
                    step(tt(scr[:, 0, META:T], scr[:, 1, META:T], e(e_re, META), MUL))
                    step(tt(scr[:, 2, META:T], scr[:, 3, META:T], e(e_im, META), MUL))
                    step(tt(scr[:, 4, META:T], scr[:, 1, META:T], e(e_im, META), MUL))
                    step(tt(scr[:, 5, META:T], scr[:, 3, META:T], e(e_re, META), MUL))
                    step.join()
                    dve.wait_ge(cx_done, tile + 1)
                    step(tt(sx[:, 0, META:T], scr[:, 0, META:T], scr[:, 2, META:T], SUB))
                    tt(sx[:, 1, META:T], scr[:, 4, META:T], scr[:, 5, META:T], ADD).then_inc(scanned, 1)
                    split(tile + Q_SCAN, 3)
                dve.wait_ge(cx_done, ut * SPU + SPU + 1)
                stt(ys[:, ds(ut, 1), :].rearrange("p a t -> p (a t)"),
                    u5[:, ds(ut, 1), META:T].rearrange("p a t -> p (a t)"), dsk[:, ds(ut, 1)], ps[:, 6, 0:SEQ],
                    MUL, ADD).then_inc(ys_done, 1)
            step.done(UT)

            g = scr[:, 0:4, 0:SEQ]
            split(Q_REST, 0)
            dve.wait_ge(ys_done, UT + 1)
            step(tt(g, ys[:, :, :], ys[:, :, :], MUL))
            step.join()
            step(ts(g, g, GELU_A, 1.0, MUL, ADD))
            step.join()
            split(Q_REST, 1)
            tt(g, g, ys[:, :, :], MUL).then_inc(z_arg, 1)
            split(Q_REST, 2)
            dve.wait_ge(z_sig, 1)
            tt(ys[:, :, :], ys[:, :, :], g, MUL).then_inc(z_val, 1)
            split(Q_REST, 3)
            dve.wait_ge(z_val, 1)
            dve.wait_ge(zhi_ready, 1)
            tt(z_lo[:, :, :], ys[:, :, :], z_hi[:, :, :].bitcast(f32), SUB).then_inc(z_ready, 1)

            f_at = (0, 272, 408, 476, 510, 528, 536, 540)

            def level(i):
                m = 1 << i
                c0 = 0 if m < META else META
                n = T - c0
                k_old, k_new = [ks[:, i + d, c0:T].rearrange("p (b s m) -> p b s m", s=2, m=m) for d in range(2)]
                q_old, q_new = [qs[:, i + 1 + d, :].rearrange("p (b s m) -> p b s m", s=2, m=m) for d in range(2)]
                skip = META // m if m < META else (1 if m == META else 0)
                at_k = skip if m >= META else 0
                f_k = fm[:, f_at[i] + at_k:f_at[i] + at_k + n // m].rearrange("p (b s) -> p b s", s=2)
                f_q = fm[:, f_at[i] + skip:f_at[i] + skip + SEQ // m].rearrange("p (b s) -> p b s", s=2)

                def wide(f, nb):
                    return f.unsqueeze(2).broadcast_to([P, nb, m])
                step.join()
                step(tt(k_new[:, :, 0, :], k_old[:, :, 0, :], wide(f_k[:, :, 1], n // m // 2), MUL))
                step(tt(q_new[:, :, 1, :], q_old[:, :, 1, :], wide(f_q[:, :, 0], SEQ // m // 2), MUL))
                step(dve.tensor_copy(k_new[:, :, 1, :], k_old[:, :, 1, :]))
                step(dve.tensor_copy(q_new[:, :, 0, :], q_old[:, :, 0, :]))
                step(tt(fm[:, f_at[i + 1]:f_at[i + 1] + n // m // 2], f_k[:, :, 0], f_k[:, :, 1], MUL))

            def head_levels(hd, part):
                if part == 0:
                    dve.wait_ge(head_sig, hd + 1)
                    step(stt(qs[:, 0, :], qfv[:, ds(hd, 1), META:T].rearrange("p a t -> p (a t)"), DK ** -0.5,
                             scr[:, 0, 0:SEQ], MUL, MUL))
                    step(ts(fm[:, 0:T], scr[:, 1, :], lb[:, 1, ds(hd, 1)], lb[:, 0, ds(hd, 1)], MUL, ADD))
                    step.join()
                    step(ts(ks[:, 0, :], fm[:, 0:T], -1.0, 1.0, MUL, ADD))
                    step(tt(qs[:, 1, :], qs[:, 0, :], fm[:, META:T], MUL))
                    for i in range(3):
                        level(i)
                else:
                    for i in range(3, 7):
                        level(i)
                    step.join()
                    ts(ks[:, 5, 0:META], ks[:, 4, 0:META], fm[:, f_at[7]:f_at[7] + 1], None, MUL).then_inc(levels, 1)

            step(dve.memset(ps[:, 4:6, :], 0.0))
            step(dve.memset(ps[:, 6:8, :], 0.0))
            split(Q_REST + 1, 0)
            split(Q_REST + 1, 1)
            dve.wait_ge(mask_ready, 1)
            head_levels(0, 0)
            split(Q_REST + 1, 2)
            head_levels(0, 1)
            split(Q_REST + 1, 3)

            def head(hd, following):
                def masked(b):
                    step(tt(prod[:, :, :], ps[:, 4 + 2 * b:6 + 2 * b, :].rearrange("p b (l t) -> p (b l) t", l=4),
                            mask[:, :, :], MUL))
                    step.join()
                    ins = dve.tensor_reduce(att[:, b, :], prod[:, :, :].rearrange("p l t -> p t l"), AX.X, ADD)
                    if b:
                        ins.then_inc(att_ready, 1)
                    else:
                        step(ins)
                dve.wait_ge(scored, hd + 1)
                masked(0)
                step.join()
                masked(1)
                if following:
                    head_levels(hd + 1, 0)
                    head_levels(hd + 1, 1)
                split(hd + Q_HEADS, 1)
                split(hd + Q_HEADS, 2)
                split(hd + Q_HEADS, 3)
                if following:
                    split(hd + Q_HEADS + 1, 0)

            split(Q_HEADS, 0)
            with dve.Fori(0, HEADS - 1) as hd:
                step.turn(hd, 42)
                head(hd, True)
            step.done(HEADS - 1)
            head(HEADS - 1, False)

            dve.wait_ge(ot_done, HEADS + 1)
            with dve.Fori(0, 4) as i:
                step.turn(i, 1)
                g3 = gout[:, ds(i * 3, 3), :]
                split(i * 2 + Q_GATES, 0)
                dve.wait_ge(sgo_ready, i + 1)
                step(tt(g3, g3, sgs[:, :, :], MUL))
                split(i * 2 + Q_GATES, 1)
                step.join()
                tt(g3, g3, qfv[:, ds(i * 3, 3), META:T], MUL).then_inc(og_ready, 1)
                split(i * 2 + Q_GATES, 2)
                split(i * 2 + Q_GATES, 3)
                split(i * 2 + Q_GATES + 1, 0)
                dve.wait_ge(og_ready, i + 1)
                dve.wait_ge(ohi_ready, i + 1)
                tt(o_lo[:, ds(i * 3, 3), :], g3, o_hi[:, ds(i * 3, 3), :].bitcast(f32), SUB).then_inc(o_ready, 1)
                for j in range(1, 4):
                    split(i * 2 + Q_GATES + 1, j)
            step.done(4)
            for c in range(2):
                for j in range(4):
                    split(Q_GATES + 8 + c, j)

            dve.wait_ge(block_out, M_GATES + GB)
            for index in range(PASS_GLU, PASS_PROJ):
                p = (index - PASS_GLU) // 2
                y = ybuf[p]

                def take_a(j, y=y):
                    dve.tensor_copy(y[:, 2 * j:2 * j + 2, :], ps[:, 2 * j:2 * j + 2, 0:SEQ]).then_inc(pair_out, 1)

                def take_b(j, y=y, p=p):
                    dve.wait_ge(glu_sig, 4 * p + j + 1)
                    yy = y[:, 2 * j:2 * j + 2, :]
                    tt(yy, ps[:, 2 * j:2 * j + 2, 0:SEQ], yy, MUL).then_inc(pair_out, 1)
                    dve.wait_ge(pair_out, 4 * (PASS_GLU + 2 * p + 1) + j + 1)
                    t = DT + 8 * p + 2 * j - 2 * GA
                    step(tt(yy, yy, gates_b[:, t:t + 2, :], MUL))
                if index % 2:
                    dve.wait_ge(pair_out, 4 * index)
                plain_pass(Q_GLU + index - PASS_GLU, 1, take_b if index % 2 else take_a)
            step.join()
            for p in range(2):
                def take_proj(j, p=p):
                    t = 8 * p + 2 * j
                    gate = gates_a[:, t:t + 2, :] if t < 2 * GA else gates_b[:, t - 2 * GA:t - 2 * GA + 2, :]
                    yy = ybuf[p][:, 2 * j:2 * j + 2, :]
                    tt(scr[:, 0:2, 0:SEQ], ps[:, 2 * j:2 * j + 2, 0:SEQ], gate, MUL).then_inc(pair_out, 1)
                    dve.wait_ge(pair_out, 4 * (PASS_PROJ + p) + j + 1)
                    tt(yy, yy, scr[:, 0:2, 0:SEQ], ADD).then_inc(merged, 1)
                    dve.wait_ge(merged, 4 * p + j + 1)
                    dve.wait_ge(mhi_ready, 4 * p + j + 1)
                    tt(x_lo[:, t:t + 2, META:T], yy, x_hi[:, t:t + 2, META:T].bitcast(f32), SUB).then_inc(m_ready, 1)
                plain_pass(Q_PROJ + 3 * p, 3, take_proj)
            for p in range(2):
                def take_out(j, p=p):
                    t = 8 * p + 2 * j
                    tt(h[:, t:t + 2, META:T], ps[:, 2 * j:2 * j + 2, 0:SEQ], h[:, t:t + 2, META:T], ADD).then_inc(pair_out, 1)

                def add(j, p=p):
                    if 4 * p + j >= 2:
                        add_squares(2, META, 4 * p + j - 1)
                def next_x(j):
                    for k in (2 * j, 2 * j + 1):
                        lower(2, META, k)
                plain_pass(Q_OUT + 4 * p, 4, take_out, add, next_x if p else None)
            for k in range(DT // 2, DT):
                lower(2, META, k)
            ffn(1, META, Q_FFN2)
            root_inverse(3, META)
            dve.wait_ge(rms_inv, 4)
            for k in range(DT):
                stt(h[:, k, META:T], h[:, k, META:T], gain[:, 3, k:k + 1], scr[:, 5, META:T], MUL, MUL).then_inc(y_final, 1)

        @block.gpsimd
        def _(pool):
            step = Tally(pool, pool_step)
            tt, ts = pool.tensor_tensor, pool.tensor_scalar

            def chain(ins):
                step(ins)
                step.join()
            pool.memset(cd[:, :, :, :], 0.0).then_inc(consts, 1)
            pool.memset(ones[:, :], 1.0 / D)
            for c, value in enumerate((1.0 / DK, EPS, -0.5)):
                pool.memset(small[:, c:c + 1], value)
            pool.memset(bd[:, :, :, :], 0.0)
            chain(pool.memset(ident[:, :], 0.0))
            pool.affine_select(out=ident[:, :], in_=ident[:, :], compare_op=ALU.not_equal, fill=1.0, base=0,
                               pattern=[[-1, P]], channel_multiplier=1).then_inc(consts, 1)
            v = [sv[:, i, :] for i in range(14)]
            lr, li = v[0], v[1]
            pool.wait_ge(sv_act, 1)
            tt(v[4], lr, v[3], MUL).then_inc(sv_pool, 1)
            chain(tt(v[5], li, v[3], MUL))
            chain(ts(v[6], v[5], INV_TWO_PI, None, MUL))
            chain(ts(v[6], v[6], ROUNDER, None, ADD))
            chain(ts(v[6], v[6], -ROUNDER, None, ADD))
            for part in TWO_PI_PARTS:
                chain(ts(v[7], v[6], part, None, MUL))
                chain(tt(v[5], v[5], v[7], SUB))
            chain(ts(v[8], v[5], 0.5, None, MUL))
            ts(v[9], v[5], 0.25, None, MUL).then_inc(sv_pool, 1)
            chain(tt(v[12], lr, lr, MUL))
            chain(tt(v[7], li, li, MUL))
            tt(v[12], v[12], v[7], ADD).then_inc(sv_pool, 1)
            pool.wait_ge(sv_act, 3)
            sn, sq, c, s, n = v[10], v[11], v[8], v[7], v[9]
            chain(tt(v[6], sq, sq, MUL))
            chain(ts(v[6], v[6], -2.0, 1.0, MUL, ADD))
            chain(tt(s, sn, v[6], MUL))
            chain(ts(s, s, 2.0, None, MUL))
            chain(tt(c, sn, sn, MUL))
            chain(ts(c, c, -2.0, 1.0, MUL, ADD))
            chain(tt(n, c, c, MUL))
            chain(tt(v[5], s, s, MUL))
            chain(tt(n, n, v[5], ADD))
            chain(ts(n, n, -0.5, 1.5, MUL, ADD))
            chain(tt(s, s, n, MUL))
            chain(tt(c, c, n, MUL))
            a_re, a_im = v[10], v[11]
            chain(tt(a_re, mag[:, :], c, MUL))
            chain(tt(a_im, mag[:, :], s, MUL))
            chain(ts(a_re, a_re, -1.0, None, ADD))
            pool.wait_ge(den_inv, 1)
            c_re, c_im = v[3], v[4]
            chain(tt(c_re, a_re, lr, MUL))
            chain(tt(c_im, a_im, li, MUL))
            chain(tt(c_re, c_re, c_im, ADD))
            chain(tt(c_re, c_re, v[13], MUL))
            chain(tt(c_im, a_im, lr, MUL))
            chain(tt(v[5], a_re, li, MUL))
            chain(tt(c_im, c_im, v[5], SUB))
            chain(tt(c_im, c_im, v[13], MUL))
            pool.wait_ge(small_in[5], 16)
            b = btmp[:, 0:2 * ST * GP].rearrange("p (r j c) -> p r j c", r=2, j=ST)
            for g in range(2):
                rows = slice(64 * g, 64 * g + 64)

                def coef(x):
                    return x[rows, :].unsqueeze(2).broadcast_to([64, ST, GP])
                for r, (other, op) in enumerate(((1, SUB), (0, ADD))):
                    out = bd[rows, r, :, g * GP:(g + 1) * GP]
                    chain(tt(out, b[rows, r, :, :], coef(c_re), MUL))
                    chain(tt(bprod[rows, :, :], b[rows, other, :, :], coef(c_im), MUL))
                    chain(tt(out, out, bprod[rows, :, :], op))
            pool.sem_inc(bbar_ready, 1)
            for g in range(2):
                pool.wait_ge(small_in[6 + g], 16)
            chain(ts(cd[:, :, 1, :], cd[:, :, 1, :], -1.0, None, MUL))
            pool.memset(e_re[:, :, 0:1], 1.0)
            chain(pool.memset(e_im[:, :, 0:1], 0.0))
            p_re, p_im, n_re, n_im = c, s, v[9], v[10]
            tmp = btmp[:, :].rearrange("p (j t) -> p j t", j=ST)
            n = 1
            while n < T:
                for t0 in range(0, min(n, T - n), 32):
                    w = min(32, n - t0, T - n - t0)
                    src, dst = slice(t0, t0 + w), slice(n + t0, n + t0 + w)

                    def power(x):
                        return x.unsqueeze(2).broadcast_to([P, ST, w])
                    for out, one, two, op in ((e_re, p_re, p_im, SUB), (e_im, p_im, p_re, ADD)):
                        chain(tt(out[:, :, dst], e_re[:, :, src], power(one), MUL))
                        chain(tt(tmp[:, :, 0:w], e_im[:, :, src], power(two), MUL))
                        chain(tt(out[:, :, dst], out[:, :, dst], tmp[:, :, 0:w], op))
                chain(tt(n_re, p_re, p_re, MUL))
                chain(tt(v[5], p_im, p_im, MUL))
                chain(tt(n_re, n_re, v[5], SUB))
                chain(tt(n_im, p_re, p_im, MUL))
                chain(ts(n_im, n_im, 2.0, None, MUL))
                p_re, p_im, n_re, n_im = n_re, n_im, p_re, p_im
                n *= 2
            pool.sem_inc(tables, 1)
            pool.wait_ge(rms_inv, 2)
            for k in range(DT):
                if k >= 4:
                    pool.wait_ge(x_ready, DT + k - 3)
                tt(scr[:, k % 4, :], h[:, k, :], scr[:, 5, :], MUL).then_inc(xf_ready, 1)
            pool.wait_ge(ys_done, UT + 1)
            chain(pool.memset(mask[:, :, :], 0.0))
            chain(pool.affine_select(out=mask[:, 0, :], in_=mask[:, 0, :], compare_op=ALU.not_equal, fill=1.0, base=0,
                                     pattern=[[-1, P]], channel_multiplier=1))
            for l in range(1, LEVELS):
                m = 1 << (l - 1)
                right = mask[:, l, :].rearrange("p (b s m) -> p b s m", s=2, m=m)[:, :, 1, :]
                nb = P // (2 * m)
                chain(pool.memset(right, 1.0))
                chain(pool.affine_select(out=right, in_=right, compare_op=ALU.is_ge, fill=0.0, base=0,
                                         pattern=[[-2 * m, nb], [0, m]], channel_multiplier=1))
                chain(pool.affine_select(out=right, in_=right, compare_op=ALU.is_ge, fill=0.0, base=m - 1,
                                         pattern=[[2 * m, nb], [0, m]], channel_multiplier=-1))
            pool.sem_inc(mask_ready, 1)
            with pool.Fori(0, HEADS) as hd:
                step.turn(hd, 2)
                pool.wait_ge(ss_ready, hd + 1)
                chain(tt(ss[:, 1, :], ss[:, 0, :], small[:, 0:1].broadcast_to([P, 2]), MUL))
                chain(tt(ss[:, 1, :], ss[:, 1, :], small[:, 1:2].broadcast_to([P, 2]), ADD))
                tt(ss[:, 1, :], ss[:, 1, :], small[:, 2:3].broadcast_to([P, 2]), ALU.pow).then_inc(rr_ready, 1)
            step.done(HEADS)


def kernel(x, meta_tokens, norm_ffn1, ffn1_w_gate, ffn1_w_up, ffn1_w_down, norm_mix, w_in, hg_lower_bounds, hg_norm,
           hg_w_proj, s5_lam_re, s5_lam_im, s5_log_step, s5_b_re, s5_b_im, s5_c_re, s5_c_im, s5_d, s5_w_glu_a,
           s5_w_glu_b, w_out, norm_ffn2, ffn2_w_gate, ffn2_w_up, ffn2_w_down, norm_final):
    import numpy as np
    import concourse.bacc as bacc
    from concourse.bass_utils import run_bass_kernel_spmd

    nc = bacc.Bacc("TRN2", target_bir_lowering=False, num_devices=1)
    arrays = {}

    def tensor(name, a):
        a = np.ascontiguousarray(a)
        arrays[name] = a
        return nc.dram_tensor(name, a.shape, mybir.dt.from_np(a.dtype), kind="ExternalInput").ap()

    def tiles(a, n):
        return np.asarray(a).reshape(n, P).T

    args = [
        tensor("xT", np.asarray(x)[0].T),
        tensor("metaT", np.asarray(meta_tokens).T),
        tensor("gains", np.stack([tiles(g, DT) for g in (norm_ffn1, norm_mix, norm_ffn2, norm_final)], 1)),
        [tensor(n, np.asarray(w)[0]) for n, w in (("gate1", ffn1_w_gate), ("up1", ffn1_w_up), ("down1", ffn1_w_down))],
        tensor("w_in", np.asarray(w_in)[0]),
        tensor("hg_lb", np.stack([tiles(r, HEADS) for r in np.asarray(hg_lower_bounds)], 1)),
        tensor("hg_norm", tiles(hg_norm, HEADS)),
        tensor("w_proj", np.asarray(hg_w_proj)[0]),
        tensor("s5v", np.stack([tiles(v, ST) for v in (s5_lam_re, s5_lam_im, np.repeat(np.asarray(s5_log_step)[0], STATE))], 1)),
        tensor("s5b", np.stack([np.asarray(b).reshape(ST, P, GP).transpose(1, 0, 2) for b in (s5_b_re, s5_b_im)], 1)),
        tensor("s5c", np.stack([np.asarray(c)[0].transpose(0, 2, 1).reshape(ST, P, GP).transpose(1, 0, 2)
                                for c in (s5_c_re, s5_c_im)], 2)),
        tensor("s5d", tiles(s5_d, UT)),
        [tensor(n, np.asarray(w)[0]) for n, w in (("glu_a", s5_w_glu_a), ("glu_b", s5_w_glu_b))],
        tensor("w_out", np.asarray(w_out)[0]),
        [tensor(n, np.asarray(w)[0]) for n, w in (("gate2", ffn2_w_gate), ("up2", ffn2_w_up), ("down2", ffn2_w_down))],
        nc.dram_tensor("outT", (D, SEQ), mybir.dt.float32, kind="ExternalOutput").ap(),
    ]
    program(nc, *args)
    r = run_bass_kernel_spmd(nc, [arrays], core_ids=[0])
    return r.results[0]["outT"].T[None]
```

```python
import concourse.bass as bass
from concourse import mybir
from contextlib import ExitStack

P = 128
D = 2048
DT = D // P
META, SEQ = 16, 256
T = META + SEQ
FF = 5632
HEADS, DK = 12, 128
HG = HEADS * DK
GROUPS, GP, STATE = 32, 16, 64
S5W = GROUPS * GP
UT = S5W // P
ST = GROUPS * STATE // P
SPU = ST // UT
EPS = 1e-6
LEVELS = 8
SLOTS = 6

KT, NC = 4, 256
RING = 4
LEAD = 3
FF_BLOCKS = FF // NC
HALVES = (12, 10)
HT = HALVES[0] * 2
HG_BLOCKS = HG // NC
U_BLOCK = 4 * HG_BLOCKS
GATE_BLOCK = U_BLOCK + S5W // NC
GATES = 2 * D // NC
GA = HEADS - HG_BLOCKS
GB = GATES - GA

FFN_QUADS = 2 * FF_BLOCKS + 2 * (FF // (KT * P))
Q_U = FFN_QUADS
Q_SCAN = Q_U + S5W // NC
Q_REST = Q_SCAN + ST
Q_HEADS = Q_REST + 3 * HG_BLOCKS - ST
Q_GATES = Q_HEADS + HEADS
Q_GLU = Q_GATES + GB
Q_PROJ = Q_GLU + 4 * (S5W // (KT * P))
Q_OUT = Q_PROJ + 2 * (HG // (KT * P))
Q_FFN2 = Q_OUT + 2 * (D // (KT * P))
UNITS = 4 * (Q_FFN2 + FFN_QUADS)
PASS_GLU, PASS_PROJ, PASS_OUT, PASS_FFN2 = 4, 8, 10, 12
PASSES_BEFORE = (0, PASS_GLU, PASS_FFN2, 16)
POOL_PAIRS = (3, 7)
NORM_BANK = (7, 0, 7, 0)
M_HEADS = 20
M_GATES = M_HEADS + HEADS

PI = 3.14159265358979
TWO_PI_PARTS = (6.28125, 0.0019340515136718750, 1.2556659146e-06)
INV_TWO_PI = 0.15915494309189535
ROUNDER = 12582912.0
GELU_A, GELU_B = 0.044715, 1.5957691216057308


class Tally:

    def __init__(self, engine, sem):
        self.engine, self.sem, self.base, self.n = engine, sem, 0, 0

    def __call__(self, ins):
        ins.then_inc(self.sem, 1)
        self.n += 1

    def join(self):
        self.engine.wait_ge(self.sem, self.base + self.n)

    def turn(self, i, per):
        self.start, self.per = self.n + (self.base if isinstance(self.base, int) else 0), per
        self.base, self.n = i * per + self.start, 0

    def done(self, times):
        assert self.n == self.per, (self.n, self.per)
        self.base, self.n = self.start + times * self.per, 0


def program(nc, xT, metaT, gains, ffn1, w_in, hg_lb, hg_norm, w_proj, s5v, s5b, s5c, s5d, w_glu, w_out, ffn2, outT):
    f32, f32r, i32 = mybir.dt.float32, mybir.dt.float32r, mybir.dt.int32
    bf16 = mybir.dt.bfloat16
    ALU, ACT, AX = mybir.AluOpType, mybir.ActivationFunctionType, mybir.AxisListType
    MUL, ADD, SUB = ALU.mult, ALU.add, ALU.subtract
    ds = bass.ds

    top = ExitStack()
    with top:
        def sem(name):
            return top.enter_context(nc.semaphore(name))

        def sb(name, shape, dt=f32):
            return top.enter_context(nc.sbuf_tensor(name, shape, dt))

        raw = sb("raw", [P, RING, KT, NC])
        w_hi = sb("w_hi", [P, RING, KT, NC], f32r)
        w_lo = sb("w_lo", [P, RING, KT, NC], f32r)
        h = sb("h", [P, DT, T])
        xs = sb("xs", [P, DT, 2, T], f32r)
        x_hi, x_lo = xs[:, :, 0, :], xs[:, :, 1, :]
        gain = sb("gain", [P, 4, DT])
        ones = sb("ones", [P, P])
        ident = sb("ident", [P, P])
        scr = sb("scr", [P, 6, T])
        lb = sb("lb", [P, 2, HEADS])
        hgn = sb("hgn", [P, HEADS])
        dsk = sb("dsk", [P, UT])
        mag = sb("mag", [P, ST])
        ss = sb("ss", [P, 2, 2])
        small = sb("small", [P, 4])
        spare = sb("spare", [P, 1])
        ps = top.enter_context(nc.psum_tensor("ps", [P, 8, 512], f32))

        def at(offset, name, shape, dt=f32):
            with ExitStack() as c:
                if offset:
                    c.enter_context(nc.sbuf_tensor("below_" + name, [P, offset], f32))
                return c.enter_context(nc.sbuf_tensor(name, shape, dt))

        TAB = 2 * HT * T + 2016
        hs = at(0, "hs", [P, HT, 2, T], f32r)
        h_hi, h_lo = hs[:, :, 0, :], hs[:, :, 1, :]
        sv = at(2 * HT * T, "sv", [P, 14, ST])
        lbt = at(2 * HT * T + 1760, "lbt", [P, 3, HEADS])
        bd = at(2 * HT * T + 224, "bd", [P, 2, ST, 2 * GP])
        btmp = at(2 * HT * T + 1248, "btmp", [P, ST * 32])
        bprod = at(2 * HT * T + 1760, "bprod", [P, ST, GP])
        e_re = at(TAB, "e_re", [P, ST, T])
        e_im = at(TAB + ST * T, "e_im", [P, ST, T])
        bt = at(TAB + 2 * ST * T, "bt", [P, UT, 2, P])
        cd = at(TAB + 2 * ST * T + 1024, "cd", [P, ST, 2, 2 * GP])
        QFV = 3 * HEADS * T
        qfv = at(0, "qfv", [P, 3 * HEADS, T])
        ys = at(QFV, "ys", [P, UT, SEQ])
        U5 = QFV + UT * SEQ
        u5 = at(U5, "u5", [P, UT, T])
        st_u = at(U5 + UT * T, "st_u", [P, T])
        st_b = at(U5 + UT * T + T, "st_b", [P, 2, P])
        st_c = at(U5 + UT * T + T + 256, "st_c", [P, SPU, 2, 2 * GP])
        sx = at(U5 + UT * T + T + 512, "sx", [P, 2, T])
        assert U5 + UT * T + T + 512 + 2 * T <= TAB
        gates_a = at(QFV, "gates_a", [P, 2 * GA, SEQ])
        zs = at(QFV + 3072, "zs", [P, UT, 2, SEQ], f32r)
        z_hi, z_lo = zs[:, :, 0, :], zs[:, :, 1, :]
        gout = at(QFV + 5120, "gout", [P, HEADS, SEQ])
        HD = QFV + 5120 + 3072
        qs = at(HD, "qs", [P, LEVELS + 1, SEQ])
        ks = at(HD + 2304, "ks", [P, LEVELS, T])
        fm = at(HD + 2304 + 2176, "fm", [P, 560])
        mask = at(HD + 5040, "mask", [P, SLOTS, P], bf16)
        prod = at(HD + 5552, "prod", [P, SLOTS, P])
        att = at(HD + 6576, "att", [P, 3, P])
        att_m = at(HD + 6960, "att_m", [META, 2, P])
        v_tok = at(HD + 7216, "v_tok", [P, 2, P])
        v_meta = at(HD + 7472, "v_meta", [META, P])
        os = at(HEADS * T, "os", [P, HEADS, 2, SEQ], f32r)
        o_hi, o_lo = os[:, :, 0, :], os[:, :, 1, :]
        gates_b = at(HD, "gates_b", [P, 2 * GB, SEQ])
        sgs = at(HD + 5120, "sgs", [P, 3, SEQ])
        y_a = at(QFV + 5120, "y_a", [P, 8, SEQ])
        y_b = at(HD + 5120, "y_b", [P, 8, SEQ])
        ybuf = (y_a, y_b)

        raw_ready = [sem(f"raw_ready{j}") for j in range(RING)]
        hi_ready = sem("hi_ready")
        lo_ready = sem("lo_ready")
        unit_done = sem("unit_done")
        x_in = [sem(f"x_in{c}") for c in range(4)]
        meta_in = sem("meta_in")
        small_in = [sem(f"small_in{c}") for c in range(9)]
        consts = sem("consts")
        dve_step = sem("dve_step")
        pool_step = sem("pool_step")
        sq_ready = sem("sq_ready")
        sq_used = sem("sq_used")
        summed = sem("summed")
        lb_exp = sem("lb_exp")
        root_ready = sem("root_ready")
        rms_inv = sem("rms_inv")
        xf_dve = sem("xf_dve")
        xf_pool = sem("xf_pool")
        xhi_ready = sem("xhi_ready")
        x_ready = sem("x_ready")
        sig_ready = sem("sig_ready")
        gated = sem("gated")
        halves = sem("halves")
        silu = sem("silu")
        hidden = sem("hidden")
        hhi_ready = sem("hhi_ready")
        h_ready = sem("h_ready")
        pair_out = sem("pair_out")
        block_out = sem("block_out")
        sv_act = sem("sv_act")
        sv_pool = sem("sv_pool")
        den_inv = sem("den_inv")
        bbar_ready = sem("bbar_ready")
        bt_psum = sem("bt_psum")
        bt_out = sem("bt_out")
        tables = sem("tables")
        staged = sem("staged")
        bu_done = sem("bu_done")
        bu_taken = sem("bu_taken")
        scanned = sem("scanned")
        cx_done = sem("cx_done")
        ys_done = sem("ys_done")
        z_arg = sem("z_arg")
        z_sig = sem("z_sig")
        z_val = sem("z_val")
        zhi_ready = sem("zhi_ready")
        z_ready = sem("z_ready")
        f_sig = sem("f_sig")
        f_made = sem("f_made")
        head_in = sem("head_in")
        v_staged = sem("v_staged")
        levels = sem("levels")
        mask_ready = sem("mask_ready")
        scored = sem("scored")
        v_ready = sem("v_ready")
        att_ready = sem("att_ready")
        o_done = sem("o_done")
        ss_ready = sem("ss_ready")
        rr_ready = sem("rr_ready")
        on_ready = sem("on_ready")
        ot_psum = sem("ot_psum")
        ot_done = sem("ot_done")
        sgo_ready = sem("sgo_ready")
        og_ready = sem("og_ready")
        ohi_ready = sem("ohi_ready")
        o_ready = sem("o_ready")
        glu_sig = sem("glu_sig")
        merged = sem("merged")
        mhi_ready = sem("mhi_ready")
        m_ready = sem("m_ready")
        gained = sem("gained")
        y_final = sem("y_final")
        y_pool = sem("y_pool")
        stored = [sem(f"stored{c}") for c in range(4)]

        block = top.enter_context(nc.Block())

        @block.sync
        def _(sp):
            def load(j, w, group, col, u):
                sp.wait_ge(lo_ready, u + 1)
                sp.dma_start(raw[:, j, :, :],
                             w.rearrange("(g t p) n -> p g t n", t=KT, p=P)[:, ds(group, 1), :, ds(col, NC)]
                             .rearrange("p g t n -> p (g t) n")).then_inc(raw_ready[j], 16)

            def column_block(w, col, q, before=None):
                for j in range(4):
                    if before:
                        before(j)
                    load(j, w, j, col, 4 * q + j)

            def passes(w, first_group, groups, q):
                for p in range(2):
                    with sp.Fori(0, groups) as g:
                        for j in range(4):
                            load(j, w, g + first_group, (4 * p + j) * NC, (g + q) * 4 + j)
                    q += groups
                return q

            def load_x(c):
                sp.dma_start(h[:, 4 * c:4 * c + 4, META:T],
                             xT.rearrange("(k p) t -> p k t", p=P)[:, 4 * c:4 * c + 4, :]).then_inc(x_in[c], 16)
                if c == 0:
                    sp.dma_start(h[:, :, 0:META], metaT.rearrange("(k p) t -> p k t", p=P)).then_inc(meta_in, 16)

            def ffn(w_gate, w_up, w_down, q):
                first = 0
                for blocks in HALVES:
                    peeled = 1 if q == 0 else 0
                    if peeled:
                        column_block(w_gate, 0, 0, load_x)
                        column_block(w_up, 0, 1)
                    with sp.Fori(peeled, blocks) as b:
                        column_block(w_gate, (b + first) * NC, b * 2 + q)
                        column_block(w_up, (b + first) * NC, b * 2 + q + 1)
                    q += 2 * blocks
                    q = passes(w_down, first // 2, blocks // 2, q)
                    first += blocks

            def columns(first, n, q):
                with sp.Fori(0, n) as b:
                    column_block(w_in, (b + first) * NC, b + q)

            ffn(*ffn1, 0)
            columns(U_BLOCK, 2, Q_U)
            with sp.Fori(0, UT) as ut:
                column_block(w_in, ut * NC, ut * SPU + Q_SCAN)
                for jj in range(1, SPU):
                    column_block(w_in, (ut * 3 + HG_BLOCKS + jj - 1) * NC, ut * SPU + Q_SCAN + jj)
            columns(UT, HG_BLOCKS - UT, Q_REST)
            columns(3 * HG_BLOCKS, HG_BLOCKS, Q_HEADS)
            columns(GATE_BLOCK, GATES, Q_HEADS + HG_BLOCKS)
            for p in range(2):
                for s in range(2):
                    for j in range(4):
                        load(j, w_glu[s], 0, (4 * p + j) * NC, 4 * (Q_GLU + 2 * p + s) + j)
            passes(w_proj, 0, HG // (KT * P), Q_PROJ)
            passes(w_out, 0, D // (KT * P), Q_OUT)
            ffn(*ffn2, Q_FFN2)
            for c in range(DT // 2):
                by_pool = sum(k <= c for k in POOL_PAIRS)
                if c in POOL_PAIRS:
                    sp.wait_ge(y_pool, by_pool)
                else:
                    sp.wait_ge(y_final, c + 1 - by_pool)
                sp.dma_start(outT.rearrange("(k p) t -> p k t", p=P)[:, 2 * c:2 * c + 2, :],
                             h[:, 2 * c:2 * c + 2, META:T]).then_inc(stored[c % 4], 16)
            for c in range(4):
                sp.wait_ge(stored[c], 32)

        @block.tensor
        def _(pe):
            pe.sem_inc(unit_done, RING)
            pe.sem_inc(cx_done, 1)

            def unit(j, u, banks, n, rhs, start, stop, need=None, wide=False):
                pe.wait_ge(lo_ready, u + RING + 1)
                by_column = [(c, k) for c in range(2) for k in range(KT)]
                by_row = [(c, k) for k in range(KT) for c in range(2)]
                for c, k in by_column if need is None else by_row:
                    if need is not None and c == 0:
                        pe.wait_ge(x_ready, need + k + 1)
                    out = ps[:, banks + c, 0:n]
                    hi, lo = w_hi[:, j, k, c * P:(c + 1) * P], w_lo[:, j, k, c * P:(c + 1) * P]
                    x = rhs(k)
                    if wide:
                        pe.matmul(ps[:, banks + c, 0:2 * n].rearrange("p (s t) -> p s t", s=2), hi, x,
                                  start=start and k == 0, stop=False)
                    else:
                        pe.matmul(out, hi, x[:, 0, :], start=start and k == 0, stop=False)
                        pe.matmul(out, hi, x[:, 1, :], start=False, stop=False)
                    last = pe.matmul(out, lo, x[:, 0, :], start=False, stop=stop and k == KT - 1)
                last.then_inc(unit_done, 1)

            def keep_warm(n, bank):
                for _ in range(n):
                    pe.matmul(ps[:, bank, 0:P], ones[:, :], ident[:, :], start=True, stop=True)

            def rows(parts, first, c0, n):
                return lambda k: parts[:, first + k, :, c0:c0 + n]

            def column_block(q, banks, c0, x_need, between=None, fresh=False, wide=False):
                for j in range(4):
                    if j or not fresh:
                        pe.wait_ge(x_ready, x_need + 4 * j + 4)
                    unit(j, 4 * q + j, banks, T - c0, rows(xs, 4 * j, c0, T - c0), j == 0, j == 3,
                         None if j or not fresh else x_need, wide)
                    if between:
                        between(j)

            def one_pass(index, q, groups, parts, c0, n, need, free=None, wide=False):
                def quad(g, start, stop):
                    need(g)
                    for j in range(4):
                        if start and free:
                            free(j)
                        if start and index:
                            pe.wait_ge(pair_out, 4 * (index - 1) + j + 1)
                        def rhs(k):
                            if isinstance(g, int):
                                return parts[:, 4 * g + k, :, c0:c0 + n]
                            return parts[:, ds(g * 4 + k, 1), :, c0:c0 + n].rearrange("p a s t -> p (a s) t")
                        unit(j, (g + q) * 4 + j, 2 * j, n, rhs, start, stop, wide=wide)
                quad(0, True, groups == 1)
                if groups > 2:
                    with pe.Fori(1, groups - 1) as g:
                        quad(g, False, False)
                if groups > 1:
                    quad(groups - 1, False, True)

            def norm(index, c0):
                if index:
                    pe.wait_ge(pair_out, 4 * PASSES_BEFORE[index] + (0 if NORM_BANK[index] else -3))
                pe.wait_ge(summed, 6 * index + 6)
                for c in range(2):
                    pe.matmul(ps[:, NORM_BANK[index], 0:T - c0], ones[:, :], scr[:, 4 + c, c0:T], start=c == 0, stop=False)
                pe.wait_ge(sq_ready, 8 * index + 8)
                for c in range(2):
                    last = pe.matmul(ps[:, NORM_BANK[index], 0:T - c0], ones[:, :], scr[:, 2 + c, c0:T], start=False,
                                     stop=c == 1)
                last.then_inc(sq_used, 1)

            def ffn(f, c0, q):
                first, index = 0, f * PASS_FFN2
                for blocks in HALVES:
                    done = f * FF_BLOCKS + first
                    if index:
                        pe.wait_ge(pair_out, 4 * index - 2)

                    def block(b, mean=False):
                        pe.wait_ge(gated, b + done + 1)
                        column_block(b * 2 + q, 0, c0, f * 2 * DT, fresh=mean, wide=f == 1)
                        if mean:
                            norm(2 * f, c0)
                        pe.wait_ge(hidden, b + done + 1)
                        column_block(b * 2 + q + 1, 2, c0, f * 2 * DT, wide=f == 1)
                    peeled = 0 if first else 1
                    if peeled:
                        block(0, True)
                    with pe.Fori(peeled, blocks) as b:
                        block(b)
                    q += 2 * blocks
                    for p in range(2):
                        def free(j):
                            if j < 2:
                                pe.wait_ge((gated, hidden)[j], 1 + done + blocks)
                        one_pass(index, q, blocks // 2, hs, c0, T - c0,
                                 lambda g: pe.wait_ge(h_ready, g * 2 + done + 2), None if p else free, f == 1)
                        q += blocks // 2
                        index += 1
                    first += blocks

            pe.wait_ge(consts, 2)
            keep_warm(14, 0)
            ffn(0, 0, 0)
            norm(1, 0)
            pe.wait_ge(pair_out, 4 * PASS_GLU)
            pe.wait_ge(bbar_ready, 1)
            for ut in range(UT):
                for r in range(2):
                    last = pe.transpose(ps[:, 4 + r, ut * P:(ut + 1) * P],
                                        bd[:, r, SPU * ut:SPU * (ut + 1), :].rearrange("p a b -> p (a b)"), ident[:, :])
            last.then_inc(bt_psum, 1)
            keep_warm(14, 2)
            pe.wait_ge(root_ready, 2)
            for m in range(2):
                column_block(Q_U + m, 2 * m, 0, DT, fresh=m == 0)
            pe.wait_ge(block_out, 2)
            with pe.Fori(0, UT) as ut:
                def project_in(jj, turn):
                    for r in range(2):
                        last = pe.matmul(ps[:, 4 + r, 0:T], st_b[32 * jj:32 * jj + 32, r, :], st_u[32 * jj:32 * jj + 32, :],
                                         start=True, stop=True)
                    last.then_inc(bu_done, 1)
                for jj in range(SPU):
                    pe.wait_ge(block_out, ut * SPU + jj + 1)

                    def between(j, jj=jj):
                        if j == 0 and jj == 0:
                            pe.wait_ge(staged, ut + 1)
                            pe.wait_ge(bu_taken, ut * SPU + 1)
                            project_in(0, ut)
                        if j == 2 and jj < SPU - 1:
                            pe.wait_ge(bu_taken, ut * SPU + jj + 2)
                            project_in(jj + 1, ut)
                    column_block(ut * SPU + Q_SCAN + jj, 2 * (jj % 2), 0 if jj else META, DT, between)
                    pe.wait_ge(scanned, ut * SPU + jj + 1)
                    if jj == 0:
                        pe.wait_ge(ys_done, ut + 1)
                    for r in range(2):
                        last = pe.matmul(ps[32 * jj:32 * jj + 32, 6, 0:SEQ], st_c[:, jj, r, :], sx[:, r, META:T],
                                         start=r == 0, stop=r == 1)
                    last.then_inc(cx_done, 1)
            for m in (18, 19):
                pe.wait_ge(block_out, m - 1)
                column_block(Q_U + m, 2 * (m % 2), META, DT)
            pe.wait_ge(block_out, M_HEADS - 1)
            keep_warm(10, 0)
            pe.wait_ge(block_out, M_HEADS)
            pe.wait_ge(ys_done, UT + 1)

            def score(hd):
                pe.wait_ge(levels, hd + 1)
                pe.wait_ge(v_staged, hd + 1)
                for b in range(2):
                    pe.transpose(ps[:, 2, b * P:(b + 1) * P], scr[:, 2, META + b * P:META + (b + 1) * P], ident[:, :])
                pe.transpose(ps[0:META, 2, 2 * P:3 * P], scr[:, 2, 0:META], ident[:, :])
                blk = [slice(META + b * P, META + (b + 1) * P) for b in range(2)]
                pe.matmul(ps[:, 3, 0:P], ks[:, 7, blk[0]], qs[:, 8, P:2 * P], start=True, stop=True)
                pe.matmul(ps[0:META, 3, P:2 * P], ks[:, 4, 0:META], qs[:, 8, 0:P], start=True, stop=True)
                pe.matmul(ps[0:META, 3, 2 * P:3 * P], ks[:, 5, 0:META], qs[:, 8, P:2 * P], start=True, stop=True)
                for b in range(2):
                    for l in range(SLOTS):
                        if b and l == 4:
                            pe.wait_ge(ot_done, hd + 1)
                        k = max(l - 1, 0)
                        out = ps[:, 4 + 2 * b + l // 4, (l % 4) * P:(l % 4 + 1) * P]
                        queries = qs[:, l, b * P:(b + 1) * P]
                        if l:
                            out, queries = [a.rearrange("p (b s m) -> p b s m", s=2, m=1 << (l - 1))[:, :, 1, :]
                                            for a in (out, queries)]
                        pe.matmul(out, ks[:, k, blk[b]], queries, start=True, stop=True)
                    for l in range(SLOTS, LEVELS):
                        m = 1 << (l - 1)
                        for t in range(0, P, 2 * m):
                            last = pe.matmul(ps[t:t + m, 5 + 2 * b, P + t + m:P + t + 2 * m],
                                             ks[:, l - 1, META + b * P + t:META + b * P + t + m],
                                             qs[:, l, b * P + t + m:b * P + t + 2 * m], start=True, stop=True)
                last.then_inc(scored, 1)

            def mix(hd):
                pe.wait_ge(att_ready, hd + 1)
                pe.wait_ge(v_ready, hd + 1)
                pe.matmul(ps[:, 2, 0:P], att[:, 0, :], v_tok[:, 0, :], start=True, stop=False)
                pe.matmul(ps[:, 2, 0:P], att_m[0:META, 0, :], v_meta[0:META, :], start=False, stop=True)
                pe.matmul(ps[:, 2, P:2 * P], att[:, 1, :], v_tok[:, 1, :], start=True, stop=False)
                pe.matmul(ps[:, 2, P:2 * P], att[:, 2, :], v_tok[:, 0, :], start=False, stop=False)
                pe.matmul(ps[:, 2, P:2 * P], att_m[0:META, 1, :], v_meta[0:META, :], start=False, stop=True)\
                    .then_inc(o_done, 1)

            def back(hd):
                pe.wait_ge(on_ready, hd + 1)
                for b in range(2):
                    last = pe.transpose(ps[:, 7, b * P:(b + 1) * P], scr[:, 4, b * P:(b + 1) * P], ident[:, :])
                last.then_inc(ot_psum, 1)

            def head(hd):
                score(hd)
                pe.wait_ge(block_out, hd + M_HEADS)
                column_block(hd + Q_HEADS, 0, META, DT, lambda j: mix(hd) if j == 1 else None)
                back(hd)

            with pe.Fori(0, HEADS) as hd:
                head(hd)
            with pe.Fori(0, GB // 2) as i:
                for c in range(2):
                    pe.wait_ge(block_out, i * 2 + M_GATES + c - 1)
                    column_block(i * 2 + Q_GATES + c, 2 - 2 * c, META, DT)
            pe.wait_ge(block_out, M_GATES + GB)
            for index in range(PASS_GLU, PASS_PROJ):
                one_pass(index, Q_GLU + index - PASS_GLU, 1, zs, 0, SEQ, lambda g: pe.wait_ge(z_ready, 1))
            for p in range(2):
                one_pass(PASS_PROJ + p, Q_PROJ + 3 * p, 3, os, 0, SEQ, lambda g: pe.wait_ge(o_ready, 4))
            for p in range(2):
                one_pass(PASS_OUT + p, Q_OUT + 4 * p, 4, xs, META, SEQ, lambda g: pe.wait_ge(m_ready, g * 2 + 2))
            ffn(1, META, Q_FFN2)
            norm(3, META)

        @block.scalar
        def _(act):
            act.sem_inc(ot_done, 1)
            act.dma_start(gain[:, :, :], gains).then_inc(small_in[0], 16)

            def split(q, j):
                slot = (j + LEAD) % 4
                if isinstance(q, int) and 4 * q + j + LEAD >= UNITS:
                    return
                q1 = q + (j + LEAD) // 4
                act.wait_ge(raw_ready[slot], q1 * 16 + 16)
                act.wait_ge(unit_done, q * 4 + j + LEAD + 1)
                act.activation(w_hi[:, slot, :, :], raw[:, slot, :, :], ACT.Copy).then_inc(hi_ready, 1)

            def square(index, c0, k):
                if index:
                    act.wait_ge(pair_out, 4 * (PASSES_BEFORE[index] - 2) + k + 1)
                if k >= 3:
                    act.wait_ge(summed, 6 * index + k - 2)
                at_k = 2 * (k % 2) if k else 4
                act.activation(scr[:, at_k:at_k + 2, c0:T], h[:, 2 * k:2 * k + 2, c0:T], ACT.Square).then_inc(sq_ready, 1)

            def root(index, c0):
                act.wait_ge(sq_used, index + 1)
                act.activation(scr[:, 4, c0:T], ps[:, NORM_BANK[index], 0:T - c0], ACT.Sqrt, bias=small[:, 1:2])\
                    .then_inc(root_ready, 1)

            def load_sqrt():
                act.activation(spare[:, :], small[:, 0:1], ACT.Sqrt)

            def upper(index, c0, k):
                act.activation(x_hi[:, k, c0:T], h[:, k, c0:T], ACT.Copy, scale=gain[:, index, k:k + 1])\
                    .then_inc(xhi_ready, 1)

            def plain_pass(q, groups, after=None, beside=None):
                if groups > 1:
                    with act.Fori(0, groups - 1) as g:
                        for j in range(4):
                            split(g + q, j)
                for j in range(4):
                    split(q + groups - 1, j)
                    if j and after:
                        after(j - 1)
                    if beside:
                        beside(j)
                if after:
                    after(3)

            def last_gain(k):
                act.wait_ge(sq_ready, 8 * 3 + k + 1)
                for t in (2 * k, 2 * k + 1):
                    ins = act.activation(h[:, t, META:T], h[:, t, META:T], ACT.Copy, scale=gain[:, 3, t:t + 1])
                ins.then_inc(gained, 1)

            def ffn(f, c0, q, between=None):
                first = 0
                for blocks in HALVES:
                    done = f * FF_BLOCKS + first

                    def block(b, mean=False):
                        for j in range(1 if mean and not f else 0, 4):
                            split(b * 2 + q, j)
                        if mean:
                            root(2 * f, c0)
                        split(b * 2 + q + 1, 0)
                        act.wait_ge(gated, b + done + 2)
                        act.activation(scr[:, 2:4, c0:T], scr[:, 0:2, c0:T], ACT.Sigmoid).then_inc(sig_ready, 1)
                        for j in range(1, 4):
                            split(b * 2 + q + 1, j)
                        act.wait_ge(hidden, b + done + 2)
                        act.activation(h_hi[:, ds(b * 2, 2), c0:T], scr[:, 2:4, c0:T], ACT.Copy).then_inc(hhi_ready, 1)
                    peeled = 0 if first else 1
                    if peeled:
                        block(0, True)
                    with act.Fori(peeled, blocks) as b:
                        block(b)
                    q += 2 * blocks
                    if between and not first:
                        between(0)
                    for p in range(2):
                        def after(j, p=p):
                            k = 4 * p + j
                            if k == 7:
                                load_sqrt()
                            square(1 + 2 * f, c0, k)
                            if f and k:
                                last_gain(k - 1)
                        plain_pass(q, blocks // 2, after if first else None)
                        q += blocks // 2
                        if between and not first:
                            between(1 + p)
                    first += blocks

            def head_inputs(hd):
                def tile(t):
                    return qfv[:, ds(hd + t, 1), :].rearrange("p a t -> p (a t)")
                act.activation(scr[:, 1, :], tile(HEADS), ACT.Sigmoid).then_inc(f_sig, 1)
                act.activation(scr[:, 0, 0:SEQ], tile(0)[:, META:T], ACT.Sigmoid)
                act.wait_ge(f_sig, hd + 1)
                act.activation(fm[:, 0:T], scr[:, 1, :], ACT.Identity, scale=lb[:, 1, ds(hd, 1)],
                               bias=lb[:, 0, ds(hd, 1)]).then_inc(f_made, 1)
                act.activation(scr[:, 2, :], tile(2 * HEADS), ACT.Copy).then_inc(v_staged, 1)
                act.wait_ge(f_made, hd + 1)
                act.activation(ks[:, 0, :], fm[:, 0:T], ACT.Identity, scale=-1.0, bias=small[:, 3:4]).then_inc(head_in, 1)

            def parameters(stage):
                if stage == 0:
                    act.wait_ge(small_in[1], 16)
                    act.activation(sv[:, 3, :], sv[:, 2, :], ACT.Exp).then_inc(sv_act, 1)
                    act.wait_ge(dve_step, 4)
                    act.activation(lbt[:, 0:2, :], lbt[:, 0:2, :], ACT.Exp).then_inc(lb_exp, 1)
                elif stage == 1:
                    act.wait_ge(sv_pool, 1)
                    act.activation(mag[:, :], sv[:, 4, :], ACT.Exp).then_inc(sv_act, 1)
                else:
                    act.wait_ge(sv_pool, 2)
                    act.activation(sv[:, 10:12, :], sv[:, 8:10, :], ACT.Sin).then_inc(sv_act, 1)

            act.wait_ge(consts, 2)
            act.activation(spare[:, :], small[:, 0:1], ACT.Copy)
            act.wait_ge(meta_in, 16)
            act.wait_ge(small_in[0], 16)
            for c in range(4):
                act.wait_ge(x_in[c], 16)
                for k in range(4 * c, 4 * c + 4):
                    upper(0, 0, k)
                if c < LEAD:
                    act.wait_ge(raw_ready[c], 16)
                    act.activation(w_hi[:, c, :, :], raw[:, c, :, :], ACT.Copy).then_inc(hi_ready, 1)
                else:
                    split(0, 0)
                if c < 2:
                    square(0, 0, 2 * c)
                    square(0, 0, 2 * c + 1)
            act.dma_start(sv[:, 0:3, :], s5v).then_inc(small_in[1], 16)
            act.dma_start(lb[:, :, :], hg_lb).then_inc(small_in[2], 16)
            act.dma_start(hgn[:, :], hg_norm).then_inc(small_in[3], 16)
            act.dma_start(dsk[:, :], s5d).then_inc(small_in[4], 16)
            act.dma_start(btmp[:, 0:2 * ST * GP].rearrange("p (r j c) -> p r j c", r=2, j=ST), s5b).then_inc(small_in[5], 16)
            for k in range(4, DT // 2):
                square(0, 0, k)
            for g in range(2):
                act.dma_start(cd[64 * g:64 * g + 64, :, :, g * GP:(g + 1) * GP], s5c[64 * g:64 * g + 64])\
                    .then_inc(small_in[6 + g], 16)
            ffn(0, 0, 0, parameters)
            root(1, 0)
            for k in range(DT):
                act.wait_ge(xf_dve if k < 2 else xf_pool, k + 1 if k < 2 else k - 1)
                act.activation(x_hi[:, k, :], scr[:, k % 4, :], ACT.Copy, scale=gain[:, 1, k:k + 1]).then_inc(xhi_ready, 1)
                if k % 4 == 3 and k > 3:
                    split(Q_U, k // 4 - 1)
            act.wait_ge(bt_psum, 1)
            for r in range(2):
                ins = act.activation(bt[:, :, r, :], ps[:, 4 + r, :].rearrange("p (u s) -> p u s", u=UT), ACT.Copy)
            ins.then_inc(bt_out, 1)

            def take_block(m, out, banks, n, func):
                act.wait_ge(unit_done, (m + Q_U) * 4 + RING + 4)
                act.activation(out, ps[:, banks:banks + 2, 0:n], func).then_inc(block_out, 1)

            for m in range(2):
                for j in range(0 if m else 3, 4):
                    split(Q_U + m, j)
                take_block(m, u5[:, 2 * m:2 * m + 2, :], 2 * m, T, ACT.Copy)
            act.wait_ge(tables, 1)
            act.wait_ge(bt_out, 1)
            with act.Fori(0, UT) as ut:
                act.wait_ge(block_out, 2)
                act.wait_ge(cx_done, ut * SPU + 1)
                act.activation(st_u[:, :], u5[:, ds(ut, 1), :].rearrange("p a t -> p (a t)"), ACT.Copy)
                act.activation(st_b[:, :, :], bt[:, ds(ut, 1), :, :].rearrange("p a r s -> p (a r) s"), ACT.Copy)
                act.activation(st_c[:, :, :, :], cd[:, ds(ut * SPU, SPU), :, :], ACT.Copy).then_inc(staged, 1)
                for jj in range(SPU):
                    for j in range(4):
                        split(ut * SPU + Q_SCAN + jj, j)
                    if jj:
                        take_block(ut * SPU + 2 + jj, qfv[:, ds(ut * 6 + HEADS + 2 * jj - 2, 2), :], 2 * (jj % 2), T, ACT.Copy)
                    else:
                        take_block(ut * SPU + 2, qfv[:, ds(ut * 2, 2), META:T], 0, SEQ, ACT.Copy)
            for m in (18, 19):
                for j in range(4):
                    split(Q_U + m, j)
                    if m == 18 and j == 1:
                        act.wait_ge(z_arg, 1)
                        act.activation(scr[:, 0:4, 0:SEQ], scr[:, 0:4, 0:SEQ], ACT.Sigmoid, scale=GELU_B).then_inc(z_sig, 1)
                    if m == 18 and j == 3:
                        act.wait_ge(z_val, 1)
                        act.activation(z_hi[:, :, :], ys[:, :, :], ACT.Copy).then_inc(zhi_ready, 1)
                    if m == 19 and j == 0:
                        act.wait_ge(z_ready, 1)
                        act.wait_ge(dve_step, 8)
                        head_inputs(0)
                take_block(m, qfv[:, 2 * m - 28:2 * m - 26, META:T], 2 * (m % 2), SEQ, ACT.Copy)

            def beside_head(hd, out, func, following):
                act.wait_ge(scored, hd + 1)
                act.activation(v_tok[:, :, :], ps[:, 2, 0:2 * P].rearrange("p (b v) -> p b v", b=2), ACT.Copy)
                act.activation(v_meta[:, :], ps[0:META, 2, 2 * P:3 * P], ACT.Copy)
                act.activation(att[:, 2, :], ps[:, 3, 0:P], ACT.Copy)
                act.activation(att_m[:, :, :], ps[0:META, 3, P:3 * P].rearrange("p (b v) -> p b v", b=2), ACT.Copy)\
                    .then_inc(v_ready, 1)
                if following:
                    act.wait_ge(levels, hd + 1)
                    head_inputs(hd + 1)
                split(hd + Q_HEADS, 1)
                act.wait_ge(o_done, hd + 1)
                for b in range(2):
                    ins = act.activation(scr[:, 3, b * P:(b + 1) * P], ps[:, 2, b * P:(b + 1) * P], ACT.Square,
                                         accum_out=ss[:, 0, b:b + 1])
                ins.then_inc(ss_ready, 1)
                split(hd + Q_HEADS, 2)
                act.wait_ge(rr_ready, hd + 1)
                for b in range(2):
                    ins = act.activation(scr[:, 4, b * P:(b + 1) * P], ps[:, 2, b * P:(b + 1) * P], ACT.Copy,
                                         scale=ss[:, 1, b:b + 1])
                ins.then_inc(on_ready, 1)
                split(hd + Q_HEADS, 3)
                take_block(hd + M_HEADS, out, 0, SEQ, func)
                act.wait_ge(ot_psum, hd + 1)
                act.activation(qfv[:, ds(hd, 1), META:T].rearrange("p a t -> p (a t)"), ps[:, 7, 0:SEQ], ACT.Copy,
                               scale=hgn[:, ds(hd, 1)]).then_inc(ot_done, 1)
                if following:
                    split(hd + Q_HEADS + 1, 0)

            split(Q_HEADS, 0)
            act.wait_ge(small_in[3], 16)
            with act.Fori(0, HG_BLOCKS) as hd:
                beside_head(hd, gout[:, ds(hd * 2, 2), :], ACT.Copy, True)
            with act.Fori(HG_BLOCKS, HEADS - 1) as hd:
                beside_head(hd, gates_a[:, ds(hd * 2 - HEADS, 2), :], ACT.Sigmoid, True)
            beside_head(HEADS - 1, gates_a[:, HEADS - 2:HEADS, :], ACT.Sigmoid, False)

            def gate_pair(i, c, side=None):
                for j in range(4):
                    split(i * 2 + Q_GATES + c, j)
                    if side:
                        side(j)
                take_block(i * 2 + M_GATES + c, gates_b[:, ds(i * 4 + 2 * c, 2), :], 2 - 2 * c, SEQ, ACT.Sigmoid)

            act.wait_ge(ot_done, HEADS + 1)
            with act.Fori(0, 4) as i:
                def side(j):
                    if j == 0:
                        act.activation(sgs[:, :, :], gout[:, ds(i * 3, 3), :], ACT.Sigmoid).then_inc(sgo_ready, 1)
                    if j == 3:
                        act.wait_ge(og_ready, i + 1)
                        act.activation(o_hi[:, ds(i * 3, 3), :], gout[:, ds(i * 3, 3), :], ACT.Copy).then_inc(ohi_ready, 1)
                gate_pair(i, 0, side)
                gate_pair(i, 1)
            gate_pair(4, 0)
            gate_pair(4, 1)

            for index in range(PASS_GLU, PASS_PROJ):
                q = Q_GLU + index - PASS_GLU

                def glu_gate(j, index=index):
                    act.wait_ge(unit_done, 4 * (Q_GLU + index - PASS_GLU) + RING + j + 1)
                    act.activation(ps[:, 2 * j:2 * j + 2, 0:SEQ], ps[:, 2 * j:2 * j + 2, 0:SEQ], ACT.Sigmoid)\
                        .then_inc(glu_sig, 1)
                plain_pass(q, 1, glu_gate if index % 2 else None)
            for p in range(2):
                def take_merged(j, p=p):
                    act.wait_ge(merged, 4 * p + j + 1)
                    act.activation(x_hi[:, 8 * p + 2 * j:8 * p + 2 * j + 2, META:T], ybuf[p][:, 2 * j:2 * j + 2, :],
                                   ACT.Copy).then_inc(mhi_ready, 1)
                plain_pass(Q_PROJ + 3 * p, 3, take_merged)
            def next_x(j):
                if j == 0:
                    act.wait_ge(pair_out, 4 * (PASS_OUT + 1))
                    act.wait_ge(unit_done, 4 * (Q_OUT + 6) + RING)
                for k in (2 * j, 2 * j + 1):
                    upper(2, META, k)
            for p in range(2):
                plain_pass(Q_OUT + 4 * p, 4, lambda j, p=p: square(2, META, 4 * p + j), next_x if p else None)
            act.wait_ge(unit_done, 4 * Q_FFN2 + RING)
            for k in range(DT // 2, DT):
                upper(2, META, k)
            ffn(1, META, Q_FFN2)
            root(3, META)
            last_gain(7)


        @block.vector
        def _(dve):
            step = Tally(dve, dve_step)
            tt, ts, stt = dve.tensor_tensor, dve.tensor_scalar, dve.scalar_tensor_tensor
            dve.sem_inc(lo_ready, RING)
            for credit in (gated, hidden, bu_taken, ys_done):
                dve.sem_inc(credit, 1)

            def split(q, j):
                slot = (j + LEAD) % 4
                if isinstance(q, int) and 4 * q + j + LEAD >= UNITS:
                    return
                dve.wait_ge(hi_ready, q * 4 + j + LEAD + 1)
                tt(w_lo[:, slot, :, :], raw[:, slot, :, :], w_hi[:, slot, :, :].bitcast(f32), SUB).then_inc(lo_ready, 1)

            def settle(q, j):
                dve.wait_ge(lo_ready, q * 4 + j + LEAD + 1 + RING)

            def root_inverse(index, c0):
                dve.wait_ge(root_ready, index + 1)
                dve.reciprocal(scr[:, 5, c0:T], scr[:, 4, c0:T]).then_inc(rms_inv, 1)

            def lower(index, c0, k):
                dve.wait_ge(xhi_ready, index * DT + k + 1)
                stt(x_lo[:, k, c0:T], h[:, k, c0:T], gain[:, index, k:k + 1], x_hi[:, k, c0:T].bitcast(f32), MUL, SUB)\
                    .then_inc(x_ready, 1)

            def add_squares(index, c0, k):
                dve.wait_ge(sq_ready, 8 * index + k + 1)
                if k > 1:
                    dve.wait_ge(summed, 6 * index + k - 1)
                at_k = 2 * (k % 2)
                tt(scr[:, 4:6, c0:T], scr[:, 4:6, c0:T], scr[:, at_k:at_k + 2, c0:T], ADD).then_inc(summed, 1)

            def plain_pass(q, groups, take, before=None, beside=None):
                if groups > 1:
                    with dve.Fori(0, groups - 1) as g:
                        for j in range(4):
                            split(g + q, j)
                for j in range(5):
                    if j:
                        if before:
                            before(j - 1)
                        dve.wait_ge(unit_done, 4 * (q + groups - 1) + RING + j)
                        take(j - 1)
                    if j < 4:
                        split(q + groups - 1, j)
                        if beside:
                            beside(j)

            def ffn(f, c0, q, between=None):
                first = 0
                inverse = scr[:, 5:6, c0:T].broadcast_to([P, 2, T - c0])
                gate, sig = scr[:, 0:2, c0:T], scr[:, 2:4, c0:T]
                for blocks in HALVES:
                    done = f * FF_BLOCKS + first

                    def block(b, mean=False):
                        for j in range(1 if mean and not f else 0, 4):
                            split(b * 2 + q, j)
                        if mean:
                            root_inverse(2 * f, c0)
                            dve.wait_ge(rms_inv, 2 * f + 1)
                        dve.wait_ge(unit_done, b * 8 + RING + 4 * q + 4)
                        if f:
                            tt(gate, ps[:, 0:2, 0:SEQ], inverse, MUL)
                            tt(sig, ps[:, 0:2, SEQ:], inverse, MUL).then_inc(halves, 1)
                            dve.wait_ge(halves, b * 2 + 2 * first + 1)
                            tt(gate, gate, sig, ADD).then_inc(gated, 1)
                        else:
                            tt(gate, ps[:, 0:2, 0:T], inverse, MUL).then_inc(gated, 1)
                        split(b * 2 + q + 1, 0)
                        dve.wait_ge(sig_ready, b + done + 1)
                        tt(gate, gate, sig, MUL).then_inc(silu, 1)
                        split(b * 2 + q + 1, 1)
                        dve.wait_ge(silu, b * 2 + 2 * done + 1)
                        tt(gate, gate, inverse, MUL).then_inc(silu, 1)
                        split(b * 2 + q + 1, 2)
                        split(b * 2 + q + 1, 3)
                        dve.wait_ge(silu, b * 2 + 2 * done + 2)
                        dve.wait_ge(unit_done, b * 8 + RING + 4 * q + 8)
                        if f:
                            tt(sig, ps[:, 2:4, 0:SEQ], gate, MUL)
                            tt(gate, ps[:, 2:4, SEQ:], gate, MUL).then_inc(halves, 1)
                            dve.wait_ge(halves, b * 2 + 2 * first + 2)
                            tt(sig, sig, gate, ADD).then_inc(hidden, 1)
                        else:
                            tt(sig, ps[:, 2:4, 0:T], gate, MUL).then_inc(hidden, 1)
                        dve.wait_ge(hhi_ready, b + done + 1)
                        tt(h_lo[:, ds(b * 2, 2), c0:T], sig, h_hi[:, ds(b * 2, 2), c0:T].bitcast(f32), SUB)\
                            .then_inc(h_ready, 1)
                    peeled = 0 if first else 1
                    if peeled:
                        block(0, True)
                    with dve.Fori(peeled, blocks) as b:
                        block(b)
                    q += 2 * blocks
                    for p in range(2):
                        def residual(j, p=p):
                            rows = slice(8 * p + 2 * j, 8 * p + 2 * j + 2)
                            if f:
                                step(stt(h[:, rows, c0:T], ps[:, 2 * j:2 * j + 2, SEQ:], 0.5, h[:, rows, c0:T], MUL, ADD))
                                step.join()
                            stt(h[:, rows, c0:T], ps[:, 2 * j:2 * j + 2, 0:T - c0], 0.5, h[:, rows, c0:T], MUL, ADD)\
                                .then_inc(pair_out, 1)
                        if first:
                            dve.wait_ge(pair_out, 4 * (f * PASS_FFN2 + p + 1))

                        def add(j, p=p):
                            if 4 * p + j >= 2:
                                add_squares(1 + 2 * f, c0, 4 * p + j - 1)
                        plain_pass(q, blocks // 2, residual, add if first else None)
                        q += blocks // 2
                        if between and not first:
                            between(1 + p)
                    first += blocks

            step(dve.memset(ps[:, 4:8, T:], 0.0))

            def parameters(stage):
                if stage == 1:
                    dve.wait_ge(lb_exp, 1)
                    step(tt(lbt[:, 2, :], lbt[:, 0, :], lbt[:, 1, :], ADD))
                    step.join()
                    step(dve.reciprocal(lbt[:, 1, :], lbt[:, 2, :]))
                    step.join()
                    step(tt(lb[:, 0, :], lbt[:, 0, :], lbt[:, 1, :], MUL))
                    step.join()
                    step(ts(lb[:, 1, :], lb[:, 0, :], -1.0, 1.0, MUL, ADD))
                if stage == 2:
                    dve.wait_ge(sv_pool, 3)
                    dve.reciprocal(sv[:, 13, :], sv[:, 12, :]).then_inc(den_inv, 1)

            dve.wait_ge(small_in[0], 16)
            for c in range(4):
                for k in range(4 * c, 4 * c + 4):
                    lower(0, 0, k)
                if c < LEAD:
                    dve.wait_ge(hi_ready, c + 1)
                    tt(w_lo[:, c, :, :], raw[:, c, :, :], w_hi[:, c, :, :].bitcast(f32), SUB).then_inc(lo_ready, 1)
                else:
                    split(0, 0)
                if c < 2:
                    for k in (2 * c, 2 * c + 1):
                        if k:
                            add_squares(0, 0, k)
            for k in range(4, 7):
                add_squares(0, 0, k)
            dve.wait_ge(small_in[2], 16)
            step(tt(lbt[:, 2, :], lb[:, 0, :], lb[:, 1, :], ALU.max))
            step.join()
            step(tt(lbt[:, 0, :], lb[:, 0, :], lbt[:, 2, :], SUB))
            step(tt(lbt[:, 1, :], lb[:, 1, :], lbt[:, 2, :], SUB))
            ffn(0, 0, 0, parameters)
            root_inverse(1, 0)
            dve.wait_ge(rms_inv, 2)
            for k in range(2):
                tt(scr[:, k, :], h[:, k, :], scr[:, 5, :], MUL).then_inc(xf_dve, 1)
            for k in range(DT):
                dve.wait_ge(xhi_ready, DT + k + 1)
                stt(x_lo[:, k, :], scr[:, k % 4, :], gain[:, 1, k:k + 1], x_hi[:, k, :].bitcast(f32), MUL, SUB)\
                    .then_inc(x_ready, 1)
                if k % 4 == 3 and k > 3:
                    split(Q_U, k // 4 - 1)
            split(Q_U, 3)
            for j in range(4):
                split(Q_U + 1, j)

            dve.wait_ge(tables, 1)
            dve.wait_ge(small_in[4], 16)
            with dve.Fori(0, UT) as ut:
                step.turn(ut, SPU * 12)
                for jj in range(SPU):
                    tile = ut * SPU + jj

                    def e(table, c0):
                        return table[:, ds(ut * SPU + jj, 1), c0:T].rearrange("p a t -> p (a t)")
                    split(tile + Q_SCAN, 0)
                    settle(tile + Q_SCAN, 0)
                    dve.wait_ge(bu_done, tile + 1)
                    step(tt(scr[:, 0, :], ps[:, 4, 0:T], e(e_re, 0), MUL))
                    step(tt(scr[:, 1, :], ps[:, 5, 0:T], e(e_im, 0), MUL))
                    step(tt(scr[:, 2, :], ps[:, 5, 0:T], e(e_re, 0), MUL))
                    tt(scr[:, 3, :], ps[:, 4, 0:T], e(e_im, 0), MUL).then_inc(bu_taken, 1)
                    split(tile + Q_SCAN, 1)
                    dve.wait_ge(bu_taken, tile + 2)
                    step(tt(scr[:, 0, :], scr[:, 0, :], scr[:, 1, :], ADD))
                    step(tt(scr[:, 2, :], scr[:, 2, :], scr[:, 3, :], SUB))
                    step.join()
                    decay = mag[:, ds(tile, 1)].broadcast_to([P, T])
                    step(dve.tensor_tensor_scan(scr[:, 1, :], decay, scr[:, 0, :], 0.0, MUL, ADD))
                    step(dve.tensor_tensor_scan(scr[:, 3, :], decay, scr[:, 2, :], 0.0, MUL, ADD))
                    step.join()
                    split(tile + Q_SCAN, 2)
                    step(tt(scr[:, 0, META:T], scr[:, 1, META:T], e(e_re, META), MUL))
                    step(tt(scr[:, 2, META:T], scr[:, 3, META:T], e(e_im, META), MUL))
                    step(tt(scr[:, 4, META:T], scr[:, 1, META:T], e(e_im, META), MUL))
                    step(tt(scr[:, 5, META:T], scr[:, 3, META:T], e(e_re, META), MUL))
                    step.join()
                    dve.wait_ge(cx_done, tile + 1)
                    step(tt(sx[:, 0, META:T], scr[:, 0, META:T], scr[:, 2, META:T], SUB))
                    tt(sx[:, 1, META:T], scr[:, 4, META:T], scr[:, 5, META:T], ADD).then_inc(scanned, 1)
                    split(tile + Q_SCAN, 3)
                dve.wait_ge(cx_done, ut * SPU + SPU + 1)
                stt(ys[:, ds(ut, 1), :].rearrange("p a t -> p (a t)"),
                    u5[:, ds(ut, 1), META:T].rearrange("p a t -> p (a t)"), dsk[:, ds(ut, 1)], ps[:, 6, 0:SEQ],
                    MUL, ADD).then_inc(ys_done, 1)
            step.done(UT)

            g = scr[:, 0:4, 0:SEQ]
            split(Q_REST, 0)
            dve.wait_ge(ys_done, UT + 1)
            step(tt(g, ys[:, :, :], ys[:, :, :], MUL))
            step.join()
            step(ts(g, g, GELU_A, 1.0, MUL, ADD))
            step.join()
            split(Q_REST, 1)
            tt(g, g, ys[:, :, :], MUL).then_inc(z_arg, 1)
            split(Q_REST, 2)
            dve.wait_ge(z_sig, 1)
            tt(ys[:, :, :], ys[:, :, :], g, MUL).then_inc(z_val, 1)
            split(Q_REST, 3)
            dve.wait_ge(z_val, 1)
            dve.wait_ge(zhi_ready, 1)
            tt(z_lo[:, :, :], ys[:, :, :], z_hi[:, :, :].bitcast(f32), SUB).then_inc(z_ready, 1)

            f_at = (0, 272, 408, 476, 510, 528, 536, 540)

            def level(i):
                m = 1 << i
                c0 = 0 if m < META else META
                n = T - c0
                k_old, k_new = [ks[:, i + d, c0:T].rearrange("p (b s m) -> p b s m", s=2, m=m) for d in range(2)]
                q_old, q_new = [qs[:, i + 1 + d, :].rearrange("p (b s m) -> p b s m", s=2, m=m) for d in range(2)]
                skip = META // m if m < META else (1 if m == META else 0)
                at_k = skip if m >= META else 0
                f_k = fm[:, f_at[i] + at_k:f_at[i] + at_k + n // m].rearrange("p (b s) -> p b s", s=2)
                f_q = fm[:, f_at[i] + skip:f_at[i] + skip + SEQ // m].rearrange("p (b s) -> p b s", s=2)

                def wide(f, nb):
                    return f.unsqueeze(2).broadcast_to([P, nb, m])
                step.join()
                step(tt(k_new[:, :, 0, :], k_old[:, :, 0, :], wide(f_k[:, :, 1], n // m // 2), MUL))
                step(tt(q_new[:, :, 1, :], q_old[:, :, 1, :], wide(f_q[:, :, 0], SEQ // m // 2), MUL))
                step(dve.tensor_copy(k_new[:, :, 1, :], k_old[:, :, 1, :]))
                step(dve.tensor_copy(q_new[:, :, 0, :], q_old[:, :, 0, :]))
                step(tt(fm[:, f_at[i + 1]:f_at[i + 1] + n // m // 2], f_k[:, :, 0], f_k[:, :, 1], MUL))

            def head_levels(hd, part):
                if part == 0:
                    dve.wait_ge(head_in, hd + 1)
                    step(stt(qs[:, 0, :], qfv[:, ds(hd, 1), META:T].rearrange("p a t -> p (a t)"), DK ** -0.5,
                             scr[:, 0, 0:SEQ], MUL, MUL))
                    step.join()
                    step(tt(qs[:, 1, :], qs[:, 0, :], fm[:, META:T], MUL))
                    for i in range(3):
                        level(i)
                else:
                    for i in range(3, 7):
                        level(i)
                    step.join()
                    ts(ks[:, 5, 0:META], ks[:, 4, 0:META], fm[:, f_at[7]:f_at[7] + 1], None, MUL).then_inc(levels, 1)

            split(Q_REST + 1, 0)
            head_levels(0, 0)
            split(Q_REST + 1, 1)
            head_levels(0, 1)
            split(Q_REST + 1, 2)
            split(Q_REST + 1, 3)
            dve.wait_ge(mask_ready, 1)

            def head(hd, following):
                def masked(b):
                    step(tt(prod[:, :, :],
                            ps[:, 4 + 2 * b:6 + 2 * b, :].rearrange("p b (l t) -> p (b l) t", l=4)[:, 0:SLOTS, :], mask[:, :, :], MUL))
                    step.join()
                    ins = dve.tensor_reduce(att[:, b, :], prod[:, :, :].rearrange("p l t -> p t l"), AX.X, ADD)
                    if b:
                        ins.then_inc(att_ready, 1)
                    else:
                        step(ins)
                dve.wait_ge(scored, hd + 1)
                masked(0)
                step.join()
                masked(1)
                if following:
                    head_levels(hd + 1, 0)
                    head_levels(hd + 1, 1)
                split(hd + Q_HEADS, 1)
                split(hd + Q_HEADS, 2)
                split(hd + Q_HEADS, 3)
                if following:
                    split(hd + Q_HEADS + 1, 0)

            split(Q_HEADS, 0)
            with dve.Fori(0, HEADS - 1) as hd:
                step.turn(hd, 40)
                head(hd, True)
            step.done(HEADS - 1)
            head(HEADS - 1, False)

            dve.wait_ge(ot_done, HEADS + 1)
            with dve.Fori(0, 4) as i:
                step.turn(i, 1)
                g3 = gout[:, ds(i * 3, 3), :]
                split(i * 2 + Q_GATES, 0)
                dve.wait_ge(sgo_ready, i + 1)
                step(tt(g3, g3, sgs[:, :, :], MUL))
                split(i * 2 + Q_GATES, 1)
                step.join()
                tt(g3, g3, qfv[:, ds(i * 3, 3), META:T], MUL).then_inc(og_ready, 1)
                split(i * 2 + Q_GATES, 2)
                split(i * 2 + Q_GATES, 3)
                split(i * 2 + Q_GATES + 1, 0)
                dve.wait_ge(og_ready, i + 1)
                dve.wait_ge(ohi_ready, i + 1)
                tt(o_lo[:, ds(i * 3, 3), :], g3, o_hi[:, ds(i * 3, 3), :].bitcast(f32), SUB).then_inc(o_ready, 1)
                for j in range(1, 4):
                    split(i * 2 + Q_GATES + 1, j)
            step.done(4)
            for c in range(2):
                for j in range(4):
                    split(Q_GATES + 8 + c, j)

            dve.wait_ge(block_out, M_GATES + GB)
            for index in range(PASS_GLU, PASS_PROJ):
                p = (index - PASS_GLU) // 2
                y = ybuf[p]

                def take_a(j, y=y):
                    dve.tensor_copy(y[:, 2 * j:2 * j + 2, :], ps[:, 2 * j:2 * j + 2, 0:SEQ]).then_inc(pair_out, 1)

                def take_b(j, y=y, p=p):
                    dve.wait_ge(glu_sig, 4 * p + j + 1)
                    yy = y[:, 2 * j:2 * j + 2, :]
                    tt(yy, ps[:, 2 * j:2 * j + 2, 0:SEQ], yy, MUL).then_inc(pair_out, 1)
                    dve.wait_ge(pair_out, 4 * (PASS_GLU + 2 * p + 1) + j + 1)
                    t = DT + 8 * p + 2 * j - 2 * GA
                    step(tt(yy, yy, gates_b[:, t:t + 2, :], MUL))
                if index % 2:
                    dve.wait_ge(pair_out, 4 * index)
                plain_pass(Q_GLU + index - PASS_GLU, 1, take_b if index % 2 else take_a)
            step.join()
            for p in range(2):
                def take_proj(j, p=p):
                    t = 8 * p + 2 * j
                    gate = gates_a[:, t:t + 2, :] if t < 2 * GA else gates_b[:, t - 2 * GA:t - 2 * GA + 2, :]
                    yy = ybuf[p][:, 2 * j:2 * j + 2, :]
                    tt(scr[:, 0:2, 0:SEQ], ps[:, 2 * j:2 * j + 2, 0:SEQ], gate, MUL).then_inc(pair_out, 1)
                    dve.wait_ge(pair_out, 4 * (PASS_PROJ + p) + j + 1)
                    tt(yy, yy, scr[:, 0:2, 0:SEQ], ADD).then_inc(merged, 1)
                    dve.wait_ge(merged, 4 * p + j + 1)
                    dve.wait_ge(mhi_ready, 4 * p + j + 1)
                    tt(x_lo[:, t:t + 2, META:T], yy, x_hi[:, t:t + 2, META:T].bitcast(f32), SUB).then_inc(m_ready, 1)
                plain_pass(Q_PROJ + 3 * p, 3, take_proj)
            for p in range(2):
                def take_out(j, p=p):
                    t = 8 * p + 2 * j
                    tt(h[:, t:t + 2, META:T], ps[:, 2 * j:2 * j + 2, 0:SEQ], h[:, t:t + 2, META:T], ADD).then_inc(pair_out, 1)

                def add(j, p=p):
                    if 4 * p + j >= 2:
                        add_squares(2, META, 4 * p + j - 1)
                def next_x(j):
                    for k in (2 * j, 2 * j + 1):
                        lower(2, META, k)
                plain_pass(Q_OUT + 4 * p, 4, take_out, add, next_x if p else None)
            for k in range(DT // 2, DT):
                lower(2, META, k)
            ffn(1, META, Q_FFN2)
            root_inverse(3, META)
            dve.wait_ge(rms_inv, 4)
            for k in range(DT // 2):
                if k not in POOL_PAIRS:
                    dve.wait_ge(gained, k + 1)
                    y = h[:, 2 * k:2 * k + 2, META:T]
                    tt(y, y, scr[:, 5:6, META:T].broadcast_to([P, 2, SEQ]), MUL).then_inc(y_final, 1)

        @block.gpsimd
        def _(pool):
            step = Tally(pool, pool_step)
            tt, ts = pool.tensor_tensor, pool.tensor_scalar

            def chain(ins):
                step(ins)
                step.join()
            pool.memset(cd[:, :, :, :], 0.0).then_inc(consts, 1)
            pool.memset(ones[:, :], 1.0 / D)
            for c, value in enumerate((1.0 / DK, EPS, -0.5, 1.0)):
                pool.memset(small[:, c:c + 1], value)
            pool.memset(bd[:, :, :, :], 0.0)
            chain(pool.memset(ident[:, :], 0.0))
            pool.affine_select(out=ident[:, :], in_=ident[:, :], compare_op=ALU.not_equal, fill=1.0, base=0,
                               pattern=[[-1, P]], channel_multiplier=1).then_inc(consts, 1)
            v = [sv[:, i, :] for i in range(14)]
            lr, li = v[0], v[1]
            pool.wait_ge(sv_act, 1)
            tt(v[4], lr, v[3], MUL).then_inc(sv_pool, 1)
            chain(tt(v[5], li, v[3], MUL))
            chain(ts(v[6], v[5], INV_TWO_PI, None, MUL))
            chain(ts(v[6], v[6], ROUNDER, None, ADD))
            chain(ts(v[6], v[6], -ROUNDER, None, ADD))
            for part in TWO_PI_PARTS:
                chain(ts(v[7], v[6], part, None, MUL))
                chain(tt(v[5], v[5], v[7], SUB))
            chain(ts(v[8], v[5], 0.5, None, MUL))
            ts(v[9], v[5], 0.25, None, MUL).then_inc(sv_pool, 1)
            chain(tt(v[12], lr, lr, MUL))
            chain(tt(v[7], li, li, MUL))
            tt(v[12], v[12], v[7], ADD).then_inc(sv_pool, 1)
            pool.wait_ge(sv_act, 3)
            sn, sq, c, s, n = v[10], v[11], v[8], v[7], v[9]
            chain(tt(v[6], sq, sq, MUL))
            chain(ts(v[6], v[6], -2.0, 1.0, MUL, ADD))
            chain(tt(s, sn, v[6], MUL))
            chain(ts(s, s, 2.0, None, MUL))
            chain(tt(c, sn, sn, MUL))
            chain(ts(c, c, -2.0, 1.0, MUL, ADD))
            chain(tt(n, c, c, MUL))
            chain(tt(v[5], s, s, MUL))
            chain(tt(n, n, v[5], ADD))
            chain(ts(n, n, -0.5, 1.5, MUL, ADD))
            chain(tt(s, s, n, MUL))
            chain(tt(c, c, n, MUL))
            a_re, a_im = v[10], v[11]
            chain(tt(a_re, mag[:, :], c, MUL))
            chain(tt(a_im, mag[:, :], s, MUL))
            chain(ts(a_re, a_re, -1.0, None, ADD))
            pool.wait_ge(den_inv, 1)
            c_re, c_im = v[3], v[4]
            chain(tt(c_re, a_re, lr, MUL))
            chain(tt(c_im, a_im, li, MUL))
            chain(tt(c_re, c_re, c_im, ADD))
            chain(tt(c_re, c_re, v[13], MUL))
            chain(tt(c_im, a_im, lr, MUL))
            chain(tt(v[5], a_re, li, MUL))
            chain(tt(c_im, c_im, v[5], SUB))
            chain(tt(c_im, c_im, v[13], MUL))
            pool.wait_ge(small_in[5], 16)
            b = btmp[:, 0:2 * ST * GP].rearrange("p (r j c) -> p r j c", r=2, j=ST)
            for g in range(2):
                rows = slice(64 * g, 64 * g + 64)

                def coef(x):
                    return x[rows, :].unsqueeze(2).broadcast_to([64, ST, GP])
                for r, (other, op) in enumerate(((1, SUB), (0, ADD))):
                    out = bd[rows, r, :, g * GP:(g + 1) * GP]
                    chain(tt(out, b[rows, r, :, :], coef(c_re), MUL))
                    chain(tt(bprod[rows, :, :], b[rows, other, :, :], coef(c_im), MUL))
                    chain(tt(out, out, bprod[rows, :, :], op))
            pool.sem_inc(bbar_ready, 1)
            for g in range(2):
                pool.wait_ge(small_in[6 + g], 16)
            chain(ts(cd[:, :, 1, :], cd[:, :, 1, :], -1.0, None, MUL))
            pool.memset(e_re[:, :, 0:1], 1.0)
            chain(pool.memset(e_im[:, :, 0:1], 0.0))
            p_re, p_im, n_re, n_im = c, s, v[9], v[10]
            tmp = btmp[:, :].rearrange("p (j t) -> p j t", j=ST)
            n = 1
            while n < T:
                for t0 in range(0, min(n, T - n), 32):
                    w = min(32, n - t0, T - n - t0)
                    src, dst = slice(t0, t0 + w), slice(n + t0, n + t0 + w)

                    def power(x):
                        return x.unsqueeze(2).broadcast_to([P, ST, w])
                    for out, one, two, op in ((e_re, p_re, p_im, SUB), (e_im, p_im, p_re, ADD)):
                        chain(tt(out[:, :, dst], e_re[:, :, src], power(one), MUL))
                        chain(tt(tmp[:, :, 0:w], e_im[:, :, src], power(two), MUL))
                        chain(tt(out[:, :, dst], out[:, :, dst], tmp[:, :, 0:w], op))
                chain(tt(n_re, p_re, p_re, MUL))
                chain(tt(v[5], p_im, p_im, MUL))
                chain(tt(n_re, n_re, v[5], SUB))
                chain(tt(n_im, p_re, p_im, MUL))
                chain(ts(n_im, n_im, 2.0, None, MUL))
                p_re, p_im, n_re, n_im = n_re, n_im, p_re, p_im
                n *= 2
            pool.sem_inc(tables, 1)
            pool.wait_ge(rms_inv, 2)
            for k in range(2, DT):
                if k >= 4:
                    pool.wait_ge(x_ready, DT + k - 3)
                tt(scr[:, k % 4, :], h[:, k, :], scr[:, 5, :], MUL).then_inc(xf_pool, 1)
            pool.wait_ge(ys_done, UT + 1)
            chain(pool.memset(mask[:, :, :], 0.0))
            chain(pool.affine_select(out=mask[:, 0, :], in_=mask[:, 0, :], compare_op=ALU.not_equal, fill=1.0, base=0,
                                     pattern=[[-1, P]], channel_multiplier=1))
            for l in range(1, SLOTS - 1):
                m = 1 << (l - 1)
                right = mask[:, l, :].rearrange("p (b s m) -> p b s m", s=2, m=m)[:, :, 1, :]
                nb = P // (2 * m)
                chain(pool.memset(right, 1.0))
                chain(pool.affine_select(out=right, in_=right, compare_op=ALU.is_ge, fill=0.0, base=0,
                                         pattern=[[-2 * m, nb], [0, m]], channel_multiplier=1))
                chain(pool.affine_select(out=right, in_=right, compare_op=ALU.is_ge, fill=0.0, base=m - 1,
                                         pattern=[[2 * m, nb], [0, m]], channel_multiplier=-1))
            m = 1 << (SLOTS - 2)
            late = mask[:, SLOTS - 1, :].rearrange("p (b m) -> p b m", m=m)
            chain(pool.memset(late, 1.0))
            chain(pool.affine_select(out=late, in_=late, compare_op=ALU.is_ge, fill=0.0, base=-1,
                                     pattern=[[m, P // m], [0, m]], channel_multiplier=-1))
            pool.sem_inc(mask_ready, 1)
            with pool.Fori(0, HEADS) as hd:
                step.turn(hd, 2)
                pool.wait_ge(ss_ready, hd + 1)
                chain(tt(ss[:, 1, :], ss[:, 0, :], small[:, 0:1].broadcast_to([P, 2]), MUL))
                chain(tt(ss[:, 1, :], ss[:, 1, :], small[:, 1:2].broadcast_to([P, 2]), ADD))
                tt(ss[:, 1, :], ss[:, 1, :], small[:, 2:3].broadcast_to([P, 2]), ALU.pow).then_inc(rr_ready, 1)
            step.done(HEADS)
            pool.wait_ge(rms_inv, 4)
            for k in POOL_PAIRS:
                pool.wait_ge(gained, k + 1)
                y = h[:, 2 * k:2 * k + 2, META:T]
                tt(y, y, scr[:, 5:6, META:T].broadcast_to([P, 2, SEQ]), MUL).then_inc(y_pool, 1)


def kernel(x, meta_tokens, norm_ffn1, ffn1_w_gate, ffn1_w_up, ffn1_w_down, norm_mix, w_in, hg_lower_bounds, hg_norm,
           hg_w_proj, s5_lam_re, s5_lam_im, s5_log_step, s5_b_re, s5_b_im, s5_c_re, s5_c_im, s5_d, s5_w_glu_a,
           s5_w_glu_b, w_out, norm_ffn2, ffn2_w_gate, ffn2_w_up, ffn2_w_down, norm_final):
    import numpy as np
    import concourse.bacc as bacc
    from concourse.bass_utils import run_bass_kernel_spmd

    nc = bacc.Bacc("TRN2", target_bir_lowering=False, num_devices=1)
    arrays = {}

    def tensor(name, a):
        a = np.ascontiguousarray(a)
        arrays[name] = a
        return nc.dram_tensor(name, a.shape, mybir.dt.from_np(a.dtype), kind="ExternalInput").ap()

    def tiles(a, n):
        return np.asarray(a).reshape(n, P).T

    args = [
        tensor("xT", np.asarray(x)[0].T),
        tensor("metaT", np.asarray(meta_tokens).T),
        tensor("gains", np.stack([tiles(g, DT) for g in (norm_ffn1, norm_mix, norm_ffn2, norm_final)], 1)),
        [tensor(n, np.asarray(w)[0]) for n, w in (("gate1", ffn1_w_gate), ("up1", ffn1_w_up), ("down1", ffn1_w_down))],
        tensor("w_in", np.asarray(w_in)[0]),
        tensor("hg_lb", np.stack([tiles(r, HEADS) for r in np.asarray(hg_lower_bounds)], 1)),
        tensor("hg_norm", tiles(hg_norm, HEADS)),
        tensor("w_proj", np.asarray(hg_w_proj)[0]),
        tensor("s5v", np.stack([tiles(v, ST) for v in (s5_lam_re, s5_lam_im, np.repeat(np.asarray(s5_log_step)[0], STATE))], 1)),
        tensor("s5b", np.stack([np.asarray(b).reshape(ST, P, GP).transpose(1, 0, 2) for b in (s5_b_re, s5_b_im)], 1)),
        tensor("s5c", np.stack([np.asarray(c)[0].transpose(0, 2, 1).reshape(ST, P, GP).transpose(1, 0, 2)
                                for c in (s5_c_re, s5_c_im)], 2)),
        tensor("s5d", tiles(s5_d, UT)),
        [tensor(n, np.asarray(w)[0]) for n, w in (("glu_a", s5_w_glu_a), ("glu_b", s5_w_glu_b))],
        tensor("w_out", np.asarray(w_out)[0]),
        [tensor(n, np.asarray(w)[0]) for n, w in (("gate2", ffn2_w_gate), ("up2", ffn2_w_up), ("down2", ffn2_w_down))],
        nc.dram_tensor("outT", (D, SEQ), mybir.dt.float32, kind="ExternalOutput").ap(),
    ]
    program(nc, *args)
    r = run_bass_kernel_spmd(nc, [arrays], core_ids=[0])
    return r.results[0]["outT"].T[None]
```
